# Optimizing a Trainium2 kernel written in Bass

```python
import math
import jax
import jax.numpy as jnp
from jax import lax
import numpy as np

D_MODEL = 1024
BATCH = 1
SEQ = 256
DEPTH = 2

GRID_W = 64
CTX_LEN = 256
N_EVEN = (DEPTH + 1) // 2
N_ODD = DEPTH // 2
EPS = 1e-6
N_MOD = 6

GROUP_DIM = 64
HY_WIDTH = 3 * D_MODEL // 4
FN_WIDTH = D_MODEL - HY_WIDTH
FN_GROUPS = FN_WIDTH // GROUP_DIM
EVEN_IN = 3 * HY_WIDTH + FN_WIDTH
HY_EMB_DIM = 33
HY_FILTER_HIDDEN = 64
HY_DECAY_TARGET = 1e-2
HY_FAST_DECAY_PCT = 0.3
HY_SLOW_DECAY_PCT = 1.5
D_FF = ((8 * D_MODEL // 3 + 255) // 256) * 256

HEAD_DIM = 64
N_Q_HEADS = (D_MODEL // 2) // HEAD_DIM
N_KV_HEADS = 2
Q_PER_KV = N_Q_HEADS // N_KV_HEADS
ATT_WIDTH = N_Q_HEADS * HEAD_DIM
KV_WIDTH = N_KV_HEADS * HEAD_DIM
SC_WIDTH = D_MODEL - ATT_WIDTH
ODD_IN = ATT_WIDTH + 2 * KV_WIDTH + 3 * SC_WIDTH
WINDOW = 128
BLOCK = 128
ROPE_BASE = 10000.0
N_EXPERTS = 8
TOP_K = 2
D_FF_EXPERT = 7 * D_MODEL // 2
NEG_INF = -1e30

kernel_name = "hybrid_hyena_fnet_shortconv_swa_moe_dit"

def rms_norm(x, g):
    xf = x.astype(jnp.float32)
    y = xf * lax.rsqrt(jnp.mean(xf * xf, axis=-1, keepdims=True) + EPS)
    return (y * g.astype(jnp.float32)).astype(x.dtype)

def ada_params(cond, w, b):
    m = jax.nn.silu(cond) @ w + b
    return jnp.split(m[..., None, :], N_MOD, axis=-1)

def modulate(x, g, shift, scale):
    return rms_norm(x, g) * (1 + scale) + shift

def short_conv(u, w):
    L = u.shape[1]
    up = jnp.pad(u, ((0, 0), (1, 1), (0, 0)))
    return up[:, :L] * w[0] + up[:, 1:L + 1] * w[1] + up[:, 2:] * w[2]

def swiglu(h, wg, wu, wd):
    return (jax.nn.silu(h @ wg) * (h @ wu)) @ wd

def hyena_kernel(L, w1, b1, freq, w2, b2, w3):
    f32 = jnp.float32
    t = jnp.linspace(0.0, 1.0, L, dtype=f32)[:, None]
    bands = (HY_EMB_DIM - 1) // 2
    ang = (2.0 * math.pi / L) * jnp.arange(L, dtype=f32)[:, None] * jnp.linspace(1e-4, bands - 1, bands, dtype=f32)[None, :]
    z = jnp.concatenate([t, jnp.cos(ang), -jnp.sin(ang)], axis=-1)
    fr = freq.astype(f32)
    h = jnp.sin(fr * (z @ w1.astype(f32) + b1.astype(f32)))
    h = jnp.sin(fr * (h @ w2.astype(f32) + b2.astype(f32)))
    h = h @ w3.astype(f32)
    max_decay = math.log(HY_DECAY_TARGET) / HY_FAST_DECAY_PCT
    min_decay = math.log(HY_DECAY_TARGET) / HY_SLOW_DECAY_PCT
    deltas = jnp.abs(jnp.linspace(min_decay, max_decay, HY_WIDTH, dtype=f32))
    decay = jnp.exp(-t * deltas[None, :])
    h_fwd = h[:, :HY_WIDTH] * decay
    h_bwd = h[1:, HY_WIDTH:] * decay[1:]
    l1 = jnp.sum(jnp.abs(h_fwd), axis=0) + jnp.sum(jnp.abs(h_bwd), axis=0)
    kern = jnp.concatenate([h_fwd, jnp.zeros((1, HY_WIDTH), f32), h_bwd[::-1]], axis=0)
    return kern / l1

def fft_conv_bidir(u, kern):
    L = u.shape[1]
    n = 2 * L
    u_f = jnp.fft.rfft(u.astype(jnp.float32), n=n, axis=1)
    k_f = jnp.fft.rfft(kern, n=n, axis=0)
    return jnp.fft.irfft(u_f * k_f[None], n=n, axis=1)[:, :L]

def hyena_mix(p, short_w, w1, b1, freq, w2, b2, w3, skip):
    L = p.shape[1]
    p = short_conv(p, short_w)
    x0, x1, v = jnp.split(p, 3, axis=-1)
    u = v * x1
    kern = hyena_kernel(L, w1, b1, freq, w2, b2, w3)
    y = fft_conv_bidir(u, kern).astype(u.dtype) + u * skip
    return x0 * y

def fourier_mix(f):
    B, L, _ = f.shape
    fg = f.astype(jnp.float32).reshape(B, L, FN_GROUPS, GROUP_DIM)
    y = jnp.fft.fft2(fg, axes=(1, 3), norm="ortho").real
    return y.reshape(B, L, FN_WIDTH).astype(f.dtype)

def axial_rope(x, rows, cols):
    half = HEAD_DIM // 2
    quarter = half // 2
    inv_freq = ROPE_BASE ** (-jnp.arange(quarter, dtype=jnp.float32) / quarter)
    xf = x.astype(jnp.float32)

    def rotate(xa, pos):
        ang = pos.astype(jnp.float32)[:, None] * inv_freq[None, :]
        cos = jnp.cos(ang)[None, :, None, :]
        sin = jnp.sin(ang)[None, :, None, :]
        a1, a2 = xa[..., :quarter], xa[..., quarter:]
        return jnp.concatenate([a1 * cos - a2 * sin, a2 * cos + a1 * sin], axis=-1)

    out = jnp.concatenate([rotate(xf[..., :half], rows), rotate(xf[..., half:], cols)], axis=-1)
    return out.astype(x.dtype)

def window_attention(q, k, v, kc, vc, sink):
    B, L = q.shape[0], q.shape[1]
    n_blocks = L // BLOCK
    qg = q.reshape(B, L, N_KV_HEADS, Q_PER_KV, HEAD_DIM)
    kp = jnp.pad(k, ((0, 0), (BLOCK, BLOCK), (0, 0), (0, 0)))
    vp = jnp.pad(v, ((0, 0), (BLOCK, BLOCK), (0, 0), (0, 0)))
    scale = HEAD_DIM ** -0.5
    a_idx = jnp.arange(BLOCK)[:, None]
    b_idx = jnp.arange(3 * BLOCK)[None, :]
    band = jnp.abs(b_idx - BLOCK - a_idx) <= WINDOW
    sink_l = sink.astype(jnp.float32).reshape(1, N_KV_HEADS, Q_PER_KV, 1, 1)
    n_ctx = kc.shape[1]

    def attend_block(i):
        start = i * BLOCK
        qb = lax.dynamic_slice_in_dim(qg, start, BLOCK, axis=1)
        kb = lax.dynamic_slice_in_dim(kp, start, 3 * BLOCK, axis=1)
        vb = lax.dynamic_slice_in_dim(vp, start, 3 * BLOCK, axis=1)
        kpos = start - BLOCK + jnp.arange(3 * BLOCK)
        mask = band & ((kpos >= 0) & (kpos < L))[None, :]
        s_loc = jnp.einsum("bqhgd,bshd->bhgqs", qb, kb).astype(jnp.float32) * scale
        s_loc = jnp.where(mask, s_loc, NEG_INF)
        s_ctx = jnp.einsum("bqhgd,bchd->bhgqc", qb, kc).astype(jnp.float32) * scale
        s_sink = jnp.broadcast_to(sink_l, (B, N_KV_HEADS, Q_PER_KV, BLOCK, 1))
        p = jax.nn.softmax(jnp.concatenate([s_loc, s_ctx, s_sink], axis=-1), axis=-1)
        p_loc = p[..., :3 * BLOCK].astype(v.dtype)
        p_ctx = p[..., 3 * BLOCK:3 * BLOCK + n_ctx].astype(v.dtype)
        return jnp.einsum("bhgqs,bshd->bqhgd", p_loc, vb) + jnp.einsum("bhgqc,bchd->bqhgd", p_ctx, vc)

    out = lax.map(attend_block, jnp.arange(n_blocks))
    return jnp.moveaxis(out, 0, 1).reshape(B, L, ATT_WIDTH)

def context_attention(qc, kc, vc, sink):
    B, C = qc.shape[0], qc.shape[1]
    qg = qc.reshape(B, C, N_KV_HEADS, Q_PER_KV, HEAD_DIM)
    s = jnp.einsum("bqhgd,bshd->bhgqs", qg, kc).astype(jnp.float32) * HEAD_DIM ** -0.5
    s_sink = jnp.broadcast_to(sink.astype(jnp.float32).reshape(1, N_KV_HEADS, Q_PER_KV, 1, 1), (B, N_KV_HEADS, Q_PER_KV, C, 1))
    p = jax.nn.softmax(jnp.concatenate([s, s_sink], axis=-1), axis=-1)[..., :C].astype(vc.dtype)
    return jnp.einsum("bhgqs,bshd->bqhgd", p, vc).reshape(B, C, ATT_WIDTH)

def short_gated_conv_mix(s, conv_w):
    gate_b, gate_c, hx = jnp.split(s, 3, axis=-1)
    return gate_b * short_conv(gate_c * hx, conv_w)

def moe_swiglu(h, router_w, router_b, wg, wu, wd):
    logits = (h @ router_w + router_b).astype(jnp.float32)
    top_val, top_idx = lax.top_k(logits, TOP_K)
    gates = jax.nn.softmax(top_val, axis=-1)
    combine = jnp.einsum("blk,blke->ble", gates, jax.nn.one_hot(top_idx, N_EXPERTS, dtype=jnp.float32)).astype(h.dtype)
    out = jnp.zeros_like(h)
    for e in range(N_EXPERTS):
        out = out + combine[..., e:e + 1] * swiglu(h, wg[e], wu[e], wd[e])
    return out

def even_layer(x, ctx, mod_x, mod_c, norm1, norm2, w_in, hy_short, hy_w1, hy_b1, hy_freq, hy_w2, hy_b2, hy_w3, hy_skip, w_out, ffn_wg, ffn_wu, ffn_wd):
    def run(s, mod):
        sh1, sc1, g1, sh2, sc2, g2 = mod
        p = modulate(s, norm1, sh1, sc1) @ w_in
        y_h = hyena_mix(p[..., :3 * HY_WIDTH], hy_short, hy_w1, hy_b1, hy_freq, hy_w2, hy_b2, hy_w3, hy_skip)
        y_f = fourier_mix(p[..., 3 * HY_WIDTH:])
        s = s + g1 * (jnp.concatenate([y_h, y_f], axis=-1) @ w_out)
        return s + g2 * swiglu(modulate(s, norm2, sh2, sc2), ffn_wg, ffn_wu, ffn_wd)

    x_new = run(x, mod_x)
    ctx_new = run(ctx, mod_c) if mod_c is not None else None
    return x_new, ctx_new

def odd_layer(x, ctx, mod_x, mod_c, rows, cols, need_ctx, norm1, norm2, w_in, q_norm, k_norm, sink, sc_conv, w_out, router_w, router_b, moe_wg, moe_wu, moe_wd):
    B, L, _ = x.shape
    n_ctx = ctx.shape[1]
    csh1, csc1, cg1, csh2, csc2, cg2 = mod_c
    hc = modulate(ctx, norm1, csh1, csc1)
    if need_ctx:
        pc = hc @ w_in
        qc, kc, vc, sc_c = jnp.split(pc, [ATT_WIDTH, ATT_WIDTH + KV_WIDTH, ATT_WIDTH + 2 * KV_WIDTH], axis=-1)
    else:
        kvc = hc @ w_in[:, ATT_WIDTH:ATT_WIDTH + 2 * KV_WIDTH]
        kc, vc = jnp.split(kvc, 2, axis=-1)
    kc = rms_norm(kc.reshape(B, n_ctx, N_KV_HEADS, HEAD_DIM), k_norm)
    vc = vc.reshape(B, n_ctx, N_KV_HEADS, HEAD_DIM)

    sh1, sc1, g1, sh2, sc2, g2 = mod_x
    p = modulate(x, norm1, sh1, sc1) @ w_in
    q, k, v, s = jnp.split(p, [ATT_WIDTH, ATT_WIDTH + KV_WIDTH, ATT_WIDTH + 2 * KV_WIDTH], axis=-1)
    q = axial_rope(rms_norm(q.reshape(B, L, N_Q_HEADS, HEAD_DIM), q_norm), rows, cols)
    k = axial_rope(rms_norm(k.reshape(B, L, N_KV_HEADS, HEAD_DIM), k_norm), rows, cols)
    v = v.reshape(B, L, N_KV_HEADS, HEAD_DIM)
    y_att = window_attention(q, k, v, kc, vc, sink)
    y_sc = short_gated_conv_mix(s, sc_conv)
    x = x + g1 * (jnp.concatenate([y_att, y_sc], axis=-1) @ w_out)
    x = x + g2 * moe_swiglu(modulate(x, norm2, sh2, sc2), router_w, router_b, moe_wg, moe_wu, moe_wd)

    if need_ctx:
        qc = rms_norm(qc.reshape(B, n_ctx, N_Q_HEADS, HEAD_DIM), q_norm)
        yc = jnp.concatenate([context_attention(qc, kc, vc, sink), short_gated_conv_mix(sc_c, sc_conv)], axis=-1) @ w_out
        ctx = ctx + cg1 * yc
        ctx = ctx + cg2 * moe_swiglu(modulate(ctx, norm2, csh2, csc2), router_w, router_b, moe_wg, moe_wu, moe_wd)
    else:
        ctx = None
    return x, ctx

def setup_inputs(seed: int = 0) -> dict:
    key = jax.random.key(seed)
    ks = iter(jax.random.split(key, 48))
    f32 = jnp.float32
    D = D_MODEL
    NE, NO = N_EVEN, N_ODD

    def nrm(shape, scale):
        return jax.random.normal(next(ks), shape, f32) * scale

    def gain(shape):
        return 1.0 + nrm(shape, 0.02)

    return {
        "x": nrm((BATCH, SEQ, D), 1.0),
        "c": nrm((BATCH, D), 1.0),
        "ctx": nrm((BATCH, CTX_LEN, D), 1.0),
        "c_ctx": nrm((D,), 1.0),
        "e_ada_w": nrm((NE, D, N_MOD * D), D ** -0.5),
        "e_ada_b": nrm((NE, N_MOD * D), 0.02),
        "e_norm1": gain((NE, D)),
        "e_norm2": gain((NE, D)),
        "e_w_in": nrm((NE, D, EVEN_IN), D ** -0.5),
        "e_hy_short": nrm((NE, 3, 3 * HY_WIDTH), 3 ** -0.5),
        "e_hy_w1": nrm((NE, HY_EMB_DIM, HY_FILTER_HIDDEN), HY_EMB_DIM ** -0.5),
        "e_hy_b1": nrm((NE, HY_FILTER_HIDDEN), 0.02),
        "e_hy_freq": gain((NE, HY_FILTER_HIDDEN)),
        "e_hy_w2": nrm((NE, HY_FILTER_HIDDEN, HY_FILTER_HIDDEN), HY_FILTER_HIDDEN ** -0.5),
        "e_hy_b2": nrm((NE, HY_FILTER_HIDDEN), 0.02),
        "e_hy_w3": nrm((NE, HY_FILTER_HIDDEN, 2 * HY_WIDTH), HY_FILTER_HIDDEN ** -0.5),
        "e_hy_skip": nrm((NE, HY_WIDTH), 1.0),
        "e_w_out": nrm((NE, D, D), D ** -0.5),
        "e_ffn_wg": nrm((NE, D, D_FF), D ** -0.5),
        "e_ffn_wu": nrm((NE, D, D_FF), D ** -0.5),
        "e_ffn_wd": nrm((NE, D_FF, D), D_FF ** -0.5),
        "o_ada_w": nrm((NO, D, N_MOD * D), D ** -0.5),
        "o_ada_b": nrm((NO, N_MOD * D), 0.02),
        "o_norm1": gain((NO, D)),
        "o_norm2": gain((NO, D)),
        "o_w_in": nrm((NO, D, ODD_IN), D ** -0.5),
        "o_q_norm": gain((NO, HEAD_DIM)),
        "o_k_norm": gain((NO, HEAD_DIM)),
        "o_sink": nrm((NO, N_Q_HEADS), 0.5),
        "o_sc_conv": nrm((NO, 3, SC_WIDTH), 3 ** -0.5),
        "o_w_out": nrm((NO, D, D), D ** -0.5),
        "o_router_w": nrm((NO, D, N_EXPERTS), D ** -0.5),
        "o_router_b": nrm((NO, N_EXPERTS), 0.01),
        "o_moe_wg": nrm((NO, N_EXPERTS, D, D_FF_EXPERT), D ** -0.5),
        "o_moe_wu": nrm((NO, N_EXPERTS, D, D_FF_EXPERT), D ** -0.5),
        "o_moe_wd": nrm((NO, N_EXPERTS, D_FF_EXPERT, D), D_FF_EXPERT ** -0.5),
    }

def reference(x, c, ctx, c_ctx,
              e_ada_w, e_ada_b, e_norm1, e_norm2, e_w_in, e_hy_short, e_hy_w1, e_hy_b1, e_hy_freq,
              e_hy_w2, e_hy_b2, e_hy_w3, e_hy_skip, e_w_out, e_ffn_wg, e_ffn_wu, e_ffn_wd,
              o_ada_w, o_ada_b, o_norm1, o_norm2, o_w_in, o_q_norm, o_k_norm, o_sink, o_sc_conv,
              o_w_out, o_router_w, o_router_b, o_moe_wg, o_moe_wu, o_moe_wd):
    L = x.shape[1]
    n_rows = L // GRID_W
    rows = jnp.repeat(jnp.arange(n_rows, dtype=jnp.int32), GRID_W)
    cols = jnp.tile(jnp.arange(GRID_W, dtype=jnp.int32), n_rows)
    for layer in range(DEPTH):
        j = layer // 2
        need_ctx = layer < DEPTH - 1
        if layer % 2 == 0:
            mod_x = ada_params(c, e_ada_w[j], e_ada_b[j])
            mod_c = ada_params(c_ctx, e_ada_w[j], e_ada_b[j]) if need_ctx else None
            x, ctx = even_layer(x, ctx, mod_x, mod_c, e_norm1[j], e_norm2[j], e_w_in[j], e_hy_short[j],
                                e_hy_w1[j], e_hy_b1[j], e_hy_freq[j], e_hy_w2[j], e_hy_b2[j], e_hy_w3[j],
                                e_hy_skip[j], e_w_out[j], e_ffn_wg[j], e_ffn_wu[j], e_ffn_wd[j])
        else:
            mod_x = ada_params(c, o_ada_w[j], o_ada_b[j])
            mod_c = ada_params(c_ctx, o_ada_w[j], o_ada_b[j])
            x, ctx = odd_layer(x, ctx, mod_x, mod_c, rows, cols, need_ctx, o_norm1[j], o_norm2[j], o_w_in[j],
                               o_q_norm[j], o_k_norm[j], o_sink[j], o_sc_conv[j], o_w_out[j],
                               o_router_w[j], o_router_b[j], o_moe_wg[j], o_moe_wu[j], o_moe_wd[j])
    return x


_drawn_inputs = setup_inputs


def setup_inputs(seed=0):
    import zlib

    import numpy as np

    out = dict(_drawn_inputs(seed))
    spreads = {}
    factors = {'e_hy_b1': 8.0,
     'e_hy_freq': 8.0,
     'e_hy_b2': 5.5,
     'o_q_norm': 8.0,
     'o_k_norm': 8.0,
     'o_sink': 8.0,
     'o_router_b': 11.531,
     'o_norm2': 2.771}
    for name, (base, spread) in spreads.items():
        noise = np.random.default_rng([zlib.crc32(name.encode()), seed]).standard_normal(out[name].shape)
        drawn = base * np.exp(spread * noise) if base else spread * noise
        out[name] = jnp.asarray(drawn.astype(out[name].dtype))
    for name, factor in factors.items():
        out[name] = (out[name] * factor).astype(out[name].dtype)
    return out
```

```python
from contextlib import ExitStack

import numpy as np
import concourse.bass as bass
from concourse import mybir

F32 = mybir.dt.float32
F32R = mybir.dt.float32r
I32 = mybir.dt.int32
ACT = mybir.ActivationFunctionType
ALU = mybir.AluOpType
AX = mybir.AxisListType

P = 128
D = 1024
KT = D // P
L = 256
T = 2 * L
EPS = 1e-6
HY = 768
HT = HY // P
HALF = HY // 2
FF_PAIRS = 2816 // 256
NEXP = 8
CHUNK = 512
NCH = 3584 // CHUNK
ROUND_BLOCKS = 6 * NCH
OVER = 3
NTAB = NEXP + OVER + 1

RAW = 6
SPLIT = 3
BLK = 2048
POOL_SLOT = 5

ADA_BLOCKS = 48
WIN, WOUT, FFN = 10, 4, 6 * FF_PAIRS
OWIN, OWOUT = 9, 4
J_WIN = 0
J_WOUT = J_WIN + WIN
J_FFN = J_WOUT + WOUT
J_OWIN = J_FFN + FFN
J_OWOUT = J_OWIN + OWIN
J_MOE = J_OWOUT + OWOUT

WIN_TILES = [18, 19] + [s + 2 * i + a for i in range(3) for s in (6, 12, 0) for a in range(2)]
OWIN_TILES = [4, 5, 0, 1, 2, 3] + [6 + s + i for i in range(4) for s in (4, 8, 0)]

VEC = {}


def _columns():
    at = 0
    for name, n in (("e_ada_b", 48), ("o_ada_b", 48), ("e_norm1", 8), ("e_norm2", 8), ("o_norm1", 8),
                    ("o_norm2", 8), ("short", 54), ("skip", 6), ("b1", 1), ("freq", 1), ("b2", 1),
                    ("q_norm", 1), ("k_norm", 1), ("sc", 12), ("sink", 8), ("router_b", 8), ("cond", 16)):
        VEC[name] = slice(at, at + n)
        at += n
    return at


NVEC = _columns()


HEADS = [h for i in range(4) for h in (i, i + 4)]

ROUND = 1.5 * 2 ** 23
TURN = (6.28125, float(2 * np.pi - 6.28125))


def gate_block(c):
    return 6 * c - 2 if c else 0


def down_block(c):
    return 6 * c + 8 if c < NCH - 1 else ROUND_BLOCKS - 2


class Steps:

    def __init__(self, engine, sem):
        self.engine, self.sem, self.n = engine, sem, 0

    def step(self, instruction):
        instruction.then_inc(self.sem, 1)
        self.n += 1
        self.engine.wait_ge(self.sem, self.n)


def block_at(j, turn=0, per=0):
    b = ADA_BLOCKS + j
    uses = b // RAW + 1
    return b % RAW, (uses + turn * (per // RAW) if per else uses)


def build(nc, a, out):
    ctx = ExitStack()
    with ctx:
        def sb(name, shape, dt=F32, where=ctx):
            return where.enter_context(nc.sbuf_tensor(name, shape, dt))

        def sem(name):
            return ctx.enter_context(nc.semaphore(name))

        raw = sb("raw", [P, RAW, BLK])
        whi = sb("whi", [P, SPLIT, BLK], F32R)
        wlo = sb("wlo", [P, SPLIT, BLK], F32R)
        hhi = sb("hhi", [P, KT, T], F32R)
        hlo = sb("hlo", [P, KT, T], F32R)
        vec = sb("vec", [P, NVEC])
        ident = sb("ident", [P, P])
        mean = sb("mean", [P, P])
        emod = sb("emod", [P, 48, 2])
        omod = sb("omod", [P, 48, 2])
        gain = sb("gain", [P, 4, KT, 2])
        scond = sb("scond", [P, 16])
        eps = sb("eps", [P, 1])
        ones = sb("ones", [P, 1])
        il1 = sb("il1", [P, HT])

        even = ExitStack()
        kf = sb("kf", [P, 5, HY], where=even)
        dft = sb("dft", [P, 2, 512], where=even)
        start = ExitStack()
        xin = sb("xin", [P, KT, T], where=start)
        dft2 = sb("dft2", [P, 2, 256], where=start)
        decay = sb("decay", [P, 2, HY], where=start)
        hf = sb("hf", [P, 2, HALF], where=start)
        hb = sb("hb", [P, 2, HALF], where=start)
        hs = sb("hs", [P, 2, HALF], where=start)
        hd = sb("hd", [P, 2, HALF], where=start)
        w3 = sb("w3", [64, 2 * HY], where=start)
        w12 = sb("w12", [64, 128], where=start)
        zt = sb("zt", [33, L], where=start)
        sarg = sb("sarg", [64, L], where=start)
        sred = sb("sred", [64, L], where=start)
        sq0 = sb("sq0", [P, 2, T], where=start)
        ssum0 = sb("ssum0", [P, T], where=start)
        rstd0 = sb("rstd0", [P, T], where=start)
        start.close()
        x0c = sb("x0c", [P, HT, T], where=even)
        u = sb("u", [P, HT, T], where=even)
        utok = sb("utok", [P, 4, HY], where=even)
        tabs = sb("tabs", [P, 2, 512], where=even)
        fnt = sb("fnt", [P, 2, T], where=even)
        bdft = sb("bdft", [P, 256], where=even)
        tmp = sb("tmp", [P, 4, T], where=even)
        even.close()

        res = sb("res", [P, KT, T])
        norm = ExitStack()
        sq = sb("sq", [P, 2, T], where=norm)
        ssum = sb("ssum", [P, T], where=norm)
        rstd = sb("rstd", [P, T], where=norm)
        ffn = ExitStack()
        facc = sb("facc", [P, KT, T], where=ffn)
        ahi = sb("ahi", [P, 2, T], F32R, where=ffn)
        alo = sb("alo", [P, 2, T], F32R, where=ffn)
        sil = sb("sil", [P, 2, T], where=ffn)
        ffn.close()
        odd = ExitStack()
        qt = sb("qt", [P, 4, L], where=odd)
        kpad = sb("kpad", [P, 2, T], where=odd)
        vpad = sb("vpad", [P, 4, 2, P], where=odd)
        ysc = sb("ysc", [P, 4, L], where=odd)
        mask = sb("mask", [P, 2, L], where=odd)
        smax = sb("smax", [P, 8], where=odd)
        nmax = sb("nmax", [P, 8], where=odd)
        ssm = sb("ssm", [P, 8], where=odd)
        esink = sb("esink", [P, 8], where=odd)
        sden = sb("sden", [P, 8], where=odd)
        mix = ExitStack()
        qraw = sb("qraw", [P, 3, T], where=mix)
        qsq = sb("qsq", [P, 3, T], where=mix)
        qn = sb("qn", [P, 3, T], where=mix)
        rr = sb("rr", [P, T], where=mix)
        ra = sb("ra", [P, L], where=mix)
        rb = sb("rb", [P, L], where=mix)
        vt = sb("vt", [P, T], where=mix)
        gcs = sb("gcs", [P, L], where=mix)
        gm = sb("gm", [P, L], where=mix)
        gcv = sb("gcv", [P, L], where=mix)
        rope = sb("rope", [P, 2, L], where=mix)
        rot = sb("rot", [P, P], where=mix)
        bd64 = sb("bd64", [P, P], where=mix)
        mix.close()
        sc = sb("sc", [P, 8, T], where=odd)
        pt = sb("pt", [P, 2, 4, P], where=odd)
        odd.close()
        norm.close()
        macc = sb("macc", [P, KT, L])
        route = ExitStack()
        ht = sb("ht", [P, KT, L], where=route)
        route.close()
        yhi = sb("yhi", [P, D], F32R)
        ylo = sb("ylo", [P, D], F32R)
        hkhi = sb("hkhi", [P, 2, D], F32R)
        hklo = sb("hklo", [P, 2, D], F32R)
        rw = sb("rw", [P, KT, NEXP])
        lg = sb("lg", [P, 2, NEXP])
        gt = sb("gt", [P, 2, NEXP, NEXP])
        eq = sb("eq", [P, 2, NEXP, NEXP])
        low = sb("low", [P, NEXP, NEXP])
        rank = sb("rank", [P, 2, NEXP])
        sel = sb("sel", [P, 2, NEXP])
        top = sb("top", [P, 2])
        ex = sb("ex", [P, 2, NEXP])
        den = sb("den", [P, 2])
        ov = sb("ov", [P, NEXP])
        ovr = sb("ovr", [P, NEXP])
        osel = sb("osel", [P, NEXP])
        obc = sb("obc", [P, 2, NEXP])
        enum = sb("enum", [P, NEXP])
        info = sb("info", [P, 4])
        infoi = sb("infoi", [P, 4], I32)
        tri = sb("tri", [P, 2, P])
        iota = sb("iota", [P, P])
        ptab = sb("ptab", [P, 2, NTAB])
        ctab = sb("ctab", [P, 2, NTAB])
        cw = sb("cw", [P, 2])
        hot = sb("hot", [P, 2, P], F32R)
        hott = sb("hott", [P, L], F32R)
        wslot = sb("wslot", [P, 1])
        ghi = sb("ghi", [P, KT, P], F32R)
        glo = sb("glo", [P, KT, P], F32R)
        sg = sb("sg", [P, CHUNK])
        am = sb("am", [P, CHUNK])
        athi = sb("athi", [P, 4, P], F32R)
        atlo = sb("atlo", [P, 4, P], F32R)
        ps = [ctx.enter_context(nc.psum_tensor(f"ps{i}", [P, 512], F32)) for i in range(8)]

        raw_loaded = [sem(f"raw_loaded{i}") for i in range(RAW)]
        raw_free = [sem(f"raw_free{i}") for i in range(RAW)]
        hi_made = sem("hi_made")
        used = sem("used")
        c_even = sem("c_even")
        c_x = sem("c_x")
        c_filt = sem("c_filt")
        c_four = sem("c_four")
        c_g = sem("c_g")
        c_res = sem("c_res")
        c_odd = sem("c_odd")
        c_mask = sem("c_mask")
        c_moe = sem("c_moe")
        c_iota = sem("c_iota")
        setup = sem("setup")
        zeroed = sem("zeroed")
        silu_c = sem("silu_c")
        mods = sem("mods")
        f_ps = sem("f_ps")
        f_arg = sem("f_arg")
        f_sin = sem("f_sin")
        f_taps = sem("f_taps")
        f_abs = sem("f_abs")
        f_k = sem("f_k")
        f_kcopy = sem("f_kcopy")
        f_l1 = sem("f_l1")
        f_il1 = sem("f_il1")
        n_sq = sem("n_sq")
        n_sum = sem("n_sum")
        n_mean = sem("n_mean")
        n_root = sem("n_root")
        n_h = sem("n_h")
        n_hi = sem("n_hi")
        n_ready = sem("n_ready")
        w_ps = sem("w_ps")
        w_mid = sem("w_mid")
        w_free = sem("w_free")
        u_made = sem("u_made")
        ut_ps = sem("ut_ps")
        ut_copy = sem("ut_copy")
        fn_ab = sem("fn_ab")
        fn_abc = sem("fn_abc")
        m_ps = sem("m_ps")
        m_z = sem("m_z")
        m_hi = sem("m_hi")
        m_ready = sem("m_ready")
        x_ps = sem("x_ps")
        x_prod = sem("x_prod")
        x_spec = sem("x_spec")
        skips = sem("skips")
        o_ps = sem("o_ps")
        res_done = sem("res_done")
        ff_silu = sem("ff_silu")
        ff_a = sem("ff_a")
        ff_hi = sem("ff_hi")
        ff_lo = sem("ff_lo")
        ff_d = sem("ff_d")
        ff_added = sem("ff_added")
        q_ps = sem("q_ps")
        q_sq = sem("q_sq")
        q_raw = sem("q_raw")
        q_ms = sem("q_ms")
        q_root = sem("q_root")
        q_n = sem("q_n")
        q_rot = sem("q_rot")
        q_done = sem("q_done")
        v_copy = sem("v_copy")
        v_ps = sem("v_ps")
        v_done = sem("v_done")
        s_gc = sem("s_gc")
        s_hx = sem("s_hx")
        s_y = sem("s_y")
        a_s = sem("a_s")
        a_ctx = sem("a_ctx")
        a_loc = sem("a_loc")
        a_max = sem("a_max")
        a_sink = sem("a_sink")
        a_exp = sem("a_exp")
        a_p = sem("a_p")
        a_t = sem("a_t")
        a_tc = sem("a_tc")
        a_o = sem("a_o")
        r_lg = sem("r_lg")
        r_sub = sem("r_sub")
        r_exp = sem("r_exp")
        r_sel = sem("r_sel")
        r_pos = sem("r_pos")
        r_tab = sem("r_tab")
        t_ps = sem("t_ps")
        t_hi = sem("t_hi")
        t_lo = sem("t_lo")
        misc = sem("misc")
        misc_free = sem("misc_free")
        hot_made = sem("hot_made")
        g_hi = sem("g_hi")
        e_silu = sem("e_silu")
        e_a = sem("e_a")
        e_t = sem("e_t")
        e_hi = sem("e_hi")
        e_lo = sem("e_lo")
        e_yhi = sem("e_yhi")
        e_y = sem("e_y")
        y_done = sem("y_done")
        stored = sem("stored")
        dve_s = sem("dve_s")

        block = ctx.enter_context(nc.Block())

        def oin_free(n):
            if n < 6:
                return (v_copy, 1) if n == 1 else (q_raw, max(n, 1))
            return (s_gc, s_hx, s_y)[(n - 6) % 3], (n - 6) // 3 + 1

        def col(name, i=0, n=1):
            at = VEC[name].start + i
            return vec[:, at:at + n]

        def half(ap):
            return ap.rearrange("p (s t) -> p s t", s=2)

        def split_block(j):
            return whi[:, j % SPLIT, :], wlo[:, j % SPLIT, :]

        @block.sync
        def _(sp):
            def load(slot, uses, src, n=BLK):
                if not (isinstance(uses, int) and uses == 1):
                    sp.wait_ge(raw_free[slot], uses - 1)
                sp.dma_start(raw[:, slot, 0:n], src).then_inc(raw_loaded[slot], 16)

            def at(src, i):
                return src[bass.ds(i, 1)].rearrange("a p n -> p (a n)")

            for s in range(RAW):
                load(s, 1, a["w_ada"][s])
            with sp.Fori(1, ADA_BLOCKS // RAW) as r:
                for s in range(RAW):
                    load(s, r + 1, at(a["w_ada"], r * RAW + s))
            for j in range(WIN):
                load(*block_at(J_WIN + j), a["w_in"][j])
            for j in range(WOUT):
                load(*block_at(J_WOUT + j), a["w_out"][j])
            with sp.Fori(0, FF_PAIRS) as r:
                for s in range(6):
                    load(*block_at(J_FFN + s, r, 6), at(a["w_ffn"], r * 6 + s), BLK // 2)
            for j in range(OWIN):
                load(*block_at(J_OWIN + j), a["w_oin"][j])
            for j in range(OWOUT):
                load(*block_at(J_OWOUT + j), a["w_oout"][j])

            def round_of(r, expert):
                for i in range(ROUND_BLOCKS):
                    load(*block_at(J_MOE + i, r, ROUND_BLOCKS), at(a["w_moe"], expert * ROUND_BLOCKS + i))

            with sp.Fori(0, NEXP) as r:
                round_of(r, r)
            sp.wait_ge(r_tab, 1)
            crowded = sp.value_load(infoi[0:1, 0:1], min_val=0, max_val=OVER)
            with sp.Fori(NEXP, NEXP + OVER) as r:
                with sp.If(r < crowded + NEXP):
                    round_of(r, sp.value_load(infoi[0:1, bass.ds(r - (NEXP - 1), 1)], min_val=0, max_val=NEXP - 1))
            sp.wait_ge(y_done, KT)
            sp.dma_start(out.rearrange("(k p) t -> p k t", p=P), res[:, :, 0:L]).then_inc(stored, 16)
            sp.wait_ge(stored, 16)

        @block.tensor
        def _(pe):
            mm = nc.tensor.matmul

            def wait_block(j, turn=0, per=0):
                slot, uses = block_at(j, turn, per)
                pe.wait_ge(raw_free[slot], uses)

            def three(dst, w, x, start, stop):
                mm(dst, w[0], x[0], start=start, stop=False)
                mm(dst, w[0], x[1], start=False, stop=False)
                return mm(dst, w[1], x[0], start=False, stop=stop)

            def hidden(k, n):
                return hhi[:, k, 0:n], hlo[:, k, 0:n]

            def weights(j, at):
                return whi[:, j % SPLIT, at:at + P], wlo[:, j % SPLIT, at:at + P]

            def modulation(r0, r1, bank=7, first=0):
                with pe.Fori(r0, r1) as r:
                    for s in range(RAW):
                        pe.wait_ge(raw_loaded[s], (r + 1) * 16)
                        for q in range(2):
                            dst = ps[bank][:, bass.ds(r * 24 + ((s * 2 + q) * 2 - first * 24), 2)]
                            for k in range(KT):
                                m = mm(dst, raw[:, s, k * 256 + q * P:k * 256 + q * P + P],
                                       scond[:, 2 * k:2 * k + 2], start=(k == 0), stop=(k == KT - 1))
                        m.then_inc(raw_free[s], 1)

            def filter_taps(h):
                pe.wait_ge(f_sin, 2)
                if h:
                    pe.wait_ge(f_taps, 1)
                for t in range(2):
                    for side in range(2):
                        m = mm(ps[2 * side + t][:, 0:HALF], sred[:, t * P:(t + 1) * P],
                               w3[:, side * HY + h * HALF:side * HY + (h + 1) * HALF], start=True, stop=True)
                m.then_inc(f_ps, 1)

            def filter_spectrum(h):
                pe.wait_ge(f_taps, h + 1)
                tiles = ((dft, 0, hs), (dft2, P, hs), (dft, P, hs), (dft2, 0, hd), (dft, 3 * P, hd))
                for m_, (table, at, src) in enumerate(tiles):
                    n = 5 * h + m_
                    if n >= 2:
                        pe.wait_ge(f_kcopy, n - 1)
                    for k in range(2):
                        m = mm(ps[4 + n % 2][:, 0:HALF], table[:, k, at:at + P], src[:, k, :],
                               start=(k == 0), stop=(k == 1))
                    m.then_inc(f_k, 1)
                pe.wait_ge(f_abs, h + 1)
                for c in range(3):
                    for i, src in enumerate((hf, hf, hb, hb)):
                        m = mm(ps[6][:, 3 * h + c:3 * h + c + 1], src[:, i % 2, c * P:(c + 1) * P], ones[:],
                               start=(i == 0), stop=(i == 3))
                m.then_inc(f_l1, 1)

            pe.wait_ge(c_filt, 16 * 6)
            mm(ps[0][0:64, 0:L], w12[0:33, 0:64], zt[:], start=True, stop=True).then_inc(f_ps, 1)
            pe.wait_ge(silu_c, 1)
            modulation(0, 1)
            pe.wait_ge(f_sin, 1)
            mm(ps[1][0:64, 0:L], w12[0:64, 64:128], sred[:], start=True, stop=True).then_inc(f_ps, 1)
            modulation(1, 2)
            filter_taps(0)
            modulation(2, 3)
            pe.wait_ge(setup, 1)
            filter_spectrum(0)
            filter_taps(1)
            modulation(3, 4)
            filter_spectrum(1)

            def norm_mean(n, s, width):
                pe.wait_ge(n_sum, 7 * n + 7)
                if n == 0:
                    pe.wait_ge(f_il1, 1)
                mm(ps[6][:, 0:width], mean[:], s[:, 0:width], start=True, stop=True).then_inc(n_mean, 1)

            norm_mean(0, ssum0, T)
            modulation(4, 8, 3, 4)

            def transpose_u(c):
                pe.wait_ge(u_made, c + 1)
                if c >= 2:
                    pe.wait_ge(ut_copy, c - 1)
                for s in range(4):
                    m = nc.tensor.transpose(ps[4 + c % 2][:, s * P:(s + 1) * P], u[:, c, s * P:(s + 1) * P], ident[:])
                m.then_inc(ut_ps, 1)

            for n in range(2 * WIN):
                j, q = n // 2, n % 2
                if q == 0:
                    wait_block(J_WIN + j)
                if n >= 4:
                    pe.wait_ge(w_free, n - 3)
                if n == 3:
                    pe.wait_ge(mods, 1)
                for k in range(KT):
                    if n == 0:
                        pe.wait_ge(n_ready, k + 1)
                    m = three(ps[n % 4][:], weights(J_WIN + j, k * 256 + q * P), hidden(k, T), k == 0, k == KT - 1)
                m.then_inc(used if q else w_ps, 1)
                if n >= 9 and (n - 9) % 6 == 0:
                    transpose_u((n - 9) // 3)
                    transpose_u((n - 9) // 3 + 1)
            transpose_u(4)
            transpose_u(5)

            pe.wait_ge(c_four, 32)
            pe.wait_ge(w_free, 2 * WIN)
            for q in range(2):
                for s in range(4):
                    m = mm(ps[2 * q + s // 2][:, (s % 2) * 256:(s % 2) * 256 + 256], fnt[:, q, s * P:(s + 1) * P],
                           bdft[:], start=True, stop=True)
                m.then_inc(fn_ab, 1)
            pe.wait_ge(ut_copy, HT)
            for q in range(2):
                pe.wait_ge(fn_abc, q + 1)
                ab = tmp[:, 2 * q:2 * q + 2, :].rearrange("p a (b n) -> p (a b) n", b=2)
                for s in range(2):
                    for i in range(4):
                        k, part = i // 2, i % 2
                        m = mm(ps[4 + q][:, s * L:(s + 1) * L], ab[:, 2 * s + k, part * P:(part + 1) * P],
                               tabs[:, k, part * L:(part + 1) * L], start=(i == 0), stop=(i == 3))
                m.then_inc(m_ps, 1)

            tok = utok[:].rearrange("p (s k) c -> p s k c", s=2)
            inverse = tabs[:].rearrange("p a (b n) -> p (a b) n", b=2)

            def forward(i):
                if i >= 2:
                    pe.wait_ge(x_prod, i - 1)
                for part in range(4):
                    for k in range(2):
                        m = mm(half(ps[2 * (i % 2) + part // 2][:, (part % 2) * 256:(part % 2) * 256 + 256]),
                               dft[:, k, part * P:(part + 1) * P], tok[:, :, k, i * P:(i + 1) * P],
                               start=(k == 0), stop=(k == 1))
                m.then_inc(x_ps, 1)

            def backward(i):
                pe.wait_ge(x_spec, i + 1)
                if i == 0:
                    pe.wait_ge(c_g, 16)
                if i >= 2:
                    pe.wait_ge(m_z, i - 1)
                else:
                    pe.wait_ge(m_ready, i + 1)
                for s in range(2):
                    for part in range(4):
                        spec = tmp[:, 2 * (part // 2), :].rearrange("p (m s c) -> p m s c", m=2, s=2)
                        m = mm(ps[4 + i % 2][:, s * L:(s + 1) * L], spec[:, part % 2, s, :], inverse[:, part, :],
                               start=(part == 0), stop=(part == 3))
                m.then_inc(m_ps, 1)

            forward(0)
            for i in range(HT):
                if i + 1 < HT:
                    forward(i + 1)
                backward(i)

            def project_out(j0, order, width, ready):
                for n in range(KT):
                    j, q = n // 2, n % 2
                    if q == 0:
                        wait_block(j0 + j)
                    if n >= 4:
                        pe.wait_ge(res_done, ready[0] + n - 3)
                    for i, k in enumerate(order):
                        if n == 0:
                            pe.wait_ge(m_ready, ready[1][i])
                        m = three(ps[n % 4][:, 0:width], weights(j0 + j, k * 256 + q * P), hidden(k, width),
                                  i == 0, i == KT - 1)
                    m.then_inc(used if q else o_ps, 1)

            project_out(J_WOUT, (6, 7, 0, 1, 2, 3, 4, 5), T, (0, range(1, 9)))
            norm_mean(1, ssum, T)

            def ffn_in(first, bank, free, turn, pair, per):
                for h in range(2):
                    j = first + h
                    wait_block(j, turn, per)
                    if h == 0 and free is not None:
                        pe.wait_ge(free, 2 * pair)
                    for q in range(2):
                        for kk in range(4):
                            k = 4 * h + kk
                            if free is None and bank == 0 and q == 0:
                                pe.wait_ge(n_ready, 8 + k + 1)
                            m = three(ps[bank + q][:], weights(j, kk * 256 + q * P), hidden(k, T),
                                      k == 0, k == KT - 1)
                    m.then_inc(used, 1)

            def ffn_down(first, turn, pair, per):
                wait_block(first, turn, per)
                wait_block(first + 1, turn, per)
                pe.wait_ge(ff_lo, 2 * pair + 2)
                for d in range(KT):
                    pe.wait_ge(ff_added, 8 * pair + d + 1)
                    m0 = three(ps[4 + d % 4][:], weights(first, d * P), (ahi[:, 0], alo[:, 0]), True, False)
                    m = three(ps[4 + d % 4][:], weights(first + 1, d * P), (ahi[:, 1], alo[:, 1]), False, True)
                    if d == KT - 1:
                        m0.then_inc(used, 1)
                    m.then_inc(used if d == KT - 1 else ff_d, 1)

            ffn_in(J_FFN, 0, None, 0, 0, 0)
            ffn_in(J_FFN + 2, 2, None, 0, 0, 0)
            with pe.Fori(0, FF_PAIRS - 1) as r:
                ffn_in(J_FFN + 4, 0, ff_silu, r, r + 1, 6)
                ffn_down(J_FFN + 6, r, r, 6)
                ffn_in(J_FFN + 8, 2, ff_a, r, r + 1, 6)
            ffn_down(J_FFN + FFN - 2, 0, FF_PAIRS - 1, 0)
            norm_mean(2, ssum, T)

            def qk_square(y):
                pe.wait_ge(q_sq, 1 if y == 0 else 1 + 2 * y)
                if y == 0:
                    pe.wait_ge(c_odd, 48)
                if y == 1:
                    pe.wait_ge(v_done, 1)
                if y == 2:
                    pe.wait_ge(q_root, 1)
                mm(ps[4 + y % 2][:], bd64[:], qsq[:, y], start=True, stop=True).then_inc(q_ms, 1)

            def qk_rotate(y):
                pe.wait_ge(q_n, y + 1)
                if y == 2:
                    pe.wait_ge(q_done, 1)
                mm(ps[6 + y % 2][:], rot[:], qn[:, y], start=True, stop=True).then_inc(q_rot, 1)

            def transpose_v():
                pe.wait_ge(v_copy, 1)
                for s in range(4):
                    m = nc.tensor.transpose(ps[5][:, s * P:(s + 1) * P], vt[:, s * P:(s + 1) * P], ident[:])
                m.then_inc(v_ps, 1)

            for n in range(2 * OWIN):
                j, q = n // 2, n % 2
                if q == 0:
                    wait_block(J_OWIN + j)
                if n >= 4:
                    pe.wait_ge(*oin_free(n - 4))
                width = T if n < 2 else L
                for k in range(KT):
                    if n == 0:
                        pe.wait_ge(n_ready, 16 + k + 1)
                    m = three(ps[n % 4][:, 0:width], weights(J_OWIN + j, k * 256 + q * P), hidden(k, width),
                              k == 0, k == KT - 1)
                m.then_inc(used if q else q_ps, 1)
                if n == 3:
                    qk_square(0)
                    transpose_v()
                if n == 6:
                    qk_rotate(0)
                    qk_square(1)
                if n == 8:
                    qk_square(2)
                if n == 9:
                    qk_rotate(1)
                if n == 11:
                    qk_rotate(2)

            pe.wait_ge(q_done, 3)
            pe.wait_ge(s_y, 4)
            for b in range(2):
                for x in range(8):
                    g = 8 * b + x
                    head = HEADS[x]
                    if g >= 4:
                        pe.wait_ge(a_ctx, g - 3)
                        pe.wait_ge(a_loc, g - 3)
                    else:
                        pe.wait_ge(*oin_free(14 + (x + 2) % 4))
                    mm(ps[x % 4][:], qt[:, head % 4, b * P:(b + 1) * P], kpad[:, head // 4, :],
                       start=True, stop=True).then_inc(a_s, 1)
                for x in range(9):
                    g = 8 * b + x
                    if x < 8:
                        pe.wait_ge(a_p, g + 1)
                        if g >= 2:
                            pe.wait_ge(a_tc, g - 1)
                        for s in range(4):
                            m = nc.tensor.transpose(ps[4 + x % 2][:, s * P:(s + 1) * P],
                                                    sc[:, x, s * P:(s + 1) * P], ident[:])
                        m.then_inc(a_t, 1)
                    if x >= 1:
                        y = x - 1
                        pe.wait_ge(a_tc, g)
                        if b == 0 and y == 0:
                            pe.wait_ge(v_done, 1)
                        for s in range(4):
                            m = mm(ps[6 + b][:, (y // 2) * P:(y // 2 + 1) * P], vpad[:, s, y % 2, :],
                                   pt[:, y % 2, s, :], start=(s == 0 and y % 2 == 0), stop=(s == 3 and y % 2 == 1))
                        m.then_inc(a_o, 1)

            pe.wait_ge(a_ctx, 16)
            pe.wait_ge(a_loc, 16)
            project_out(J_OWOUT, (4, 5, 6, 7, 0, 1, 2, 3), L, (16, (9, 9, 9, 9, 11, 11, 11, 11)))
            pe.wait_ge(res_done, 16 + KT)
            norm_mean(3, ssum, L)

            pe.wait_ge(n_ready, 32)
            pe.wait_ge(c_moe, 64)
            for t in range(2):
                for k in range(KT):
                    m = mm(ps[6][:, t * NEXP:(t + 1) * NEXP], ht[:, k, t * P:(t + 1) * P], rw[:, k, :],
                           start=(k == 0), stop=(k == KT - 1))
            m.then_inc(r_lg, 1)
            for t in range(2):
                for h in range(2):
                    for i in range(4):
                        m = nc.tensor.transpose(ps[2 * t + h][:, i * P:(i + 1) * P],
                                                ht[:, 4 * h + i, t * P:(t + 1) * P], ident[:])
                    m.then_inc(t_ps, 1)
            pe.wait_ge(r_sel, 1)
            mm(ps[7][:, 0:8], tri[:, 0], sel[:, 0], start=True, stop=True)
            mm(ps[7][:, 8:16], tri[:, 1], sel[:, 0], start=True, stop=False)
            mm(ps[7][:, 8:16], tri[:, 0], sel[:, 1], start=False, stop=True)
            mm(ps[7][:, 16:24], tri[:, 1], sel[:, 0], start=True, stop=False)
            mm(ps[7][:, 16:24], tri[:, 1], sel[:, 1], start=False, stop=True).then_inc(r_pos, 1)

            def gather(h, made):
                pe.wait_ge(hot_made, made)
                for kk in range(4):
                    k = 4 * h + kk
                    for i in range(4):
                        src = hklo if i % 2 else hkhi
                        m = mm(ps[7][:, kk * P:(kk + 1) * P], src[:, i // 2, k * P:(k + 1) * P], hot[:, i // 2],
                               start=(i == 0), stop=(i == 3))
                m.then_inc(misc, 1)

            def scatter(q):
                for kk in range(2):
                    k = 2 * q + kk
                    mm(ps[7][:, kk * L:(kk + 1) * L], yhi[:, k * P:(k + 1) * P], hott[:], start=True, stop=False)
                    m = mm(ps[7][:, kk * L:(kk + 1) * L], ylo[:, k * P:(k + 1) * P], hott[:], start=False, stop=True)
                m.then_inc(misc, 1)

            pe.wait_ge(t_lo, 4)
            gather(0, 1)
            pe.wait_ge(misc_free, 1)
            gather(1, 1)

            def round_of(r):
                def block_wait(i):
                    wait_block(J_MOE + i, r, ROUND_BLOCKS)
                    return J_MOE + i

                def rhs(j, at):
                    return whi[:, j % SPLIT, at:at + CHUNK], wlo[:, j % SPLIT, at:at + CHUNK]

                def chunk_in(c, first, bank):
                    for h in range(2):
                        j = block_wait(first + h)
                        for kk in range(4):
                            k = 4 * h + kk
                            w = rhs(j, kk * CHUNK)
                            mm(ps[bank][:], ghi[:, k], w[0], start=(k == 0), stop=False)
                            mm(ps[bank][:], ghi[:, k], w[1], start=False, stop=False)
                            m = mm(ps[bank][:], glo[:, k], w[0], start=False, stop=(k == KT - 1))
                        m.then_inc(used, 1)

                def gate(c):
                    if c == 0:
                        pe.wait_ge(misc_free, 7 * r + 2)
                    pe.wait_ge(e_a, NCH * r + (max(c - 1, 0) + 1))
                    chunk_in(c, gate_block(c), c % 2)

                def up(c):
                    chunk_in(c, gate_block(c) + 2, 2 + c % 2)

                def turn(c):
                    pe.wait_ge(e_a, NCH * r + (c + 2))
                    pe.wait_ge(e_lo, NCH * r + (c + 1))
                    for i in range(4):
                        m = nc.tensor.transpose(ps[6][:, i * P:(i + 1) * P], am[:, i * P:(i + 1) * P], ident[:])
                    m.then_inc(e_t, 1)

                def down(c):
                    pe.wait_ge(e_lo, NCH * r + (c + 2))
                    if c == 0:
                        pe.wait_ge(e_y, r + 1)
                    for h in range(2):
                        j = block_wait(down_block(c) + h)
                        for i in range(4):
                            f, n = 2 * h + i // 2, i % 2
                            w = rhs(j, (i // 2) * D + n * CHUNK)
                            mm(ps[4 + n][:], athi[:, f], w[0], start=(c == 0 and f == 0), stop=False)
                            mm(ps[4 + n][:], athi[:, f], w[1], start=False, stop=False)
                            m = mm(ps[4 + n][:], atlo[:, f], w[0], start=False, stop=(c == NCH - 1 and f == 3))
                        m.then_inc(used, 1)

                def spare(i):
                    pe.wait_ge(misc_free, 2 + 7 * r + i)

                for c in range(NCH):
                    gate(c)
                    if c:
                        turn(c - 1)
                    up(c)
                    if c == NCH - 1:
                        spare(5)
                        gather(0, r + 2)
                    if c:
                        down(c - 1)
                    if c == 0:
                        pe.wait_ge(e_y, r + 1)
                    if c < 4:
                        spare(c)
                        scatter(c)
                    if c == 4:
                        spare(4)
                        for t in range(2):
                            nc.tensor.transpose(ps[7][:, t * P:(t + 1) * P], hot[:, t].bitcast(F32), ident[:])
                        for t in range(2):
                            m = mm(ps[7][:, 256:257], hot[:, t].bitcast(F32), cw[:, t:t + 1],
                                   start=(t == 0), stop=(t == 1))
                        m.then_inc(misc, 1)
                turn(NCH - 1)
                spare(6)
                gather(1, r + 2)
                down(NCH - 1)

            with pe.Fori(0, NEXP) as r:
                round_of(r)
            crowded = pe.value_load(infoi[0:1, 0:1], min_val=0, max_val=OVER)
            with pe.Fori(NEXP, NEXP + OVER) as r:
                with pe.If(r < crowded + NEXP):
                    round_of(r)
            pe.wait_ge(e_y, crowded + (NEXP + 1))
            for q in range(4):
                pe.wait_ge(misc_free, crowded * 7 + (2 + 7 * NEXP + q))
                scatter(q)

        @block.scalar
        def _(act):
            def copy(dst, src, scale=1.0):
                return nc.scalar.activation(dst, src, ACT.Copy, scale=scale)

            def split(j, turn=0, per=0, n=BLK):
                slot, uses = block_at(j, turn, per)
                act.wait_ge(raw_loaded[slot], uses * 16)
                if per or j >= SPLIT:
                    act.wait_ge(used, turn * per + (j - SPLIT + 1) if per else j - SPLIT + 1)
                copy(whi[:, j % SPLIT, 0:n], raw[:, slot, 0:n]).then_inc(hi_made, 1)

            done = [0]

            def until(j_end):
                while done[0] < j_end:
                    j = done[0]
                    split(j, n=BLK // 2 if J_FFN <= j < J_OWIN else BLK)
                    done[0] += 1

            for src, dst in ((a["c_vec"], vec[:]), (a["c_sq"][0], ident[:]), (a["c_sq"][1], mean[:])):
                act.dma_start(dst, src).then_inc(c_even, 16)
            for src, dst in ((a["c_z"], zt[:]), (a["c_w12"], w12[:]), (a["c_w3"], w3[:])):
                act.dma_start(dst, src).then_inc(c_filt, 16)
            for src, dst in ((a["c_decay"], decay[:]), (a["c_dft"], dft[:]), (a["c_dft2"], dft2[:])):
                act.dma_start(dst, src).then_inc(c_filt, 16)
            act.dma_start(xin[:], a["xt"].rearrange("(k p) t -> p k t", p=P)).then_inc(c_x, 16)
            act.wait_ge(c_even, 48)
            nc.scalar.activation(scond[:], col("cond", 0, 16), ACT.Silu).then_inc(silu_c, 1)
            for i in range(2):
                act.wait_ge(f_arg, i + 1)
                nc.scalar.activation(sred[:], sarg[:], ACT.Sin).then_inc(f_sin, 1)
            for h in range(2):
                act.wait_ge(f_taps, h + 1)
                nc.scalar.activation(hf[:], hf[:], ACT.Abs)
                nc.scalar.activation(hb[:], hb[:], ACT.Abs).then_inc(f_abs, 1)
                for m in range(5):
                    act.wait_ge(f_k, 5 * h + m + 1)
                    copy(kf[:, m, h * HALF:(h + 1) * HALF], ps[4 + (5 * h + m) % 2][:, 0:HALF]).then_inc(f_kcopy, 1)

            def norm_act(n, src, ready, sqb, rs, width, h_free, full=None):
                for d in range(KT):
                    act.wait_ge(*ready(d))
                    if d >= 2:
                        act.wait_ge(n_sum, 7 * n + max(1, d - 2))
                    nc.scalar.activation(sqb[:, d % 2, 0:width], src[:, d, 0:width], ACT.Square).then_inc(n_sq, 1)
                act.wait_ge(n_mean, n + 1)
                nc.scalar.activation(rs[:, 0:width], ps[6][:, 0:width], ACT.Sqrt, bias=eps[:]).then_inc(n_root, 1)
                act.wait_ge(used, h_free) if h_free else None
                for d in range(KT):
                    act.wait_ge(n_h, 8 * n + d + 1)
                    h = sqb[:, d % 2, 0:width] if full is None else full[:, d, :]
                    copy(hhi[:, d, 0:width], h).then_inc(n_hi, 1)

            act.wait_ge(setup, 2)
            norm_act(0, xin, lambda d: (c_x, 16), sq0, rstd0, T, 0)

            for n, tile in enumerate(WIN_TILES):
                until(J_WIN + n // 2 + 3)
                act.wait_ge(*((used, n // 2 + 1) if n % 2 else (w_ps, n // 2 + 1)))
                if n < 2:
                    copy(fnt[:, n], ps[n % 4][:]).then_inc(w_free, 1)
                    continue
                i, kind, q = (n - 2) // 6, (n - 2) % 6 // 2, n % 2
                dst = (tmp[:, q], tmp[:, 2 + q], x0c[:, 2 * i + q])[kind]
                if kind < 2 and i:
                    act.wait_ge(u_made, 2 * i)
                nc.scalar.activation(dst, ps[n % 4][:], ACT.Identity, scale=col("short", 18 + tile)).then_inc(w_mid, 1)

                def copy_u(c):
                    act.wait_ge(ut_ps, c + 1)
                    copy(utok[:, :, c * P:(c + 1) * P],
                         ps[4 + c % 2][:].rearrange("p (s c) -> p s c", s=4)).then_inc(ut_copy, 1)

                if n >= 9 and (n - 9) % 6 == 0:
                    copy_u((n - 9) // 3)
                    copy_u((n - 9) // 3 + 1)
            copy_u(4)
            copy_u(5)
            act.wait_ge(u_made, HT)
            for q in range(2):
                act.wait_ge(fn_ab, q + 1)
                copy(tmp[:, 2 * q], ps[2 * q][:])
                copy(tmp[:, 2 * q + 1], ps[2 * q + 1][:]).then_inc(fn_abc, 1)
            for i in range(HT):
                nc.scalar.activation(u[:, i], u[:, i], ACT.Identity, scale=col("skip", i)).then_inc(skips, 1)
            for q in range(2):
                act.wait_ge(m_ps, q + 1)
                copy(hhi[:, HT + q], ps[4 + q][:]).then_inc(m_hi, 1)
            for i in range(HT):
                act.wait_ge(m_z, i + 1)
                copy(hhi[:, i], x0c[:, i]).then_inc(m_hi, 1)

            until(J_WOUT + 3)
            for j in range(WOUT):
                act.wait_ge(used, J_WOUT + j + 1)
                until(J_WOUT + j + 4)
            norm_act(1, res, lambda d: (res_done, d + 1), sq, rstd, T, J_FFN)

            def silu(turn):
                for q in range(2):
                    act.wait_ge(ff_lo, turn)
                    nc.scalar.activation(sil[:, q], ps[q][:], ACT.Silu).then_inc(ff_silu, 1)

            def split_a(turn):
                for q in range(2):
                    act.wait_ge(ff_a, turn + q + 1)
                    copy(ahi[:, q], sil[:, q]).then_inc(ff_hi, 1)

            until(J_FFN + 4)
            act.wait_ge(used, J_FFN + 2)
            silu(0)
            until(J_FFN + 6)
            split_a(0)
            with act.Fori(0, FF_PAIRS - 1) as r:
                for x in range(2, 5):
                    split(J_FFN + 4 + x, r, 6, BLK // 2)
                act.wait_ge(used, r * 6 + (J_FFN + 6))
                silu(r * 2 + 2)
                for x in range(5, 8):
                    split(J_FFN + 4 + x, r, 6, BLK // 2)
                split_a(r * 2 + 2)
            done[0] = J_FFN + FFN
            until(J_OWIN + 1)
            norm_act(2, res, lambda d: (res_done, 8 + d + 1), sq, rstd, T, J_FFN + FFN - 2)

            def qk_root(y):
                act.wait_ge(q_ms, y + 1)
                act.wait_ge(q_n, y) if y else None
                nc.scalar.activation(rr[:], ps[4 + y % 2][:], ACT.Sqrt, bias=eps[:]).then_inc(q_root, 1)

            for n in range(2 * OWIN):
                until(min(J_OWIN + n // 2 + 3, J_MOE))
                if n < 6 or (n - 6) % 3 == 0:
                    act.wait_ge(*((used, J_OWIN + n // 2 + 1) if n % 2 else (q_ps, n // 2 + 1)))
                src = ps[n % 4]
                if n == 0:
                    nc.scalar.activation(qsq[:, 0], src[:], ACT.Square).then_inc(q_sq, 1)
                    copy(qraw[:, 0], src[:]).then_inc(q_raw, 1)
                elif n == 1:
                    copy(vt[:], src[:]).then_inc(v_copy, 1)
                elif n < 6:
                    y, at = n // 2, (n % 2) * L
                    nc.scalar.activation(qsq[:, y, at:at + L], src[:, 0:L], ACT.Square).then_inc(q_sq, 1)
                    copy(qraw[:, y, at:at + L], src[:, 0:L]).then_inc(q_raw, 1)
                elif (n - 6) % 3 == 0:
                    if n > 6:
                        act.wait_ge(s_hx, (n - 6) // 3)
                    copy(gcs[:], src[:, 0:L]).then_inc(s_gc, 1)
                if n == 4:
                    qk_root(0)
                if n == 7:
                    qk_root(1)
                if n == 9:
                    qk_root(2)
            act.wait_ge(used, J_OWOUT)
            act.wait_ge(s_y, 4)
            copy(hhi[:, 4:8, 0:L], ysc[:]).then_inc(m_hi, 1)

            for b in range(2):
                for x in range(8):
                    g = 8 * b + x
                    act.wait_ge(a_s, g + 1)
                    copy(sc[:, x, L:T], ps[x % 4][:, L:T], 0.125).then_inc(a_ctx, 1)
                act.wait_ge(a_max, b + 1)
                nc.scalar.activation(esink[:], esink[:], ACT.Exp).then_inc(a_sink, 1)
                for x in range(8):
                    nc.scalar.activation(sc[:, x], sc[:, x], ACT.Exp, bias=nmax[:, x:x + 1],
                                         accum_out=ssm[:, x:x + 1]).then_inc(a_exp, 1)
                for x in range(8):
                    g = 8 * b + x
                    act.wait_ge(a_t, g + 1)
                    if g >= 2:
                        act.wait_ge(a_o, g - 1)
                    copy(pt[:, x % 2], ps[4 + x % 2][:].rearrange("p (s c) -> p s c", s=4)).then_inc(a_tc, 1)
                act.wait_ge(a_o, 8 * b + 8)
                copy(hhi[:, 0:4, b * P:(b + 1) * P],
                     ps[6 + b][:].rearrange("p (k c) -> p k c", k=4)).then_inc(m_hi, 1)
            for j in range(OWOUT):
                act.wait_ge(used, J_OWOUT + j + 1)
                until(min(J_OWOUT + j + 4, J_MOE))
            norm_act(3, res, lambda d: (res_done, 16 + d + 1), sq, rstd, L, J_MOE, full=ht)

            act.wait_ge(r_sub, 1)
            nc.scalar.activation(ex[:], ex[:], ACT.Exp).then_inc(r_exp, 1)
            for i in range(4):
                act.wait_ge(t_ps, i + 1)
                copy(hkhi[:, i // 2, (i % 2) * 512:(i % 2) * 512 + 512], ps[i][:]).then_inc(t_hi, 1)

            def split_gathered(h, count, gathered):
                act.wait_ge(misc, count)
                copy(ghi[:, 4 * h:4 * h + 4, :], ps[7][:].rearrange("p (k c) -> p k c", k=4)).then_inc(g_hi, 1)

            split_gathered(0, 1, 0)
            split_gathered(1, 2, 0)

            def result_hi():
                for n in range(2):
                    nc.scalar.activation(yhi[:, n * CHUNK:(n + 1) * CHUNK], ps[4 + n][:], ACT.Identity,
                                         scale=wslot[:]).then_inc(e_yhi, 1)

            act.wait_ge(zeroed, 4)
            act.wait_ge(e_a, 1)
            act.wait_ge(e_lo, 1)

            def round_of(r):
                def chunk_hi(c):
                    act.wait_ge(e_t, NCH * r + c + 1)
                    copy(athi[:], ps[6][:].rearrange("p (k c) -> p k c", k=4)).then_inc(e_hi, 1)

                for x in range(ROUND_BLOCKS):
                    if x == 3:
                        act.wait_ge(used, r * ROUND_BLOCKS + J_MOE)
                        act.wait_ge(misc_free, 7 * r + 2)
                        result_hi()
                    for c in range(NCH):
                        if x == gate_block(c) + 4:
                            act.wait_ge(used, r * ROUND_BLOCKS + (J_MOE + gate_block(c) + 2))
                            act.wait_ge(e_a, NCH * r + (c + 1))
                            nc.scalar.activation(sg[:], ps[c % 2][:], ACT.Silu).then_inc(e_silu, 1)
                        if c < NCH - 1 and x == down_block(c):
                            chunk_hi(c)
                    if x == 30:
                        act.wait_ge(misc, 7 * r + 7)
                        copy(hott[:], ps[7][:, 0:L])
                        copy(wslot[:], ps[7][:, L:L + 1]).then_inc(misc_free, 1)
                    if x == 40:
                        split_gathered(0, 7 * r + 8, r)
                    split(J_MOE + x, r, ROUND_BLOCKS)
                chunk_hi(NCH - 1)
                split_gathered(1, 7 * r + 9, r)

            with act.Fori(0, NEXP) as r:
                round_of(r)
            crowded = act.value_load(infoi[0:1, 0:1], min_val=0, max_val=OVER)
            with act.Fori(NEXP, NEXP + OVER) as r:
                with act.If(r < crowded + NEXP):
                    round_of(r)
            act.wait_ge(used, crowded * ROUND_BLOCKS + (NEXP * ROUND_BLOCKS + J_MOE))
            result_hi()

        @block.vector
        def _(dve):
            vv = nc.vector
            own = Steps(dve, dve_s)

            def split(j, turn=0, per=0, n=BLK):
                slot, uses = block_at(j, turn, per)
                if slot == POOL_SLOT:
                    return
                dve.wait_ge(hi_made, turn * per + (j + 1) if per else j + 1)
                vv.tensor_tensor(wlo[:, j % SPLIT, 0:n], raw[:, slot, 0:n], whi[:, j % SPLIT, 0:n].bitcast(F32),
                                 ALU.subtract).then_inc(raw_free[slot], 1)

            done = [0]

            def until(j_end):
                while done[0] < j_end:
                    j = done[0]
                    split(j, n=BLK // 2 if J_FFN <= j < J_OWIN else BLK)
                    done[0] += 1

            dve.wait_ge(c_even, 48)
            for i in range(2):
                dve.wait_ge(f_ps, i + 1)
                if i:
                    dve.wait_ge(f_sin, 1)
                own.step(vv.tensor_scalar(sarg[:], ps[i][0:64, 0:L], col("b1" if i == 0 else "b2")[0:64],
                                          col("freq")[0:64], ALU.add, ALU.mult))
                own.step(vv.tensor_scalar(rstd0[0:64, 0:L], sarg[:], float(1 / (2 * np.pi)), ROUND, ALU.mult, ALU.add))
                own.step(vv.tensor_scalar(rstd0[0:64, 0:L], rstd0[0:64, 0:L], ROUND, None, ALU.subtract))
                for part in TURN:
                    own.step(vv.scalar_tensor_tensor(out=sarg[:], in0=rstd0[0:64, 0:L], scalar=-part, in1=sarg[:],
                                                     op0=ALU.mult, op1=ALU.add))
                vv.tensor_scalar(sarg[:], sarg[:], 3.1415925, -3.1415925, ALU.min, ALU.max).then_inc(f_arg, 1)
            dve.wait_ge(c_filt, 16 * 6)
            for h in range(2):
                dve.wait_ge(f_ps, 3 + h)
                if h:
                    dve.wait_ge(f_l1, 1)
                for t in range(2):
                    vv.tensor_tensor(hf[:, t], ps[t][:, 0:HALF], decay[:, t, h * HALF:(h + 1) * HALF], ALU.mult)
                    m = vv.tensor_tensor(hb[:, t], ps[2 + t][:, 0:HALF], decay[:, t, h * HALF:(h + 1) * HALF], ALU.mult)
                own.step(m)
                own.step(vv.memset(hb[0:1, 0, :], 0.0))
                vv.tensor_tensor(hs[:], hf[:], hb[:], ALU.add)
                vv.tensor_tensor(hd[:], hf[:], hb[:], ALU.subtract).then_inc(f_taps, 1)
            dve.wait_ge(f_l1, 2)
            vv.reciprocal(il1[:], ps[6][:, 0:HT]).then_inc(f_il1, 1)

            def modulations(mod, bank, bias, norms, g, done=None):
                dst = mod[:]
                own.step(vv.tensor_tensor(dst, ps[bank][:, 0:96].rearrange("p (t c) -> p t c", c=2),
                                          col(bias, 0, 48).unsqueeze(2).to_broadcast([P, 48, 2]), ALU.add))
                for i in range(2):
                    m = vv.scalar_tensor_tensor(out=gain[:, g + i], in0=mod[:, 8 + 24 * i:16 + 24 * i, :], scalar=1.0,
                                                in1=col(norms[i], 0, 8).unsqueeze(2).to_broadcast([P, 8, 2]),
                                                op0=ALU.add, op1=ALU.mult)
                if done is None:
                    own.step(m)
                else:
                    m.then_inc(done, 1)

            def norm_dve(n, src, sqb, rs, width, mod, shift, full=None):
                dve.wait_ge(n_root, n + 1)
                own.step(vv.reciprocal(rs[:, 0:width], rs[:, 0:width]))

                def lo(d):
                    dve.wait_ge(n_hi, 8 * n + d + 1)
                    h = sqb[:, d % 2, 0:width] if full is None else full[:, d, :]
                    vv.tensor_tensor(hlo[:, d, 0:width], h, hhi[:, d, 0:width].bitcast(F32),
                                     ALU.subtract).then_inc(n_ready, 1)

                for d in range(KT):
                    h = sqb[:, d % 2, 0:width] if full is None else full[:, d, :]
                    if d >= 2:
                        dve.wait_ge(n_ready, 8 * n + d - 1)
                    own.step(vv.tensor_tensor(h, src[:, d, 0:width], rs[:, 0:width], ALU.mult))
                    for s in range(width // L):
                        m = vv.tensor_scalar(h[:, s * L:(s + 1) * L], h[:, s * L:(s + 1) * L], gain[:, n, d, s:s + 1],
                                             mod[:, shift + d, s:s + 1], ALU.mult, ALU.add)
                    m.then_inc(n_h, 1)
                    if d:
                        lo(d - 1)
                lo(KT - 1)

            dve.wait_ge(raw_free[RAW - 1], 4)
            modulations(emod, 7, "e_ada_b", ("e_norm1", "e_norm2"), 0)
            norm_dve(0, xin, sq0, rstd0, T, emod, 0)
            dve.wait_ge(raw_free[RAW - 1], 8)
            modulations(omod, 3, "o_ada_b", ("o_norm1", "o_norm2"), 2, mods)
            dve.wait_ge(mods, 1)

            for n, tile in enumerate(WIN_TILES):
                until(J_WIN + n // 2 + 3)
                if n < 2:
                    continue
                i, kind, q = (n - 2) // 6, (n - 2) % 6 // 2, n % 2
                dst = half((tmp[:, q], tmp[:, 2 + q], x0c[:, 2 * i + q])[kind])
                src = half(ps[n % 4][:])
                dve.wait_ge(w_mid, n - 1)
                own.step(vv.scalar_tensor_tensor(out=dst[:, :, 1:L], in0=src[:, :, 0:L - 1], scalar=col("short", tile),
                                                 in1=dst[:, :, 1:L], op0=ALU.mult, op1=ALU.add))
                vv.scalar_tensor_tensor(out=dst[:, :, 0:L - 1], in0=src[:, :, 1:L], scalar=col("short", 36 + tile),
                                        in1=dst[:, :, 0:L - 1], op0=ALU.mult, op1=ALU.add).then_inc(w_free, 1)
                if kind == 1:
                    dve.wait_ge(w_free, n + 1)
                    vv.tensor_tensor(u[:, 2 * i + q], tmp[:, q], tmp[:, 2 + q], ALU.mult).then_inc(u_made, 1)

            for q in range(2):
                dve.wait_ge(m_hi, q + 1)
                vv.tensor_tensor(hlo[:, HT + q], ps[4 + q][:], hhi[:, HT + q].bitcast(F32),
                                 ALU.subtract).then_inc(m_ready, 1)

            def products(i):
                dve.wait_ge(x_ps, i + 1)
                dve.wait_ge(m_ps, i + 2)
                at = slice(i * P, (i + 1) * P)
                re, im = ps[2 * (i % 2)], ps[2 * (i % 2) + 1]
                pairs = ((re, kf[:, 0:3:2, at]), (im, kf[:, 3:5, at]), (re, kf[:, 3:5, at]), (im, kf[:, 1:3, at]))
                for n, (x, k) in enumerate(pairs):
                    m = vv.tensor_tensor(tmp[:, n].rearrange("p (m s c) -> p m s c", m=2, s=2),
                                         x[:].rearrange("p (m s c) -> p m s c", m=2, s=2),
                                         k.unsqueeze(2).to_broadcast([P, 2, 2, P]), ALU.mult)
                m.then_inc(x_prod, 1)

            def result(i):
                dve.wait_ge(m_ps, i + 3)
                dve.wait_ge(skips, i + 1)
                own.step(vv.scalar_tensor_tensor(out=u[:, i], in0=ps[4 + i % 2][:], scalar=il1[:, i:i + 1],
                                                 in1=u[:, i], op0=ALU.mult, op1=ALU.add))
                vv.tensor_tensor(x0c[:, i], u[:, i], x0c[:, i], ALU.mult).then_inc(m_z, 1)

            def result_lo(i):
                dve.wait_ge(m_hi, 3 + i)
                vv.tensor_tensor(hlo[:, i], x0c[:, i], hhi[:, i].bitcast(F32), ALU.subtract).then_inc(m_ready, 1)

            products(0)
            for i in range(HT):
                if i + 1 < HT:
                    products(i + 1)
                result(i)
                if i:
                    result_lo(i - 1)
            result_lo(HT - 1)

            def residual(n, j, base, mod, width, lookahead):
                until(lookahead)
                dve.wait_ge(*((used, j + 1) if n % 2 else (o_ps, base // 2 + n // 2 + 1)))
                for s in range(width // L):
                    m = vv.scalar_tensor_tensor(out=res[:, n, s * L:(s + 1) * L], in0=ps[n % 4][:, s * L:(s + 1) * L],
                                                scalar=mod[:, 16 + n, s:s + 1], in1=res[:, n, s * L:(s + 1) * L],
                                                op0=ALU.mult, op1=ALU.add)
                m.then_inc(res_done, 1)

            until(J_WOUT + 3)
            dve.wait_ge(c_res, 16)
            for n in range(KT):
                residual(n, J_WOUT + n // 2, 0, emod, T, J_WOUT + n // 2 + 3)
            norm_dve(1, res, sq, rstd, T, emod, 24)

            def add_down(turn, last):
                for d in range(KT):
                    if d < KT - 1:
                        dve.wait_ge(ff_d, turn * 7 + d + 1)
                    else:
                        dve.wait_ge(used, last)
                    dve.wait_ge(ff_added, turn * 8 + (d + 1))
                    vv.tensor_tensor(facc[:, d], facc[:, d], ps[4 + d % 4][:], ALU.add).then_inc(ff_added, 1)

            def activate(turn, last):
                dve.wait_ge(used, last)
                for q in range(2):
                    dve.wait_ge(ff_silu, turn * 2 + (q + 1))
                    vv.tensor_tensor(sil[:, q], sil[:, q], ps[2 + q][:], ALU.mult).then_inc(ff_a, 1)
                for q in range(2):
                    dve.wait_ge(ff_hi, turn * 2 + (q + 1))
                    vv.tensor_tensor(alo[:, q], sil[:, q], ahi[:, q].bitcast(F32), ALU.subtract).then_inc(ff_lo, 1)

            until(J_FFN + 6)
            activate(0, J_FFN + 4)
            with dve.Fori(0, FF_PAIRS - 1) as r:
                for x in range(2, 5):
                    split(J_FFN + 4 + x, r, 6, BLK // 2)
                add_down(r, r * 6 + (J_FFN + 8))
                for x in range(5, 8):
                    split(J_FFN + 4 + x, r, 6, BLK // 2)
                activate(r + 1, r * 6 + (J_FFN + 10))
            done[0] = J_FFN + FFN
            add_down(FF_PAIRS - 1, J_FFN + FFN)
            for d in range(KT):
                dve.wait_ge(ff_added, 4 + 8 * FF_PAIRS) if d == 0 else None
                for s in range(2):
                    m = vv.scalar_tensor_tensor(out=res[:, d, s * L:(s + 1) * L], in0=facc[:, d, s * L:(s + 1) * L],
                                                scalar=emod[:, 40 + d, s:s + 1], in1=res[:, d, s * L:(s + 1) * L],
                                                op0=ALU.mult, op1=ALU.add)
                m.then_inc(res_done, 1)
            until(J_OWIN + 1)
            norm_dve(2, res, sq, rstd, T, omod, 0)

            def qk_norm(y):
                dve.wait_ge(q_root, y + 1)
                own.step(vv.reciprocal(rr[:], rr[:]))
                dve.wait_ge(q_raw, 1 + 2 * y)
                vv.scalar_tensor_tensor(out=qn[:, y], in0=qraw[:, y], scalar=col("q_norm" if y else "k_norm"),
                                        in1=rr[:], op0=ALU.mult, op1=ALU.mult).then_inc(q_n, 1)

            def qk_turn(y):
                dve.wait_ge(q_rot, y + 1)
                n = T if y else L
                dve.wait_ge(zeroed, 2)
                for dst, src, i in ((qsq, qn[:, y, 0:n], 0), (qraw, ps[6 + y % 2][:, 0:n], 1)):
                    d = dst[:, y, 0:n]
                    if y:
                        m = vv.tensor_tensor(half(d), half(src), rope[:, i:i + 1, :].to_broadcast([P, 2, L]), ALU.mult)
                    else:
                        m = vv.tensor_tensor(d, src, rope[:, i, :], ALU.mult)
                own.step(m)
                if y:
                    vv.tensor_tensor(qt[:, 2 * y - 2:2 * y, :], half(qsq[:, y]), half(qraw[:, y]),
                                     ALU.add).then_inc(q_done, 1)
                else:
                    for g in range(2):
                        rows = slice(64 * g, 64 * g + 64)
                        vv.tensor_tensor(kpad[rows, g, 0:L], qsq[rows, 0, 0:L], qraw[rows, 0, 0:L], ALU.add)
                        m = vv.tensor_copy(kpad[rows, g, L:T], qn[rows, 0, L:T])
                    m.then_inc(q_done, 1)

            def pad_v():
                dve.wait_ge(v_ps, 1)
                dve.wait_ge(zeroed, 2)
                v = ps[5][:].rearrange("p (s c) -> p s c", s=4)
                vv.tensor_copy(vpad[:, :, 0, 0:64], v[:, :, 0:64])
                vv.tensor_copy(vpad[:, :, 1, 64:128], v[:, :, 64:128]).then_inc(v_done, 1)

            for n in range(2 * OWIN):
                until(min(J_OWIN + n // 2 + 3, J_MOE))
                i, kind = (n - 6) // 3, (n - 6) % 3
                if n >= 6 and kind:
                    dve.wait_ge(*((used, J_OWIN + n // 2 + 1) if n % 2 else (q_ps, n // 2 + 1)))
                if n >= 6 and kind == 1:
                    dve.wait_ge(s_gc, i + 1)
                    vv.tensor_tensor(gm[:], gcs[:], ps[n % 4][:, 0:L], ALU.mult).then_inc(s_hx, 1)
                    dve.wait_ge(s_hx, i + 1)
                    own.step(vv.tensor_scalar(gcv[:], gm[:], col("sc", 4 + i), None, ALU.mult))
                    own.step(vv.scalar_tensor_tensor(out=gcv[:, 1:L], in0=gm[:, 0:L - 1], scalar=col("sc", i),
                                                     in1=gcv[:, 1:L], op0=ALU.mult, op1=ALU.add))
                    own.step(vv.scalar_tensor_tensor(out=gcv[:, 0:L - 1], in0=gm[:, 1:L], scalar=col("sc", 8 + i),
                                                     in1=gcv[:, 0:L - 1], op0=ALU.mult, op1=ALU.add))
                if n >= 6 and kind == 2:
                    vv.tensor_tensor(ysc[:, i], ps[n % 4][:, 0:L], gcv[:], ALU.mult).then_inc(s_y, 1)
                    dve.wait_ge(s_y, i + 1)
                if n == 4:
                    pad_v()
                    qk_norm(0)
                if n == 7:
                    qk_turn(0)
                    qk_norm(1)
                if n == 9:
                    qk_norm(2)
                if n == 10:
                    qk_turn(1)
                if n == 12:
                    qk_turn(2)
            dve.wait_ge(m_hi, 9)
            vv.tensor_tensor(hlo[:, 4:8, 0:L], ysc[:], hhi[:, 4:8, 0:L].bitcast(F32), ALU.subtract).then_inc(m_ready, 1)

            dve.wait_ge(c_mask, 16)
            for b in range(2):
                for x in range(8):
                    g = 8 * b + x
                    dve.wait_ge(a_ctx, g + 1)
                    vv.scalar_tensor_tensor(out=sc[:, x, 0:L], in0=ps[x % 4][:, 0:L], scalar=0.125, in1=mask[:, b],
                                            op0=ALU.mult, op1=ALU.add).then_inc(a_loc, 1)
                dve.wait_ge(a_ctx, 8 * b + 8)
                dve.wait_ge(a_loc, 8 * b + 8)
                own.step(vv.tensor_reduce(smax[:], sc[:], AX.X, ALU.max))
                own.step(vv.tensor_tensor(smax[:], smax[:], col("sink", 0, 8), ALU.max))
                vv.tensor_tensor(esink[:], col("sink", 0, 8), smax[:], ALU.subtract)
                vv.tensor_scalar(nmax[:], smax[:], -1.0, None, ALU.mult).then_inc(a_max, 1)
                dve.wait_ge(a_exp, 8 * b + 8)
                own.step(vv.tensor_tensor(sden[:], ssm[:], esink[:], ALU.add))
                own.step(vv.reciprocal(sden[:], sden[:]))
                for x in range(8):
                    vv.tensor_scalar(sc[:, x], sc[:, x], sden[:, x:x + 1], None, ALU.mult).then_inc(a_p, 1)
                dve.wait_ge(m_hi, 10 + b)
                vv.tensor_tensor(hlo[:, 0:4, b * P:(b + 1) * P], ps[6 + b][:].rearrange("p (k c) -> p k c", k=4),
                                 hhi[:, 0:4, b * P:(b + 1) * P].bitcast(F32), ALU.subtract).then_inc(m_ready, 1)

            for n in range(KT):
                residual(n, J_OWOUT + n // 2, 8, omod, L, min(J_OWOUT + n // 2 + 3, J_MOE))
            norm_dve(3, res, sq, rstd, L, omod, 24, full=ht)

            def by_expert(x):
                return x.unsqueeze(2).to_broadcast([P, 2, NEXP, NEXP])

            def by_token(x):
                return x.unsqueeze(2).to_broadcast([P, 2, NEXP])

            dve.wait_ge(c_moe, 64)
            vv.memset(ps[4][:], 0.0).then_inc(e_a, 1)
            vv.memset(ps[5][:], 0.0).then_inc(e_lo, 1)
            dve.wait_ge(r_lg, 1)
            own.step(vv.tensor_tensor(lg[:], ps[6][:, 0:16].rearrange("p (t e) -> p t e", t=2),
                                      col("router_b", 0, 8).unsqueeze(1).to_broadcast([P, 2, NEXP]), ALU.add))
            own.step(vv.tensor_reduce(top[:], lg[:], AX.X, ALU.max))
            vv.tensor_tensor(ex[:], lg[:], by_token(top[:]), ALU.subtract).then_inc(r_sub, 1)
            mine = lg[:].unsqueeze(3).to_broadcast([P, 2, NEXP, NEXP])
            vv.tensor_tensor(gt[:], by_expert(lg[:]), mine, ALU.is_gt)
            own.step(vv.tensor_tensor(eq[:], by_expert(lg[:]), mine, ALU.is_equal))
            own.step(vv.tensor_tensor(eq[:], eq[:], low[:].unsqueeze(1).to_broadcast([P, 2, NEXP, NEXP]), ALU.mult))
            own.step(vv.tensor_tensor(gt[:], gt[:], eq[:], ALU.add))
            own.step(vv.tensor_reduce(rank[:], gt[:], AX.X, ALU.add))
            vv.tensor_scalar(sel[:], rank[:], 2.0, None, ALU.is_lt).then_inc(r_sel, 1)
            dve.wait_ge(r_sel, 1)
            dve.wait_ge(r_exp, 1)
            own.step(vv.tensor_tensor(ex[:], ex[:], sel[:], ALU.mult))
            own.step(vv.tensor_reduce(den[:], ex[:], AX.X, ALU.add))
            own.step(vv.reciprocal(den[:], den[:]))
            own.step(vv.tensor_tensor(ctab[:, :, 0:NEXP], ex[:], by_token(den[:]), ALU.mult))
            dve.wait_ge(r_pos, 1)
            slot = ptab[:, :, 0:NEXP]
            own.step(vv.scalar_tensor_tensor(out=slot, in0=ps[7][:, 0:16].rearrange("p (t e) -> p t e", t=2),
                                             scalar=1.0, in1=sel[:], op0=ALU.add, op1=ALU.mult))
            own.step(vv.tensor_scalar(slot, slot, 1.0, None, ALU.subtract))
            own.step(vv.tensor_scalar(ov[:], ps[7][:, 16:24], float(P), None, ALU.is_gt))
            ovb = ov[:].unsqueeze(1).to_broadcast([P, NEXP, NEXP])
            own.step(vv.tensor_tensor(gt[:, 0], low[:], ovb, ALU.mult))
            own.step(vv.tensor_reduce(ovr[:], gt[:, 0], AX.X, ALU.add))
            for i in range(OVER):
                own.step(vv.scalar_tensor_tensor(out=osel[:], in0=ovr[:], scalar=float(i), in1=ov[:],
                                                 op0=ALU.is_equal, op1=ALU.mult))
                both = osel[:].unsqueeze(1).to_broadcast([P, 2, NEXP])
                own.step(vv.scalar_tensor_tensor(out=obc[:], in0=slot, scalar=float(1 - P), in1=both,
                                                 op0=ALU.add, op1=ALU.mult))
                own.step(vv.tensor_reduce(ptab[:, :, NEXP + i], obc[:], AX.X, ALU.add))
                own.step(vv.tensor_scalar(ptab[:, :, NEXP + i:NEXP + i + 1], ptab[:, :, NEXP + i:NEXP + i + 1],
                                          1.0, None, ALU.subtract))
                own.step(vv.tensor_tensor(obc[:], ctab[:, :, 0:NEXP], both, ALU.mult))
                own.step(vv.tensor_reduce(ctab[:, :, NEXP + i], obc[:], AX.X, ALU.add))
                own.step(vv.tensor_tensor(obc[:, 0], osel[:], enum[:], ALU.mult))
                own.step(vv.tensor_reduce(info[:, 1 + i:2 + i], obc[:, 0], AX.X, ALU.add))
            own.step(vv.memset(ptab[:, :, NTAB - 1:NTAB], -1.0))
            own.step(vv.memset(ctab[:, :, NTAB - 1:NTAB], 0.0))
            own.step(vv.tensor_reduce(info[:, 0:1], ov[:], AX.X, ALU.add))
            vv.tensor_copy(infoi[:], info[:]).then_inc(r_tab, 1)

            def one_hot(turn):
                vv.tensor_copy(cw[:].unsqueeze(2), ctab[:, :, bass.ds(turn, 1)])
                for t in range(2):
                    m = vv.tensor_scalar(hot[:, t], iota[:], ptab[:, t, bass.ds(turn, 1)], None, ALU.is_equal)
                m.then_inc(hot_made, 1)

            dve.wait_ge(c_iota, 16)
            one_hot(0)
            for i in range(4):
                at = slice((i % 2) * 512, (i % 2) * 512 + 512)
                dve.wait_ge(t_hi, i + 1)
                vv.tensor_tensor(hklo[:, i // 2, at], ps[i][:], hkhi[:, i // 2, at].bitcast(F32),
                                 ALU.subtract).then_inc(t_lo, 1)

            def gathered_lo(h, count):
                dve.wait_ge(g_hi, count)
                k = slice(4 * h, 4 * h + 4)
                vv.tensor_tensor(glo[:, k, :], ps[7][:].rearrange("p (k c) -> p k c", k=4), ghi[:, k, :].bitcast(F32),
                                 ALU.subtract).then_inc(misc_free, 1)

            gathered_lo(0, 1)
            gathered_lo(1, 2)
            dve.wait_ge(zeroed, 4)

            def result_lo_part(count):
                for n in range(2):
                    dve.wait_ge(e_yhi, count - 1 + n)
                    m = vv.scalar_tensor_tensor(out=ylo[:, n * CHUNK:(n + 1) * CHUNK], in0=ps[4 + n][:], scalar=wslot[:],
                                                in1=yhi[:, n * CHUNK:(n + 1) * CHUNK].bitcast(F32),
                                                op0=ALU.mult, op1=ALU.subtract)
                m.then_inc(e_y, 1)

            def add_scattered(q, count):
                dve.wait_ge(misc, count)
                vv.tensor_tensor(macc[:, 2 * q:2 * q + 2, :], macc[:, 2 * q:2 * q + 2, :], half(ps[7][:]),
                                 ALU.add).then_inc(misc_free, 1)

            def round_of(r):
                def chunk_lo(c):
                    dve.wait_ge(e_hi, NCH * r + c + 1)
                    vv.tensor_tensor(atlo[:], ps[6][:].rearrange("p (k c) -> p k c", k=4), athi[:].bitcast(F32),
                                     ALU.subtract).then_inc(e_lo, 1)

                for x in range(ROUND_BLOCKS):
                    if x == 3:
                        result_lo_part(2 * r + 2)
                    for c in range(NCH):
                        if x == gate_block(c) + 6:
                            dve.wait_ge(used, r * ROUND_BLOCKS + (J_MOE + gate_block(c) + 4))
                            dve.wait_ge(e_silu, NCH * r + c + 1)
                            vv.tensor_tensor(am[:], sg[:], ps[2 + c % 2][:], ALU.mult).then_inc(e_a, 1)
                        if c < NCH - 1 and x == down_block(c):
                            chunk_lo(c)
                    if x in (6, 12, 18, 24):
                        q = x // 6 - 1
                        add_scattered(q, 7 * r + (3 + q))
                    if x == 31:
                        dve.wait_ge(misc, 7 * r + 7)
                        one_hot(r + 1)
                    if x == 40:
                        gathered_lo(0, 2 * r + 3)
                    split(J_MOE + x, r, ROUND_BLOCKS)
                chunk_lo(NCH - 1)
                gathered_lo(1, 2 * r + 4)

            with dve.Fori(0, NEXP) as r:
                round_of(r)
            crowded = dve.value_load(infoi[0:1, 0:1], min_val=0, max_val=OVER)
            with dve.Fori(NEXP, NEXP + OVER) as r:
                with dve.If(r < crowded + NEXP):
                    round_of(r)
            result_lo_part(crowded * 2 + (2 * NEXP + 2))
            for q in range(4):
                add_scattered(q, crowded * 7 + (7 * NEXP + 3 + q))
            for k in range(KT):
                dve.wait_ge(misc_free, crowded * 7 + (7 * NEXP + 3 + k // 2))
                vv.scalar_tensor_tensor(out=res[:, k, 0:L], in0=macc[:, k], scalar=omod[:, 40 + k, 0:1],
                                        in1=res[:, k, 0:L], op0=ALU.mult, op1=ALU.add).then_inc(y_done, 1)

        @block.gpsimd
        def _(pool):
            gp = nc.gpsimd

            def split(j, turn=0, per=0, n=BLK):
                slot, uses = block_at(j, turn, per)
                if slot != POOL_SLOT:
                    return
                pool.wait_ge(hi_made, turn * per + (j + 1) if per else j + 1)
                gp.tensor_tensor(wlo[:, j % SPLIT, 0:n], raw[:, slot, 0:n], whi[:, j % SPLIT, 0:n].bitcast(F32),
                                 ALU.subtract).then_inc(raw_free[slot], 1)

            done = [0]

            def until(j_end):
                while done[0] < j_end:
                    j = done[0]
                    split(j, n=BLK // 2 if J_FFN <= j < J_OWIN else BLK)
                    done[0] += 1

            def sums(n, sqb, s, width):
                for d in range(1, KT):
                    pool.wait_ge(n_sq, 8 * n + d + 1)
                    if d > 1:
                        pool.wait_ge(n_sum, 7 * n + d - 1)
                    first = sqb[:, 0, 0:width] if d == 1 else s[:, 0:width]
                    gp.tensor_tensor(s[:, 0:width], first, sqb[:, d % 2, 0:width], ALU.add).then_inc(n_sum, 1)

            gp.memset(ones[:], 1.0).then_inc(setup, 1)
            gp.memset(eps[:], EPS).then_inc(setup, 1)
            sums(0, sq0, ssum0, T)
            pool.wait_ge(n_ready, KT)
            pool.wait_ge(f_kcopy, 10)
            pool.dma_start(tabs[:], a["c_four"]).then_inc(c_four, 16)
            pool.dma_start(bdft[:], a["c_bdft"]).then_inc(c_four, 16)
            until(J_WIN + WIN)
            pool.wait_ge(m_ps, 2)
            pool.dma_start(tabs[:], a["c_inv"]).then_inc(c_g, 16)
            for i in range(HT):
                pool.wait_ge(x_prod, i + 1)
                gp.tensor_tensor(tmp[:, 0], tmp[:, 0], tmp[:, 1], ALU.subtract)
                gp.tensor_tensor(tmp[:, 2], tmp[:, 2], tmp[:, 3], ALU.add).then_inc(x_spec, 1)
            until(J_WOUT + 3)
            pool.wait_ge(m_ready, 8)
            pool.dma_start(res[:], a["xt"].rearrange("(k p) t -> p k t", p=P)).then_inc(c_res, 16)
            until(J_FFN)
            sums(1, sq, ssum, T)
            pool.wait_ge(m_ready, 8)
            for i in range(4):
                gp.memset(facc[:, 2 * i:2 * i + 2], 0.0).then_inc(ff_added, 1)
            until(J_FFN + 6)
            with pool.Fori(0, FF_PAIRS - 1) as r:
                for x in range(2, 8):
                    split(J_FFN + 4 + x, r, 6, BLK // 2)
            done[0] = J_FFN + FFN
            until(J_OWIN + 1)
            sums(2, sq, ssum, T)
            pool.wait_ge(res_done, 16)
            gp.memset(kpad[:], 0.0).then_inc(zeroed, 1)
            gp.memset(vpad[:], 0.0).then_inc(zeroed, 1)
            for src, dst in ((a["c_rope"], rope[:]), (a["c_sq"][2], rot[:]), (a["c_sq"][3], bd64[:])):
                pool.dma_start(dst, src).then_inc(c_odd, 16)
            pool.dma_start(mask[:], a["c_mask"]).then_inc(c_mask, 16)
            until(J_MOE)
            sums(3, sq, ssum, L)
            pool.wait_ge(m_ready, 11)
            for src, dst in ((a["c_rw"], rw[:]), (a["c_low"], low[:]), (a["c_enum"], enum[:])):
                pool.dma_start(dst, src).then_inc(c_moe, 16)
            pool.dma_start(tri[:], a["c_tri"]).then_inc(c_moe, 16)
            pool.dma_start(iota[:], a["c_iota"]).then_inc(c_iota, 16)
            gp.memset(hott[:].bitcast(F32), 0.0).then_inc(zeroed, 1)
            gp.memset(wslot[:], 0.0)
            pool.wait_ge(n_ready, 32)
            gp.memset(macc[:], 0.0).then_inc(zeroed, 1)

            def round_of(r):
                for x in range(ROUND_BLOCKS):
                    split(J_MOE + x, r, ROUND_BLOCKS)

            with pool.Fori(0, NEXP) as r:
                round_of(r)
            pool.wait_ge(r_tab, 1)
            crowded = pool.value_load(infoi[0:1, 0:1], min_val=0, max_val=OVER)
            with pool.Fori(NEXP, NEXP + OVER) as r:
                with pool.If(r < crowded + NEXP):
                    round_of(r)


def tables():
    f = np.float64
    t = np.arange(L)
    k = np.arange(L)
    ang = 2 * np.pi * np.outer(t, k) / (2 * L)
    cos, sin = np.cos(ang), -np.sin(ang)
    nyquist = np.cos(np.pi * t)
    sin_n = sin.copy()
    sin_n[:, 0] = nyquist
    cos_n = cos[:, 0:P].copy()
    cos_n[:, 0] = nyquist
    rows = lambda x: np.ascontiguousarray(
        x.reshape(-1, P, x.shape[-1]).transpose(1, 0, 2)).astype(np.float32)
    weight = np.where(k == 0, 1.0, 2.0)[:, None] / (2 * L)
    inv_im = 2 * sin.T / (2 * L)
    inv_im[0] = nyquist / (2 * L)
    ch = np.arange(64)
    blocks = lambda x: np.kron(np.eye(2), x)
    ang64 = 2 * np.pi * np.outer(ch, ch) / 64
    bdft = np.concatenate([blocks(np.cos(ang64)), blocks(np.sin(ang64))], 1) / 8
    angl = 2 * np.pi * np.outer(t, t) / L
    four = np.concatenate([np.cos(angl), -np.sin(angl)], 1) / 16
    f32 = np.float32
    pos = np.linspace(0.0, 1.0, L, dtype=f32)
    bands = 16
    a = f32(2.0 * np.pi / L) * np.arange(L, dtype=f32)[:, None] * np.linspace(1e-4, bands - 1, bands, dtype=f32)[None]
    z = np.concatenate([pos[:, None], np.cos(a), -np.sin(a)], 1)
    deltas = np.abs(np.linspace(np.log(1e-2) / 1.5, np.log(1e-2) / 0.3, HY, dtype=f32))
    decay = np.exp(-pos[:, None] * deltas[None])
    p = np.arange(P) % 64
    place = np.where((p < 32)[:, None], (t // 64)[None], (t % 64)[None]).astype(f32)
    freq = (10000.0 ** (-(p % 16).astype(f32) / 16)).astype(f32)
    turn = place * freq[:, None]
    rope = np.stack([np.cos(turn), np.sin(turn)], 1)
    rot = np.zeros((P, P))
    for i in range(P):
        if i % 32 < 16:
            rot[i + 16, i] = -1.0
        else:
            rot[i - 16, i] = 1.0
    q = np.arange(P)
    mask = np.stack([np.where(np.abs(t[None] - (b * P + q)[:, None]) <= 128, 0.0, -1e30) for b in range(2)], 1)
    tri = np.stack([(q[:, None] < q[None]).astype(f), np.ones((P, P))], 1)
    e = np.arange(NEXP)
    low = np.broadcast_to((e[None, :] < e[:, None]).astype(f), (P, NEXP, NEXP))
    return {
        "c_sq": np.stack([np.eye(P), np.full((P, P), 1.0 / D), rot, blocks(np.full((64, 64), 1.0 / 64))]),
        "c_z": z.T, "c_decay": rows(decay), "c_dft": rows(np.concatenate([cos, sin_n], 1)),
        "c_dft2": rows(np.concatenate([sin[:, 0:P], cos_n], 1)),
        "c_four": rows(four), "c_bdft": bdft,
        "c_inv": rows(np.concatenate([cos.T * weight, inv_im])).reshape(P, 2, 512),
        "c_rope": rope, "c_mask": mask, "c_low": low, "c_enum": np.broadcast_to(e, (P, NEXP)),
        "c_tri": tri, "c_iota": np.broadcast_to(q, (P, P)),
    }


def column_tiles(w):
    n = w.shape[1] // 256
    return w.reshape(KT, P, n, 256).transpose(2, 1, 0, 3).reshape(n, P, BLK)


def by_tiles(w, order, axis):
    tiles = np.split(w, w.shape[axis] // P, axis)
    return np.concatenate([tiles[i] for i in order], axis)


def vectors(x):
    v = np.zeros((P, NVEC), np.float32)

    def put(name, a):
        v[:a.shape[0], VEC[name]] = a

    def cols(a):
        return a.reshape(-1, P).T

    for n in ("e_ada_b", "o_ada_b", "e_norm1", "e_norm2", "o_norm1", "o_norm2"):
        put(n, cols(x[n]))
    put("short", cols(x["e_hy_short"]))
    put("skip", cols(x["e_hy_skip"]))
    put("b1", x["e_hy_b1"].T)
    put("freq", x["e_hy_freq"].T)
    put("b2", x["e_hy_b2"].T)
    put("q_norm", np.concatenate([x["o_q_norm"].T] * 2))
    put("k_norm", np.concatenate([x["o_k_norm"].T] * 2))
    put("sc", cols(x["o_sc_conv"]))
    put("sink", np.broadcast_to(x["o_sink"][:, HEADS], (P, NEXP)))
    put("router_b", np.broadcast_to(x["o_router_b"], (P, NEXP)))
    put("cond", np.stack([cols(x["c"]), cols(x["c_ctx"])], 2).reshape(P, 16))
    return v


def layout(x):
    a = {k: np.ascontiguousarray(v, dtype=np.float32) for k, v in tables().items()}
    a["c_vec"] = vectors(x)
    a["xt"] = np.concatenate([x["x"][0].T, x["ctx"][0].T], 1)
    a["c_w12"] = np.zeros((64, P), np.float32)
    a["c_w12"][0:33, 0:64] = x["e_hy_w1"][0]
    a["c_w12"][:, 64:] = x["e_hy_w2"][0]
    a["c_w3"] = x["e_hy_w3"][0]
    a["w_ada"] = np.concatenate([column_tiles(x["e_ada_w"][0]), column_tiles(x["o_ada_w"][0])])
    a["w_in"] = column_tiles(by_tiles(x["e_w_in"][0], WIN_TILES, 1))
    a["w_out"] = column_tiles(x["e_w_out"][0])
    gate, up = (x[n][0].reshape(2, 4, P, FF_PAIRS, 256).transpose(3, 0, 2, 1, 4).reshape(FF_PAIRS, 2, P, 1024)
                for n in ("e_ffn_wg", "e_ffn_wu"))
    down = x["e_ffn_wd"][0].reshape(FF_PAIRS, 2, P, D)
    order = [gate[0], up[0]]
    for i in range(1, FF_PAIRS):
        order += [gate[i], down[i - 1], up[i]]
    a["w_ffn"] = np.concatenate(order + [down[FF_PAIRS - 1]])
    w = x["o_w_in"][0]
    heads = np.split(w[:, 0:512], 8, 1)
    w = np.concatenate([heads[h] for h in HEADS] + [w[:, 512:]], 1)
    a["w_oin"] = column_tiles(by_tiles(w, OWIN_TILES, 1))
    w = x["o_w_out"][0]
    heads = np.split(w[0:512], 8, 0)
    a["w_oout"] = column_tiles(np.concatenate([heads[h] for h in HEADS] + [w[512:]], 0))
    gate, up = (x[n][0].reshape(NEXP, 2, 4, P, NCH, CHUNK).transpose(4, 0, 1, 3, 2, 5)
                for n in ("o_moe_wg", "o_moe_wu"))
    down = x["o_moe_wd"][0].reshape(NEXP, NCH, 2, 2, P, D).transpose(1, 0, 2, 4, 3, 5)
    moe = np.empty((NEXP, ROUND_BLOCKS, P, BLK), np.float32)
    for c in range(NCH):
        g = gate_block(c)
        moe[:, g:g + 2] = gate[c].reshape(NEXP, 2, P, BLK)
        moe[:, g + 2:g + 4] = up[c].reshape(NEXP, 2, P, BLK)
        d = down_block(c)
        moe[:, d:d + 2] = down[c].reshape(NEXP, 2, P, BLK)
    a["w_moe"] = moe.reshape(NEXP * ROUND_BLOCKS, P, BLK)
    a["c_rw"] = x["o_router_w"][0].reshape(KT, P, NEXP).transpose(1, 0, 2)
    return a


def kernel(**inputs):
    import concourse.bacc as bacc
    from concourse.bass_utils import run_bass_kernel_spmd

    arrays = {n: np.ascontiguousarray(v) for n, v in layout({n: np.asarray(v) for n, v in inputs.items()}).items()}
    nc = bacc.Bacc("TRN2", target_bir_lowering=False, num_devices=1)
    a = {n: nc.dram_tensor(n, v.shape, F32, kind="ExternalInput").ap() for n, v in arrays.items()}
    out = nc.dram_tensor("out", (D, L), F32, kind="ExternalOutput").ap()
    build(nc, a, out)
    r = run_bass_kernel_spmd(nc, [arrays], core_ids=[0])
    return np.ascontiguousarray(r.results[0]["out"].T)[None]
```

```python
from contextlib import ExitStack

import numpy as np
import concourse.bass as bass
from concourse import mybir

F32 = mybir.dt.float32
F32R = mybir.dt.float32r
I32 = mybir.dt.int32
ACT = mybir.ActivationFunctionType
ALU = mybir.AluOpType
AX = mybir.AxisListType

P = 128
D = 1024
KT = D // P
L = 256
T = 2 * L
EPS = 1e-6
HY = 768
HT = HY // P
HALF = HY // 2
FF_PAIRS = 2816 // 256
NEXP = 8
CHUNK = 512
NCH = 3584 // CHUNK
ROUND_BLOCKS = 6 * NCH
OVER = 3
NTAB = NEXP + OVER + 1

RAW = 6
SPLIT = 3
BLK = 2048
POOL_SLOT = 5

ADA, WIN, WOUT = 24, 10, 4
EARLY = 4
OWIN, OWOUT = 9, 4
FFN_BODY = ["gate", "mod0", "down", "mod1", "up", "mod2"]
FFN_KINDS = ["gate", "mod0", "mod1", "up", "mod2"] + (FF_PAIRS - 1) * FFN_BODY + ["down", "mod0", "mod1", "mod2"]
MOD_TILES = {"mod0": range(0, 3), "mod1": range(3, 6), "mod2": range(6, 8)}
J_WOUT = ADA + WIN
J_FFN = J_WOUT + WOUT
J_BODY = J_FFN + 5
J_TAIL = J_BODY + 6 * (FF_PAIRS - 1)
J_OWIN = J_FFN + len(FFN_KINDS)
J_OWOUT = J_OWIN + OWIN
J_MOE = J_OWOUT + OWOUT

WIN_TILES = [18, 19] + [s + 2 * i + a for i in range(3) for s in (6, 12, 0) for a in range(2)]
OWIN_TILES = [4, 5, 0, 1, 2, 3] + [6 + s + i for i in range(4) for s in (4, 8, 0)]

VEC = {}


def _columns():
    at = 0
    for name, n in (("e_ada_b", 48), ("o_ada_b", 48), ("e_norm1", 8), ("e_norm2", 8), ("o_norm1", 8),
                    ("o_norm2", 8), ("short", 54), ("skip", 6), ("b1", 1), ("freq", 1), ("b2", 1),
                    ("q_norm", 1), ("k_norm", 1), ("sc", 12), ("sink", 8), ("router_b", 8), ("cond", 16)):
        VEC[name] = slice(at, at + n)
        at += n
    return at


NVEC = _columns()


HEADS = [h for i in range(4) for h in (i, i + 4)]

ROUND = 1.5 * 2 ** 23
TURN = (6.28125, float(2 * np.pi - 6.28125))


def gate_block(c):
    return 6 * c - 2 if c else 0


def down_block(c):
    return 6 * c + 8 if c < NCH - 1 else ROUND_BLOCKS - 2


class Steps:

    def __init__(self, engine, sem):
        self.engine, self.sem, self.n = engine, sem, 0

    def step(self, instruction):
        instruction.then_inc(self.sem, 1)
        self.n += 1
        self.engine.wait_ge(self.sem, self.n)


def win_at(b):
    return 2 * EARLY + 3 * b if b < 8 else 2 * EARLY + 24 + (b - 8)


def ada_at(c):
    return 2 * c if c < EARLY else win_at(c - EARLY) + 1


def width_of(j):
    kind = FFN_KINDS[j - J_FFN] if J_FFN <= j < J_OWIN else ""
    return len(MOD_TILES[kind]) * CHUNK if kind in MOD_TILES else BLK


def block_at(j, turn=0, per=0):
    uses = j // RAW + 1
    return j % RAW, (uses + turn * (per // RAW) if per else uses)


def build(nc, a, out):
    ctx = ExitStack()
    with ctx:
        def sb(name, shape, dt=F32, where=ctx):
            return where.enter_context(nc.sbuf_tensor(name, shape, dt))

        def sem(name):
            return ctx.enter_context(nc.semaphore(name))

        raw = sb("raw", [P, RAW, BLK])
        whi = sb("whi", [P, SPLIT, BLK], F32R)
        wlo = sb("wlo", [P, SPLIT, BLK], F32R)
        hhi = sb("hhi", [P, KT, T], F32R)
        hlo = sb("hlo", [P, KT, T], F32R)
        vec = sb("vec", [P, NVEC])
        ident = sb("ident", [P, P])
        mean = sb("mean", [P, P])
        emod = sb("emod", [P, 48, 2])
        omod = sb("omod", [P, 48, 2])
        gain = sb("gain", [P, 4, KT, 2])
        scond = sb("scond", [P, KT, 2])
        sc4 = sb("sc4", [P, KT, 4], F32R)
        rows = sb("rows", [4, 2, CHUNK])
        pick = sb("pick", [4, 2])
        eps = sb("eps", [P, 1])
        ones = sb("ones", [P, 1])
        il1 = sb("il1", [P, HT])

        even = ExitStack()
        kf = sb("kf", [P, 5, HY], where=even)
        dft = sb("dft", [P, 2, 512], where=even)
        start = ExitStack()
        xin = sb("xin", [P, KT, T], where=start)
        dft2 = sb("dft2", [P, 2, 256], where=start)
        decay = sb("decay", [P, 2, HY], where=start)
        hf = sb("hf", [P, 2, HALF], where=start)
        hb = sb("hb", [P, 2, HALF], where=start)
        hs = sb("hs", [P, 2, HALF], where=start)
        hd = sb("hd", [P, 2, HALF], where=start)
        w3 = sb("w3", [64, 2 * HY], where=start)
        w12 = sb("w12", [64, 128], where=start)
        zt = sb("zt", [33, L], where=start)
        sarg = sb("sarg", [64, L], where=start)
        sred = sb("sred", [64, L], where=start)
        sq0 = sb("sq0", [P, 2, T], where=start)
        ssum0 = sb("ssum0", [P, T], where=start)
        rstd0 = sb("rstd0", [P, T], where=start)
        start.close()
        x0c = sb("x0c", [P, HT, T], where=even)
        u = sb("u", [P, HT, T], where=even)
        utok = sb("utok", [P, 4, HY], where=even)
        tabs = sb("tabs", [P, 2, 512], where=even)
        fnt = sb("fnt", [P, 2, T], where=even)
        bdft = sb("bdft", [P, 256], where=even)
        tmp = sb("tmp", [P, 4, T], where=even)
        even.close()

        res = sb("res", [P, KT, T])
        norm = ExitStack()
        sq = sb("sq", [P, 2, T], where=norm)
        ssum = sb("ssum", [P, T], where=norm)
        rstd = sb("rstd", [P, T], where=norm)
        ffn = ExitStack()
        facc = sb("facc", [P, KT, T], where=ffn)
        ahi = sb("ahi", [P, 2, T], F32R, where=ffn)
        alo = sb("alo", [P, 2, T], F32R, where=ffn)
        sil = sb("sil", [P, 2, T], where=ffn)
        ffn.close()
        odd = ExitStack()
        qt = sb("qt", [P, 4, L], where=odd)
        kpad = sb("kpad", [P, 2, T], where=odd)
        vpad = sb("vpad", [P, 4, 2, P], where=odd)
        ysc = sb("ysc", [P, 4, L], where=odd)
        mask = sb("mask", [P, 2, L], where=odd)
        smax = sb("smax", [P, 8], where=odd)
        nmax = sb("nmax", [P, 8], where=odd)
        ssm = sb("ssm", [P, 8], where=odd)
        esink = sb("esink", [P, 8], where=odd)
        sden = sb("sden", [P, 8], where=odd)
        mix = ExitStack()
        qraw = sb("qraw", [P, 3, T], where=mix)
        qsq = sb("qsq", [P, 3, T], where=mix)
        qn = sb("qn", [P, 3, T], where=mix)
        rr = sb("rr", [P, T], where=mix)
        ra = sb("ra", [P, L], where=mix)
        rb = sb("rb", [P, L], where=mix)
        vt = sb("vt", [P, T], where=mix)
        gcs = sb("gcs", [P, L], where=mix)
        gm = sb("gm", [P, L], where=mix)
        gcv = sb("gcv", [P, L], where=mix)
        rope = sb("rope", [P, 2, L], where=mix)
        rot = sb("rot", [P, P], where=mix)
        bd64 = sb("bd64", [P, P], where=mix)
        mix.close()
        sc = sb("sc", [P, 8, T], where=odd)
        pt = sb("pt", [P, 2, 4, P], where=odd)
        odd.close()
        norm.close()
        macc = sb("macc", [P, KT, L])
        route = ExitStack()
        ht = sb("ht", [P, KT, L], where=route)
        route.close()
        yhi = sb("yhi", [P, D], F32R)
        ylo = sb("ylo", [P, D], F32R)
        hkhi = sb("hkhi", [P, 2, D], F32R)
        hklo = sb("hklo", [P, 2, D], F32R)
        rw = sb("rw", [P, KT, NEXP])
        lg = sb("lg", [P, 2, NEXP])
        gt = sb("gt", [P, 2, NEXP, NEXP])
        eq = sb("eq", [P, 2, NEXP, NEXP])
        low = sb("low", [P, NEXP, NEXP])
        rank = sb("rank", [P, 2, NEXP])
        sel = sb("sel", [P, 2, NEXP])
        top = sb("top", [P, 2])
        ex = sb("ex", [P, 2, NEXP])
        den = sb("den", [P, 2])
        ov = sb("ov", [P, NEXP])
        ovr = sb("ovr", [P, NEXP])
        osel = sb("osel", [P, NEXP])
        obc = sb("obc", [P, 2, NEXP])
        enum = sb("enum", [P, NEXP])
        info = sb("info", [P, 4])
        infoi = sb("infoi", [P, 4], I32)
        tri = sb("tri", [P, 2, P])
        iota = sb("iota", [P, P])
        ptab = sb("ptab", [P, 2, NTAB])
        ctab = sb("ctab", [P, 2, NTAB])
        cw = sb("cw", [P, 2])
        hot = sb("hot", [P, 2, P], F32R)
        hott = sb("hott", [P, L], F32R)
        wslot = sb("wslot", [P, 1])
        ghi = sb("ghi", [P, KT, P], F32R)
        glo = sb("glo", [P, KT, P], F32R)
        sg = sb("sg", [P, CHUNK])
        am = sb("am", [P, CHUNK])
        athi = sb("athi", [P, 4, P], F32R)
        atlo = sb("atlo", [P, 4, P], F32R)
        ps = [ctx.enter_context(nc.psum_tensor(f"ps{i}", [P, 512], F32)) for i in range(8)]

        raw_loaded = [sem(f"raw_loaded{i}") for i in range(RAW)]
        raw_free = [sem(f"raw_free{i}") for i in range(RAW)]
        hi_made = sem("hi_made")
        used = sem("used")
        c_vec = sem("c_vec")
        c_net = sem("c_net")
        c_even = sem("c_even")
        c_x = sem("c_x")
        c_filt = sem("c_filt")
        c_four = sem("c_four")
        c_g = sem("c_g")
        c_res = sem("c_res")
        c_odd = sem("c_odd")
        c_mask = sem("c_mask")
        c_moe = sem("c_moe")
        c_iota = sem("c_iota")
        setup = sem("setup")
        zeroed = sem("zeroed")
        silu_c = sem("silu_c")
        f_ps = sem("f_ps")
        f_arg = sem("f_arg")
        f_sin = sem("f_sin")
        f_taps = sem("f_taps")
        f_abs = sem("f_abs")
        f_k = sem("f_k")
        f_kcopy = sem("f_kcopy")
        f_l1 = sem("f_l1")
        n_sq = sem("n_sq")
        n_sum = sem("n_sum")
        n_mean = sem("n_mean")
        n_root = sem("n_root")
        n_h = sem("n_h")
        n_hi = sem("n_hi")
        n_ready = sem("n_ready")
        w_ps = sem("w_ps")
        w_mid = sem("w_mid")
        w_free = sem("w_free")
        u_made = sem("u_made")
        ut_ps = sem("ut_ps")
        ut_copy = sem("ut_copy")
        fn_ab = sem("fn_ab")
        fn_abc = sem("fn_abc")
        m_ps = sem("m_ps")
        m_z = sem("m_z")
        m_hi = sem("m_hi")
        m_ready = sem("m_ready")
        x_ps = sem("x_ps")
        x_prod = sem("x_prod")
        x_spec = sem("x_spec")
        skips = sem("skips")
        o_ps = sem("o_ps")
        res_done = sem("res_done")
        act_s = sem("act_s")
        rows_made = sem("rows_made")
        cols_made = sem("cols_made")
        emod_made = sem("emod_made")
        oa_read = sem("oa_read")
        ff_silu = sem("ff_silu")
        ff_a = sem("ff_a")
        ff_hi = sem("ff_hi")
        ff_lo = sem("ff_lo")
        ff_d = sem("ff_d")
        ff_added = sem("ff_added")
        q_ps = sem("q_ps")
        q_sq = sem("q_sq")
        q_raw = sem("q_raw")
        q_ms = sem("q_ms")
        q_root = sem("q_root")
        q_n = sem("q_n")
        q_rot = sem("q_rot")
        q_done = sem("q_done")
        v_copy = sem("v_copy")
        v_ps = sem("v_ps")
        v_done = sem("v_done")
        s_gc = sem("s_gc")
        s_hx = sem("s_hx")
        s_y = sem("s_y")
        a_s = sem("a_s")
        a_ctx = sem("a_ctx")
        a_loc = sem("a_loc")
        a_max = sem("a_max")
        a_sink = sem("a_sink")
        a_exp = sem("a_exp")
        a_p = sem("a_p")
        a_t = sem("a_t")
        a_tc = sem("a_tc")
        a_o = sem("a_o")
        r_lg = sem("r_lg")
        r_sub = sem("r_sub")
        r_exp = sem("r_exp")
        r_sel = sem("r_sel")
        r_pos = sem("r_pos")
        r_tab = sem("r_tab")
        t_ps = sem("t_ps")
        t_hi = sem("t_hi")
        t_lo = sem("t_lo")
        misc = sem("misc")
        misc_free = sem("misc_free")
        hot_made = sem("hot_made")
        g_hi = sem("g_hi")
        e_silu = sem("e_silu")
        e_a = sem("e_a")
        e_t = sem("e_t")
        e_hi = sem("e_hi")
        e_lo = sem("e_lo")
        e_yhi = sem("e_yhi")
        e_y = sem("e_y")
        y_done = sem("y_done")
        stored = sem("stored")
        dve_s = sem("dve_s")

        block = ctx.enter_context(nc.Block())

        def oin_free(n):
            if n < 6:
                return (v_copy, 1) if n == 1 else (q_raw, max(n, 1))
            return (s_gc, s_hx, s_y)[(n - 6) % 3], (n - 6) // 3 + 1

        def col(name, i=0, n=1):
            at = VEC[name].start + i
            return vec[:, at:at + n]

        def half(ap):
            return ap.rearrange("p (s t) -> p s t", s=2)

        def split_block(j):
            return whi[:, j % SPLIT, :], wlo[:, j % SPLIT, :]

        @block.sync
        def _(sp):
            def load(slot, uses, src, n=BLK):
                if not (isinstance(uses, int) and uses == 1):
                    sp.wait_ge(raw_free[slot], uses - 1)
                sp.dma_start(raw[:, slot, 0:n], src).then_inc(raw_loaded[slot], 16)

            def at(src, i):
                return src[bass.ds(i, 1)].rearrange("a p n -> p (a n)")

            for j in range(2 * EARLY):
                load(*block_at(j), a["w_ada"][j])
            for b in range(WIN):
                load(*block_at(win_at(b)), a["w_in"][b])
                if EARLY + b < ADA // 2:
                    for h in range(2):
                        load(*block_at(ada_at(EARLY + b) + h), a["w_ada"][2 * (EARLY + b) + h])
            for j in range(WOUT):
                load(*block_at(J_WOUT + j), a["w_out"][j])

            def load_ffn(j, src, turn=0, per=0):
                n = width_of(j)
                load(*block_at(j, turn, per), src[:, 0:n], n)

            for j in range(J_FFN, J_BODY):
                load_ffn(j, a["w_ffn"][j - J_FFN])
            with sp.Fori(0, FF_PAIRS - 1) as r:
                for x in range(6):
                    load_ffn(J_BODY + x, at(a["w_ffn"], r * 6 + (J_BODY - J_FFN + x)), r, 6)
            for j in range(J_TAIL, J_OWIN):
                load_ffn(j, a["w_ffn"][j - J_FFN])
            for j in range(OWIN):
                load(*block_at(J_OWIN + j), a["w_oin"][j])
            for j in range(OWOUT):
                load(*block_at(J_OWOUT + j), a["w_oout"][j])

            def round_of(r, expert):
                for i in range(ROUND_BLOCKS):
                    load(*block_at(J_MOE + i, r, ROUND_BLOCKS), at(a["w_moe"], expert * ROUND_BLOCKS + i))

            with sp.Fori(0, NEXP) as r:
                round_of(r, r)
            sp.wait_ge(r_tab, 1)
            crowded = sp.value_load(infoi[0:1, 0:1], min_val=0, max_val=OVER)
            with sp.Fori(NEXP, NEXP + OVER) as r:
                with sp.If(r < crowded + NEXP):
                    round_of(r, sp.value_load(infoi[0:1, bass.ds(r - (NEXP - 1), 1)], min_val=0, max_val=NEXP - 1))
            sp.wait_ge(y_done, KT)
            sp.dma_start(out.rearrange("(k p) t -> p k t", p=P), res[:, :, 0:L]).then_inc(stored, 16)
            sp.wait_ge(stored, 16)

        @block.tensor
        def _(pe):
            mm = nc.tensor.matmul

            def wait_block(j, turn=0, per=0):
                slot, uses = block_at(j, turn, per)
                pe.wait_ge(raw_free[slot], uses)

            def three(dst, w, x, start, stop):
                mm(dst, w[0], x[0], start=start, stop=False)
                mm(dst, w[0], x[1], start=False, stop=False)
                return mm(dst, w[1], x[0], start=False, stop=stop)

            def hidden(k, n):
                return hhi[:, k, 0:n], hlo[:, k, 0:n]

            def weights(j, at):
                return whi[:, j % SPLIT, at:at + P], wlo[:, j % SPLIT, at:at + P]

            def modulation(j, tiles, bank, turn=0, per=0):
                wait_block(j, turn, per)
                for i, k in enumerate(tiles):
                    at = slice(i * CHUNK, (i + 1) * CHUNK)
                    mm(ps[bank][0:4, :], sc4[:, k, :], whi[:, j % SPLIT, at], start=(k == 0), stop=False)
                    m = mm(ps[bank][0:4, :], sc4[:, k, :], wlo[:, j % SPLIT, at], start=False, stop=(k == KT - 1))
                m.then_inc(used, 1)

            def even_modulation(c):
                if c:
                    pe.wait_ge(rows_made, c)
                for h in range(2):
                    modulation(ada_at(c) + h, range(4 * h, 4 * h + 4), 6)

            def to_columns(bank, at, buf, made):
                pe.wait_ge(rows_made, made)
                for q in range(4):
                    m = mm(ps[bank][:, at + 2 * q:at + 2 * q + 2], rows[:, buf, q * P:(q + 1) * P], pick[:],
                           start=True, stop=True)
                m.then_inc(cols_made, 1)

            def even_columns(c):
                if c == 0:
                    pe.wait_ge(setup, 3)
                if c == EARLY:
                    pe.wait_ge(emod_made, 1)
                to_columns(7, 8 * c, c % 2, c + 1)

            def filter_taps(h):
                pe.wait_ge(f_sin, 2)
                if h:
                    pe.wait_ge(f_taps, 1)
                for t in range(2):
                    for side in range(2):
                        m = mm(ps[2 * side + t][:, 0:HALF], sred[:, t * P:(t + 1) * P],
                               w3[:, side * HY + h * HALF:side * HY + (h + 1) * HALF], start=True, stop=True)
                m.then_inc(f_ps, 1)

            def filter_spectrum(h):
                pe.wait_ge(f_taps, h + 1)
                tiles = ((dft, 0, hs), (dft2, P, hs), (dft, P, hs), (dft2, 0, hd), (dft, 3 * P, hd))
                for m_, (table, at, src) in enumerate(tiles):
                    n = 5 * h + m_
                    if n >= 2:
                        pe.wait_ge(f_kcopy, n - 1)
                    for k in range(2):
                        m = mm(ps[4 + n % 2][:, 0:HALF], table[:, k, at:at + P], src[:, k, :],
                               start=(k == 0), stop=(k == 1))
                    m.then_inc(f_k, 1)
                pe.wait_ge(f_abs, h + 1)
                for c in range(3):
                    for i, src in enumerate((hf, hf, hb, hb)):
                        at = 4 * ADA + 3 * h + c
                        m = mm(ps[7][:, at:at + 1], src[:, i % 2, c * P:(c + 1) * P], ones[:],
                               start=(i == 0), stop=(i == 3))
                m.then_inc(f_l1, 1)

            pe.wait_ge(c_net, 16 * 2)
            mm(ps[0][0:64, 0:L], w12[0:33, 0:64], zt[:], start=True, stop=True).then_inc(f_ps, 1)
            pe.wait_ge(silu_c, 1)
            even_modulation(0)
            pe.wait_ge(f_sin, 1)
            mm(ps[1][0:64, 0:L], w12[0:64, 64:128], sred[:], start=True, stop=True).then_inc(f_ps, 1)
            even_modulation(1)
            even_columns(0)
            pe.wait_ge(c_filt, 16 * 4)
            filter_taps(0)
            even_modulation(2)
            even_columns(1)
            filter_spectrum(0)
            filter_taps(1)
            even_modulation(3)
            even_columns(2)
            filter_spectrum(1)

            def norm_mean(n, s, width):
                pe.wait_ge(n_sum, 7 * n + 7)
                if n == 0:
                    pe.wait_ge(f_kcopy, 10)
                mm(ps[6 if n else 5][:, 0:width], mean[:], s[:, 0:width], start=True, stop=True).then_inc(n_mean, 1)

            norm_mean(0, ssum0, T)
            even_columns(3)

            def transpose_u(c):
                pe.wait_ge(u_made, c + 1)
                if c >= 2:
                    pe.wait_ge(ut_copy, c - 1)
                for s in range(4):
                    m = nc.tensor.transpose(ps[4 + c % 2][:, s * P:(s + 1) * P], u[:, c, s * P:(s + 1) * P], ident[:])
                m.then_inc(ut_ps, 1)

            for n in range(2 * WIN):
                j, q = n // 2, n % 2
                if q == 0:
                    wait_block(win_at(j))
                if n >= 4:
                    pe.wait_ge(w_free, n - 3)
                for k in range(KT):
                    if n == 0:
                        pe.wait_ge(n_ready, k + 1)
                    m = three(ps[n % 4][:], weights(win_at(j), k * 256 + q * P), hidden(k, T), k == 0, k == KT - 1)
                m.then_inc(used if q else w_ps, 1)
                if q and EARLY + j < ADA // 2:
                    even_modulation(EARLY + j)
                if q and 1 <= j <= ADA // 2 - EARLY:
                    even_columns(EARLY + j - 1)
                if n >= 9 and (n - 9) % 6 == 0:
                    transpose_u((n - 9) // 3)
                    transpose_u((n - 9) // 3 + 1)
            transpose_u(4)
            transpose_u(5)

            pe.wait_ge(c_four, 32)
            pe.wait_ge(w_free, 2 * WIN)
            for q in range(2):
                for s in range(4):
                    m = mm(ps[2 * q + s // 2][:, (s % 2) * 256:(s % 2) * 256 + 256], fnt[:, q, s * P:(s + 1) * P],
                           bdft[:], start=True, stop=True)
                m.then_inc(fn_ab, 1)
            pe.wait_ge(ut_copy, HT)
            for q in range(2):
                pe.wait_ge(fn_abc, q + 1)
                ab = tmp[:, 2 * q:2 * q + 2, :].rearrange("p a (b n) -> p (a b) n", b=2)
                for s in range(2):
                    for i in range(4):
                        k, part = i // 2, i % 2
                        m = mm(ps[4 + q][:, s * L:(s + 1) * L], ab[:, 2 * s + k, part * P:(part + 1) * P],
                               tabs[:, k, part * L:(part + 1) * L], start=(i == 0), stop=(i == 3))
                m.then_inc(m_ps, 1)

            tok = utok[:].rearrange("p (s k) c -> p s k c", s=2)
            inverse = tabs[:].rearrange("p a (b n) -> p (a b) n", b=2)

            def forward(i):
                if i >= 2:
                    pe.wait_ge(x_prod, i - 1)
                for part in range(4):
                    for k in range(2):
                        m = mm(half(ps[2 * (i % 2) + part // 2][:, (part % 2) * 256:(part % 2) * 256 + 256]),
                               dft[:, k, part * P:(part + 1) * P], tok[:, :, k, i * P:(i + 1) * P],
                               start=(k == 0), stop=(k == 1))
                m.then_inc(x_ps, 1)

            def backward(i):
                pe.wait_ge(x_spec, i + 1)
                if i == 0:
                    pe.wait_ge(c_g, 16)
                if i >= 2:
                    pe.wait_ge(m_z, i - 1)
                else:
                    pe.wait_ge(m_ready, i + 1)
                for s in range(2):
                    for part in range(4):
                        spec = tmp[:, 2 * (part // 2), :].rearrange("p (m s c) -> p m s c", m=2, s=2)
                        m = mm(ps[4 + i % 2][:, s * L:(s + 1) * L], spec[:, part % 2, s, :], inverse[:, part, :],
                               start=(part == 0), stop=(part == 3))
                m.then_inc(m_ps, 1)

            forward(0)
            for i in range(HT):
                if i + 1 < HT:
                    forward(i + 1)
                backward(i)

            def project_out(j0, order, width, ready):
                for n in range(KT):
                    j, q = n // 2, n % 2
                    if q == 0:
                        wait_block(j0 + j)
                    if n >= 4:
                        pe.wait_ge(res_done, ready[0] + n - 3)
                    for i, k in enumerate(order):
                        if n == 0:
                            pe.wait_ge(m_ready, ready[1][i])
                        m = three(ps[n % 4][:, 0:width], weights(j0 + j, k * 256 + q * P), hidden(k, width),
                                  i == 0, i == KT - 1)
                    m.then_inc(used if q else o_ps, 1)

            project_out(J_WOUT, (6, 7, 0, 1, 2, 3, 4, 5), T, (0, range(1, 9)))
            norm_mean(1, ssum, T)

            def ffn_in(j, bank, free, turn, pair, per):
                wait_block(j, turn, per)
                if free is not None:
                    pe.wait_ge(free, 2 * pair)
                for q in range(2):
                    for k in range(KT):
                        if free is None and bank == 0 and q == 0:
                            pe.wait_ge(n_ready, 8 + k + 1)
                        m = three(ps[bank + q][:], weights(j, k * 256 + q * P), hidden(k, T), k == 0, k == KT - 1)
                m.then_inc(used, 1)

            def ffn_down(j, turn, pair, per):
                wait_block(j, turn, per)
                pe.wait_ge(ff_lo, 2 * pair + 2)
                for d in range(KT):
                    if d == 2:
                        pe.wait_ge(oa_read, pair + 1)
                    pe.wait_ge(ff_added, 8 * pair + (d + 2 if d >= 3 else 4))
                    three(ps[4 + d % 3][:], weights(j, d * P), (ahi[:, 0], alo[:, 0]), True, False)
                    m = three(ps[4 + d % 3][:], weights(j, D + d * P), (ahi[:, 1], alo[:, 1]), False, True)
                    m.then_inc(used if d == KT - 1 else ff_d, 1)

            def odd_columns(pair):
                pe.wait_ge(ff_added, 8 * pair + 4)
                to_columns(6, 0, 0, pair + (ADA // 2 + 1))

            def odd_modulation(j, kind, turn=0, per=0):
                modulation(j, MOD_TILES[kind], 7, turn, per)

            ffn_in(J_FFN, 0, None, 0, 0, 0)
            pe.wait_ge(emod_made, 2)
            odd_modulation(J_FFN + 1, "mod0")
            odd_modulation(J_FFN + 2, "mod1")
            ffn_in(J_FFN + 3, 2, None, 0, 0, 0)
            odd_modulation(J_FFN + 4, "mod2")
            with pe.Fori(0, FF_PAIRS - 1) as r:
                ffn_in(J_BODY, 0, ff_silu, r, r + 1, 6)
                odd_columns(r)
                odd_modulation(J_BODY + 1, "mod0", r, 6)
                ffn_down(J_BODY + 2, r, r, 6)
                odd_modulation(J_BODY + 3, "mod1", r, 6)
                ffn_in(J_BODY + 4, 2, ff_a, r, r + 1, 6)
                odd_modulation(J_BODY + 5, "mod2", r, 6)
            odd_columns(FF_PAIRS - 1)
            ffn_down(J_TAIL, 0, FF_PAIRS - 1, 0)
            odd_modulation(J_TAIL + 1, "mod0")
            odd_modulation(J_TAIL + 2, "mod1")
            odd_modulation(J_TAIL + 3, "mod2")
            odd_columns(FF_PAIRS)
            pe.wait_ge(oa_read, FF_PAIRS + 1)
            norm_mean(2, ssum, T)

            def qk_square(y):
                pe.wait_ge(q_sq, 1 if y == 0 else 1 + 2 * y)
                if y == 0:
                    pe.wait_ge(c_odd, 48)
                if y == 1:
                    pe.wait_ge(v_done, 1)
                if y == 2:
                    pe.wait_ge(q_root, 1)
                mm(ps[4 + y % 2][:], bd64[:], qsq[:, y], start=True, stop=True).then_inc(q_ms, 1)

            def qk_rotate(y):
                pe.wait_ge(q_n, y + 1)
                if y == 2:
                    pe.wait_ge(q_done, 1)
                mm(ps[6 + y % 2][:], rot[:], qn[:, y], start=True, stop=True).then_inc(q_rot, 1)

            def transpose_v():
                pe.wait_ge(v_copy, 1)
                for s in range(4):
                    m = nc.tensor.transpose(ps[5][:, s * P:(s + 1) * P], vt[:, s * P:(s + 1) * P], ident[:])
                m.then_inc(v_ps, 1)

            for n in range(2 * OWIN):
                j, q = n // 2, n % 2
                if q == 0:
                    wait_block(J_OWIN + j)
                if n >= 4:
                    pe.wait_ge(*oin_free(n - 4))
                width = T if n < 2 else L
                for k in range(KT):
                    if n == 0:
                        pe.wait_ge(n_ready, 16 + k + 1)
                    m = three(ps[n % 4][:, 0:width], weights(J_OWIN + j, k * 256 + q * P), hidden(k, width),
                              k == 0, k == KT - 1)
                m.then_inc(used if q else q_ps, 1)
                if n == 3:
                    qk_square(0)
                    transpose_v()
                if n == 6:
                    qk_rotate(0)
                    qk_square(1)
                if n == 8:
                    qk_square(2)
                if n == 9:
                    qk_rotate(1)
                if n == 11:
                    qk_rotate(2)

            pe.wait_ge(q_done, 3)
            pe.wait_ge(s_y, 4)
            for b in range(2):
                for x in range(8):
                    g = 8 * b + x
                    head = HEADS[x]
                    if g >= 4:
                        pe.wait_ge(a_ctx, g - 3)
                        pe.wait_ge(a_loc, g - 3)
                    else:
                        pe.wait_ge(*oin_free(14 + (x + 2) % 4))
                    mm(ps[x % 4][:], qt[:, head % 4, b * P:(b + 1) * P], kpad[:, head // 4, :],
                       start=True, stop=True).then_inc(a_s, 1)
                for x in range(9):
                    g = 8 * b + x
                    if x < 8:
                        pe.wait_ge(a_p, g + 1)
                        if g >= 2:
                            pe.wait_ge(a_tc, g - 1)
                        for s in range(4):
                            m = nc.tensor.transpose(ps[4 + x % 2][:, s * P:(s + 1) * P],
                                                    sc[:, x, s * P:(s + 1) * P], ident[:])
                        m.then_inc(a_t, 1)
                    if x >= 1:
                        y = x - 1
                        pe.wait_ge(a_tc, g)
                        if b == 0 and y == 0:
                            pe.wait_ge(v_done, 1)
                        for s in range(4):
                            m = mm(ps[6 + b][:, (y // 2) * P:(y // 2 + 1) * P], vpad[:, s, y % 2, :],
                                   pt[:, y % 2, s, :], start=(s == 0 and y % 2 == 0), stop=(s == 3 and y % 2 == 1))
                        m.then_inc(a_o, 1)

            pe.wait_ge(a_ctx, 16)
            pe.wait_ge(a_loc, 16)
            project_out(J_OWOUT, (4, 5, 6, 7, 0, 1, 2, 3), L, (16, (9, 9, 9, 9, 11, 11, 11, 11)))
            pe.wait_ge(res_done, 16 + KT)
            norm_mean(3, ssum, L)

            pe.wait_ge(n_ready, 32)
            pe.wait_ge(c_moe, 64)
            for t in range(2):
                for k in range(KT):
                    m = mm(ps[6][:, t * NEXP:(t + 1) * NEXP], ht[:, k, t * P:(t + 1) * P], rw[:, k, :],
                           start=(k == 0), stop=(k == KT - 1))
            m.then_inc(r_lg, 1)
            for t in range(2):
                for h in range(2):
                    for i in range(4):
                        m = nc.tensor.transpose(ps[2 * t + h][:, i * P:(i + 1) * P],
                                                ht[:, 4 * h + i, t * P:(t + 1) * P], ident[:])
                    m.then_inc(t_ps, 1)
            pe.wait_ge(r_sel, 1)
            mm(ps[7][:, 0:8], tri[:, 0], sel[:, 0], start=True, stop=True)
            mm(ps[7][:, 8:16], tri[:, 1], sel[:, 0], start=True, stop=False)
            mm(ps[7][:, 8:16], tri[:, 0], sel[:, 1], start=False, stop=True)
            mm(ps[7][:, 16:24], tri[:, 1], sel[:, 0], start=True, stop=False)
            mm(ps[7][:, 16:24], tri[:, 1], sel[:, 1], start=False, stop=True).then_inc(r_pos, 1)

            def gather(h, made):
                pe.wait_ge(hot_made, made)
                for kk in range(4):
                    k = 4 * h + kk
                    for i in range(4):
                        src = hklo if i % 2 else hkhi
                        m = mm(ps[7][:, kk * P:(kk + 1) * P], src[:, i // 2, k * P:(k + 1) * P], hot[:, i // 2],
                               start=(i == 0), stop=(i == 3))
                m.then_inc(misc, 1)

            def scatter(q):
                for kk in range(2):
                    k = 2 * q + kk
                    mm(ps[7][:, kk * L:(kk + 1) * L], yhi[:, k * P:(k + 1) * P], hott[:], start=True, stop=False)
                    m = mm(ps[7][:, kk * L:(kk + 1) * L], ylo[:, k * P:(k + 1) * P], hott[:], start=False, stop=True)
                m.then_inc(misc, 1)

            pe.wait_ge(t_lo, 4)
            gather(0, 1)
            pe.wait_ge(misc_free, 1)
            gather(1, 1)

            def round_of(r):
                def block_wait(i):
                    wait_block(J_MOE + i, r, ROUND_BLOCKS)
                    return J_MOE + i

                def rhs(j, at):
                    return whi[:, j % SPLIT, at:at + CHUNK], wlo[:, j % SPLIT, at:at + CHUNK]

                def chunk_in(c, first, bank):
                    for h in range(2):
                        j = block_wait(first + h)
                        for kk in range(4):
                            k = 4 * h + kk
                            w = rhs(j, kk * CHUNK)
                            mm(ps[bank][:], ghi[:, k], w[0], start=(k == 0), stop=False)
                            mm(ps[bank][:], ghi[:, k], w[1], start=False, stop=False)
                            m = mm(ps[bank][:], glo[:, k], w[0], start=False, stop=(k == KT - 1))
                        m.then_inc(used, 1)

                def gate(c):
                    if c == 0:
                        pe.wait_ge(misc_free, 7 * r + 2)
                    pe.wait_ge(e_a, NCH * r + (max(c - 1, 0) + 1))
                    chunk_in(c, gate_block(c), c % 2)

                def up(c):
                    chunk_in(c, gate_block(c) + 2, 2 + c % 2)

                def turn(c):
                    pe.wait_ge(e_a, NCH * r + (c + 2))
                    pe.wait_ge(e_lo, NCH * r + (c + 1))
                    for i in range(4):
                        m = nc.tensor.transpose(ps[6][:, i * P:(i + 1) * P], am[:, i * P:(i + 1) * P], ident[:])
                    m.then_inc(e_t, 1)

                def down(c):
                    pe.wait_ge(e_lo, NCH * r + (c + 2))
                    if c == 0:
                        pe.wait_ge(e_y, r + 1)
                    for h in range(2):
                        j = block_wait(down_block(c) + h)
                        for i in range(4):
                            f, n = 2 * h + i // 2, i % 2
                            w = rhs(j, (i // 2) * D + n * CHUNK)
                            mm(ps[4 + n][:], athi[:, f], w[0], start=(c == 0 and f == 0), stop=False)
                            mm(ps[4 + n][:], athi[:, f], w[1], start=False, stop=False)
                            m = mm(ps[4 + n][:], atlo[:, f], w[0], start=False, stop=(c == NCH - 1 and f == 3))
                        m.then_inc(used, 1)

                def spare(i):
                    pe.wait_ge(misc_free, 2 + 7 * r + i)

                for c in range(NCH):
                    gate(c)
                    if c:
                        turn(c - 1)
                    up(c)
                    if c == NCH - 1:
                        spare(5)
                        gather(0, r + 2)
                    if c:
                        down(c - 1)
                    if c == 0:
                        pe.wait_ge(e_y, r + 1)
                    if c < 4:
                        spare(c)
                        scatter(c)
                    if c == 4:
                        spare(4)
                        for t in range(2):
                            nc.tensor.transpose(ps[7][:, t * P:(t + 1) * P], hot[:, t].bitcast(F32), ident[:])
                        for t in range(2):
                            m = mm(ps[7][:, 256:257], hot[:, t].bitcast(F32), cw[:, t:t + 1],
                                   start=(t == 0), stop=(t == 1))
                        m.then_inc(misc, 1)
                turn(NCH - 1)
                spare(6)
                gather(1, r + 2)
                down(NCH - 1)

            with pe.Fori(0, NEXP) as r:
                round_of(r)
            crowded = pe.value_load(infoi[0:1, 0:1], min_val=0, max_val=OVER)
            with pe.Fori(NEXP, NEXP + OVER) as r:
                with pe.If(r < crowded + NEXP):
                    round_of(r)
            pe.wait_ge(e_y, crowded + (NEXP + 1))
            for q in range(4):
                pe.wait_ge(misc_free, crowded * 7 + (2 + 7 * NEXP + q))
                scatter(q)

        @block.scalar
        def _(act):
            def copy(dst, src, scale=1.0):
                return nc.scalar.activation(dst, src, ACT.Copy, scale=scale)

            def split(j, turn=0, per=0, n=BLK):
                slot, uses = block_at(j, turn, per)
                act.wait_ge(raw_loaded[slot], uses * 16)
                if per or j >= SPLIT:
                    act.wait_ge(used, turn * per + (j - SPLIT + 1) if per else j - SPLIT + 1)
                copy(whi[:, j % SPLIT, 0:n], raw[:, slot, 0:n]).then_inc(hi_made, 1)

            done = [0]

            def until(j_end):
                while done[0] < j_end:
                    j = done[0]
                    split(j, n=width_of(j))
                    done[0] += 1

            act.dma_start(vec[:], a["c_vec"]).then_inc(c_vec, 16)
            for src, dst in ((a["c_z"], zt[:]), (a["c_w12"], w12[:])):
                act.dma_start(dst, src).then_inc(c_net, 16)
            for src, dst in ((a["c_sq"][0], ident[:]), (a["c_sq"][1], mean[:])):
                act.dma_start(dst, src).then_inc(c_even, 16)
            for src, dst in ((a["c_w3"], w3[:]), (a["c_decay"], decay[:])):
                act.dma_start(dst, src).then_inc(c_filt, 16)
            act.dma_start(xin[:], a["xt"].rearrange("(k p) t -> p k t", p=P)).then_inc(c_x, 16)
            for src, dst in ((a["c_dft"], dft[:]), (a["c_dft2"], dft2[:])):
                act.dma_start(dst, src).then_inc(c_filt, 16)
            act.wait_ge(c_vec, 16)
            nc.scalar.activation(scond[:], col("cond", 0, 16).rearrange("p (k c) -> p k c", c=2),
                                 ACT.Silu).then_inc(act_s, 1)
            act.wait_ge(act_s, 1)
            copy(sc4[:, :, 0:2], scond[:]).then_inc(act_s, 1)

            def copy_rows(bank, buf, block, cols):
                act.wait_ge(used, block)
                if cols is not None:
                    act.wait_ge(cols_made, cols)
                copy(rows[:, buf], ps[bank][0:4, :]).then_inc(rows_made, 1)

            def even_rows(c):
                copy_rows(6, c % 2, ada_at(c) + 2, c - 1 if c >= 2 else None)

            def filter_sine(i):
                act.wait_ge(f_arg, i + 1)
                nc.scalar.activation(sred[:], sarg[:], ACT.Sin).then_inc(f_sin, 1)

            def filter_out(h):
                act.wait_ge(f_taps, h + 1)
                nc.scalar.activation(hf[:], hf[:], ACT.Abs)
                nc.scalar.activation(hb[:], hb[:], ACT.Abs).then_inc(f_abs, 1)
                for m in range(5):
                    act.wait_ge(f_k, 5 * h + m + 1)
                    copy(kf[:, m, h * HALF:(h + 1) * HALF], ps[4 + (5 * h + m) % 2][:, 0:HALF]).then_inc(f_kcopy, 1)

            def norm_act(n, src, ready, sqb, rs, width, h_free, full=None):
                norm_squares(n, src, ready, sqb, width)
                norm_scale(n, sqb, rs, width, h_free, full)

            def norm_squares(n, src, ready, sqb, width):
                for d in range(KT):
                    act.wait_ge(*ready(d))
                    if d >= 2:
                        act.wait_ge(n_sum, 7 * n + max(1, d - 2))
                    nc.scalar.activation(sqb[:, d % 2, 0:width], src[:, d, 0:width], ACT.Square).then_inc(n_sq, 1)

            def norm_scale(n, sqb, rs, width, h_free, full=None):
                act.wait_ge(n_mean, n + 1)
                nc.scalar.activation(rs[:, 0:width], ps[6 if n else 5][:, 0:width], ACT.Sqrt,
                                     bias=eps[:]).then_inc(n_root, 1)
                act.wait_ge(used, h_free) if h_free else None
                for d in range(KT):
                    act.wait_ge(n_h, 8 * n + d + 1)
                    h = sqb[:, d % 2, 0:width] if full is None else full[:, d, :]
                    copy(hhi[:, d, 0:width], h).then_inc(n_hi, 1)

            until(1)
            filter_sine(0)
            until(3)
            even_rows(0)
            until(4)
            filter_sine(1)
            until(5)
            even_rows(1)
            until(7)
            norm_squares(0, xin, lambda d: (c_x, 16), sq0, T)
            even_rows(2)
            filter_out(0)
            until(8)
            even_rows(3)
            filter_out(1)
            act.wait_ge(setup, 2)
            norm_scale(0, sq0, rstd0, T, 0)

            for n, tile in enumerate(WIN_TILES):
                until(win_at(n // 2) + 3)
                act.wait_ge(*((used, win_at(n // 2) + 1) if n % 2 else (w_ps, n // 2 + 1)))
                if n < 2:
                    copy(fnt[:, n], ps[n % 4][:]).then_inc(w_free, 1)
                    if n:
                        until(win_at(0) + 5)
                        even_rows(EARLY)
                    continue
                i, kind, q = (n - 2) // 6, (n - 2) % 6 // 2, n % 2
                dst = (tmp[:, q], tmp[:, 2 + q], x0c[:, 2 * i + q])[kind]
                if kind < 2 and i:
                    act.wait_ge(u_made, 2 * i)
                nc.scalar.activation(dst, ps[n % 4][:], ACT.Identity, scale=col("short", 18 + tile)).then_inc(w_mid, 1)
                if n % 2 and EARLY + n // 2 < ADA // 2:
                    until(win_at(n // 2) + 5)
                    even_rows(EARLY + n // 2)

                def copy_u(c):
                    act.wait_ge(ut_ps, c + 1)
                    copy(utok[:, :, c * P:(c + 1) * P],
                         ps[4 + c % 2][:].rearrange("p (s c) -> p s c", s=4)).then_inc(ut_copy, 1)

                if n >= 9 and (n - 9) % 6 == 0:
                    copy_u((n - 9) // 3)
                    copy_u((n - 9) // 3 + 1)
            copy_u(4)
            copy_u(5)
            act.wait_ge(u_made, HT)
            for q in range(2):
                act.wait_ge(fn_ab, q + 1)
                copy(tmp[:, 2 * q], ps[2 * q][:])
                copy(tmp[:, 2 * q + 1], ps[2 * q + 1][:]).then_inc(fn_abc, 1)
            for i in range(HT):
                nc.scalar.activation(u[:, i], u[:, i], ACT.Identity, scale=col("skip", i)).then_inc(skips, 1)
            for q in range(2):
                act.wait_ge(m_ps, q + 1)
                copy(hhi[:, HT + q], ps[4 + q][:]).then_inc(m_hi, 1)
            for i in range(HT):
                act.wait_ge(m_z, i + 1)
                copy(hhi[:, i], x0c[:, i]).then_inc(m_hi, 1)

            until(J_WOUT + 3)
            for j in range(WOUT):
                act.wait_ge(used, J_WOUT + j + 1)
                until(J_WOUT + j + 4)
            norm_act(1, res, lambda d: (res_done, d + 1), sq, rstd, T, J_FFN)

            def silu(turn):
                for q in range(2):
                    act.wait_ge(ff_lo, turn)
                    nc.scalar.activation(sil[:, q], ps[q][:], ACT.Silu).then_inc(ff_silu, 1)

            def split_a(turn):
                for q in range(2):
                    act.wait_ge(ff_a, turn + q + 1)
                    copy(ahi[:, q], sil[:, q]).then_inc(ff_hi, 1)

            def odd_rows(pair, block):
                copy_rows(7, 0, block, pair + ADA // 2)

            until(J_FFN + 3)
            act.wait_ge(used, J_FFN + 1)
            silu(0)
            until(J_FFN + 6)
            act.wait_ge(used, J_FFN + 4)
            split_a(0)
            until(J_FFN + 7)
            with act.Fori(0, FF_PAIRS - 1) as r:
                odd_rows(r, r * 6 + J_BODY)
                for x in range(2, 4):
                    split(J_BODY + x, r, 6, width_of(J_BODY + x))
                act.wait_ge(used, r * 6 + (J_BODY + 1))
                silu(r * 2 + 2)
                for x in range(4, 8):
                    split(J_BODY + x, r, 6, width_of(J_BODY + x))
                split_a(r * 2 + 2)
            odd_rows(FF_PAIRS - 1, J_TAIL)
            done[0] = J_TAIL + 2
            until(J_OWIN)
            odd_rows(FF_PAIRS, J_OWIN)
            until(J_OWIN + 1)
            norm_act(2, res, lambda d: (res_done, 8 + d + 1), sq, rstd, T, J_TAIL + 1)

            def qk_root(y):
                act.wait_ge(q_ms, y + 1)
                act.wait_ge(q_n, y) if y else None
                nc.scalar.activation(rr[:], ps[4 + y % 2][:], ACT.Sqrt, bias=eps[:]).then_inc(q_root, 1)

            for n in range(2 * OWIN):
                until(min(J_OWIN + n // 2 + 3, J_MOE))
                if n < 6 or (n - 6) % 3 == 0:
                    act.wait_ge(*((used, J_OWIN + n // 2 + 1) if n % 2 else (q_ps, n // 2 + 1)))
                src = ps[n % 4]
                if n == 0:
                    nc.scalar.activation(qsq[:, 0], src[:], ACT.Square).then_inc(q_sq, 1)
                    copy(qraw[:, 0], src[:]).then_inc(q_raw, 1)
                elif n == 1:
                    copy(vt[:], src[:]).then_inc(v_copy, 1)
                elif n < 6:
                    y, at = n // 2, (n % 2) * L
                    nc.scalar.activation(qsq[:, y, at:at + L], src[:, 0:L], ACT.Square).then_inc(q_sq, 1)
                    copy(qraw[:, y, at:at + L], src[:, 0:L]).then_inc(q_raw, 1)
                elif (n - 6) % 3 == 0:
                    if n > 6:
                        act.wait_ge(s_hx, (n - 6) // 3)
                    copy(gcs[:], src[:, 0:L]).then_inc(s_gc, 1)
                if n == 4:
                    qk_root(0)
                if n == 7:
                    qk_root(1)
                if n == 9:
                    qk_root(2)
            act.wait_ge(used, J_OWOUT)
            act.wait_ge(s_y, 4)
            copy(hhi[:, 4:8, 0:L], ysc[:]).then_inc(m_hi, 1)

            for b in range(2):
                for x in range(8):
                    g = 8 * b + x
                    act.wait_ge(a_s, g + 1)
                    copy(sc[:, x, L:T], ps[x % 4][:, L:T], 0.125).then_inc(a_ctx, 1)
                act.wait_ge(a_max, b + 1)
                nc.scalar.activation(esink[:], esink[:], ACT.Exp).then_inc(a_sink, 1)
                for x in range(8):
                    nc.scalar.activation(sc[:, x], sc[:, x], ACT.Exp, bias=nmax[:, x:x + 1],
                                         accum_out=ssm[:, x:x + 1]).then_inc(a_exp, 1)
                for x in range(8):
                    g = 8 * b + x
                    act.wait_ge(a_t, g + 1)
                    if g >= 2:
                        act.wait_ge(a_o, g - 1)
                    copy(pt[:, x % 2], ps[4 + x % 2][:].rearrange("p (s c) -> p s c", s=4)).then_inc(a_tc, 1)
                act.wait_ge(a_o, 8 * b + 8)
                copy(hhi[:, 0:4, b * P:(b + 1) * P],
                     ps[6 + b][:].rearrange("p (k c) -> p k c", k=4)).then_inc(m_hi, 1)
            for j in range(OWOUT):
                act.wait_ge(used, J_OWOUT + j + 1)
                until(min(J_OWOUT + j + 4, J_MOE))
            norm_act(3, res, lambda d: (res_done, 16 + d + 1), sq, rstd, L, J_MOE, full=ht)

            act.wait_ge(r_sub, 1)
            nc.scalar.activation(ex[:], ex[:], ACT.Exp).then_inc(r_exp, 1)
            for i in range(4):
                act.wait_ge(t_ps, i + 1)
                copy(hkhi[:, i // 2, (i % 2) * 512:(i % 2) * 512 + 512], ps[i][:]).then_inc(t_hi, 1)

            def split_gathered(h, count, gathered):
                act.wait_ge(misc, count)
                copy(ghi[:, 4 * h:4 * h + 4, :], ps[7][:].rearrange("p (k c) -> p k c", k=4)).then_inc(g_hi, 1)

            split_gathered(0, 1, 0)
            split_gathered(1, 2, 0)

            def result_hi():
                for n in range(2):
                    nc.scalar.activation(yhi[:, n * CHUNK:(n + 1) * CHUNK], ps[4 + n][:], ACT.Identity,
                                         scale=wslot[:]).then_inc(e_yhi, 1)

            act.wait_ge(zeroed, 4)
            act.wait_ge(e_a, 1)
            act.wait_ge(e_lo, 1)

            def round_of(r):
                def chunk_hi(c):
                    act.wait_ge(e_t, NCH * r + c + 1)
                    copy(athi[:], ps[6][:].rearrange("p (k c) -> p k c", k=4)).then_inc(e_hi, 1)

                for x in range(ROUND_BLOCKS):
                    if x == 3:
                        act.wait_ge(used, r * ROUND_BLOCKS + J_MOE)
                        act.wait_ge(misc_free, 7 * r + 2)
                        result_hi()
                    for c in range(NCH):
                        if x == gate_block(c) + 4:
                            act.wait_ge(used, r * ROUND_BLOCKS + (J_MOE + gate_block(c) + 2))
                            act.wait_ge(e_a, NCH * r + (c + 1))
                            nc.scalar.activation(sg[:], ps[c % 2][:], ACT.Silu).then_inc(e_silu, 1)
                        if c < NCH - 1 and x == down_block(c):
                            chunk_hi(c)
                    if x == 30:
                        act.wait_ge(misc, 7 * r + 7)
                        copy(hott[:], ps[7][:, 0:L])
                        copy(wslot[:], ps[7][:, L:L + 1]).then_inc(misc_free, 1)
                    if x == 40:
                        split_gathered(0, 7 * r + 8, r)
                    split(J_MOE + x, r, ROUND_BLOCKS)
                chunk_hi(NCH - 1)
                split_gathered(1, 7 * r + 9, r)

            with act.Fori(0, NEXP) as r:
                round_of(r)
            crowded = act.value_load(infoi[0:1, 0:1], min_val=0, max_val=OVER)
            with act.Fori(NEXP, NEXP + OVER) as r:
                with act.If(r < crowded + NEXP):
                    round_of(r)
            act.wait_ge(used, crowded * ROUND_BLOCKS + (NEXP * ROUND_BLOCKS + J_MOE))
            result_hi()

        @block.vector
        def _(dve):
            vv = nc.vector
            own = Steps(dve, dve_s)

            def split(j, turn=0, per=0, n=BLK):
                slot, uses = block_at(j, turn, per)
                if slot == POOL_SLOT:
                    return
                dve.wait_ge(hi_made, turn * per + (j + 1) if per else j + 1)
                vv.tensor_tensor(wlo[:, j % SPLIT, 0:n], raw[:, slot, 0:n], whi[:, j % SPLIT, 0:n].bitcast(F32),
                                 ALU.subtract).then_inc(raw_free[slot], 1)

            done = [0]

            def until(j_end):
                while done[0] < j_end:
                    j = done[0]
                    split(j, n=width_of(j))
                    done[0] += 1

            def filter_argument(i):
                dve.wait_ge(f_ps, i + 1)
                if i:
                    dve.wait_ge(f_sin, 1)
                own.step(vv.tensor_scalar(sarg[:], ps[i][0:64, 0:L], col("b1" if i == 0 else "b2")[0:64],
                                          col("freq")[0:64], ALU.add, ALU.mult))
                own.step(vv.tensor_scalar(rstd0[0:64, 0:L], sarg[:], float(1 / (2 * np.pi)), ROUND, ALU.mult, ALU.add))
                own.step(vv.tensor_scalar(rstd0[0:64, 0:L], rstd0[0:64, 0:L], ROUND, None, ALU.subtract))
                for part in TURN:
                    own.step(vv.scalar_tensor_tensor(out=sarg[:], in0=rstd0[0:64, 0:L], scalar=-part, in1=sarg[:],
                                                     op0=ALU.mult, op1=ALU.add))
                vv.tensor_scalar(sarg[:], sarg[:], 3.1415925, -3.1415925, ALU.min, ALU.max).then_inc(f_arg, 1)

            def filter_taps(h):
                dve.wait_ge(f_ps, 3 + h)
                if h:
                    dve.wait_ge(f_l1, 1)
                for t in range(2):
                    vv.tensor_tensor(hf[:, t], ps[t][:, 0:HALF], decay[:, t, h * HALF:(h + 1) * HALF], ALU.mult)
                    m = vv.tensor_tensor(hb[:, t], ps[2 + t][:, 0:HALF], decay[:, t, h * HALF:(h + 1) * HALF], ALU.mult)
                own.step(m)
                own.step(vv.memset(hb[0:1, 0, :], 0.0))
                vv.tensor_tensor(hs[:], hf[:], hb[:], ALU.add)
                vv.tensor_tensor(hd[:], hf[:], hb[:], ALU.subtract).then_inc(f_taps, 1)

            dve.wait_ge(c_vec, 16)
            dve.wait_ge(act_s, 2)
            vv.tensor_tensor(sc4[:, :, 2:4], scond[:], sc4[:, :, 0:2].bitcast(F32), ALU.subtract).then_inc(silu_c, 1)
            filter_argument(0)
            until(3)
            dve.wait_ge(c_even, 32)
            vv.tensor_tensor(pick[:], ident[0:4, 0:2], ident[0:4, 2:4], ALU.add).then_inc(setup, 1)
            filter_argument(1)
            until(5)
            dve.wait_ge(c_filt, 16 * 4)
            filter_taps(0)
            until(7)
            filter_taps(1)
            until(8)

            def gains(mod, i, norm, g):
                own.step(vv.scalar_tensor_tensor(out=gain[:, g + i], in0=mod[:, 8 + 24 * i:16 + 24 * i, :], scalar=1.0,
                                                 in1=col(norm, 0, 8).unsqueeze(2).to_broadcast([P, 8, 2]),
                                                 op0=ALU.add, op1=ALU.mult))

            def even_mod(t0, t1):
                own.step(vv.tensor_tensor(emod[:, t0:t1], ps[7][:, 2 * t0:2 * t1].rearrange("p (t c) -> p t c", c=2),
                                          col("e_ada_b", t0, t1 - t0).unsqueeze(2).to_broadcast([P, t1 - t0, 2]),
                                          ALU.add))

            def norm_dve(n, src, sqb, rs, width, mod, shift, full=None):
                dve.wait_ge(n_root, n + 1)
                own.step(vv.reciprocal(rs[:, 0:width], rs[:, 0:width]))

                def lo(d):
                    dve.wait_ge(n_hi, 8 * n + d + 1)
                    h = sqb[:, d % 2, 0:width] if full is None else full[:, d, :]
                    vv.tensor_tensor(hlo[:, d, 0:width], h, hhi[:, d, 0:width].bitcast(F32),
                                     ALU.subtract).then_inc(n_ready, 1)

                for d in range(KT):
                    h = sqb[:, d % 2, 0:width] if full is None else full[:, d, :]
                    if d >= 2:
                        dve.wait_ge(n_ready, 8 * n + d - 1)
                    own.step(vv.tensor_tensor(h, src[:, d, 0:width], rs[:, 0:width], ALU.mult))
                    for s in range(width // L):
                        m = vv.tensor_scalar(h[:, s * L:(s + 1) * L], h[:, s * L:(s + 1) * L], gain[:, n, d, s:s + 1],
                                             mod[:, shift + d, s:s + 1], ALU.mult, ALU.add)
                    m.then_inc(n_h, 1)
                    if d:
                        lo(d - 1)
                lo(KT - 1)

            dve.wait_ge(cols_made, EARLY)
            even_mod(0, 4 * EARLY)
            dve.wait_ge(f_l1, 2)
            vv.reciprocal(il1[:], ps[7][:, 4 * ADA:4 * ADA + HT]).then_inc(emod_made, 1)
            gains(emod, 0, "e_norm1", 0)
            norm_dve(0, xin, sq0, rstd0, T, emod, 0)

            for n, tile in enumerate(WIN_TILES):
                until(win_at(n // 2) + 3)
                if n < 2:
                    if n:
                        until(win_at(0) + 5)
                    continue
                i, kind, q = (n - 2) // 6, (n - 2) % 6 // 2, n % 2
                dst = half((tmp[:, q], tmp[:, 2 + q], x0c[:, 2 * i + q])[kind])
                src = half(ps[n % 4][:])
                dve.wait_ge(w_mid, n - 1)
                own.step(vv.scalar_tensor_tensor(out=dst[:, :, 1:L], in0=src[:, :, 0:L - 1], scalar=col("short", tile),
                                                 in1=dst[:, :, 1:L], op0=ALU.mult, op1=ALU.add))
                vv.scalar_tensor_tensor(out=dst[:, :, 0:L - 1], in0=src[:, :, 1:L], scalar=col("short", 36 + tile),
                                        in1=dst[:, :, 0:L - 1], op0=ALU.mult, op1=ALU.add).then_inc(w_free, 1)
                if kind == 1:
                    dve.wait_ge(w_free, n + 1)
                    vv.tensor_tensor(u[:, 2 * i + q], tmp[:, q], tmp[:, 2 + q], ALU.mult).then_inc(u_made, 1)
                if n % 2 and EARLY + n // 2 < ADA // 2:
                    until(win_at(n // 2) + 5)
            dve.wait_ge(cols_made, ADA // 2)
            even_mod(4 * EARLY, 2 * ADA)
            vv.engine_nop().then_inc(emod_made, 1)
            gains(emod, 1, "e_norm2", 0)

            for q in range(2):
                dve.wait_ge(m_hi, q + 1)
                vv.tensor_tensor(hlo[:, HT + q], ps[4 + q][:], hhi[:, HT + q].bitcast(F32),
                                 ALU.subtract).then_inc(m_ready, 1)

            def products(i):
                dve.wait_ge(x_ps, i + 1)
                dve.wait_ge(m_ps, i + 2)
                at = slice(i * P, (i + 1) * P)
                re, im = ps[2 * (i % 2)], ps[2 * (i % 2) + 1]
                pairs = ((re, kf[:, 0:3:2, at]), (im, kf[:, 3:5, at]), (re, kf[:, 3:5, at]), (im, kf[:, 1:3, at]))
                for n, (x, k) in enumerate(pairs):
                    m = vv.tensor_tensor(tmp[:, n].rearrange("p (m s c) -> p m s c", m=2, s=2),
                                         x[:].rearrange("p (m s c) -> p m s c", m=2, s=2),
                                         k.unsqueeze(2).to_broadcast([P, 2, 2, P]), ALU.mult)
                m.then_inc(x_prod, 1)

            def result(i):
                dve.wait_ge(m_ps, i + 3)
                dve.wait_ge(skips, i + 1)
                own.step(vv.scalar_tensor_tensor(out=u[:, i], in0=ps[4 + i % 2][:], scalar=il1[:, i:i + 1],
                                                 in1=u[:, i], op0=ALU.mult, op1=ALU.add))
                vv.tensor_tensor(x0c[:, i], u[:, i], x0c[:, i], ALU.mult).then_inc(m_z, 1)

            def result_lo(i):
                dve.wait_ge(m_hi, 3 + i)
                vv.tensor_tensor(hlo[:, i], x0c[:, i], hhi[:, i].bitcast(F32), ALU.subtract).then_inc(m_ready, 1)

            products(0)
            for i in range(HT):
                if i + 1 < HT:
                    products(i + 1)
                result(i)
                if i:
                    result_lo(i - 1)
            result_lo(HT - 1)

            def residual(n, j, base, mod, width, lookahead):
                until(lookahead)
                dve.wait_ge(*((used, j + 1) if n % 2 else (o_ps, base // 2 + n // 2 + 1)))
                for s in range(width // L):
                    m = vv.scalar_tensor_tensor(out=res[:, n, s * L:(s + 1) * L], in0=ps[n % 4][:, s * L:(s + 1) * L],
                                                scalar=mod[:, 16 + n, s:s + 1], in1=res[:, n, s * L:(s + 1) * L],
                                                op0=ALU.mult, op1=ALU.add)
                m.then_inc(res_done, 1)

            until(J_WOUT + 3)
            dve.wait_ge(c_res, 16)
            for n in range(KT):
                residual(n, J_WOUT + n // 2, 0, emod, T, J_WOUT + n // 2 + 3)
            norm_dve(1, res, sq, rstd, T, emod, 24)

            def add_down(turn, last):
                for d in range(KT):
                    if d < KT - 1:
                        dve.wait_ge(ff_d, turn * 7 + d + 1)
                    else:
                        dve.wait_ge(used, last)
                    dve.wait_ge(ff_added, turn * 8 + (d + 1))
                    vv.tensor_tensor(facc[:, d], facc[:, d], ps[4 + d % 3][:], ALU.add).then_inc(ff_added, 1)

            def activate(turn, last):
                dve.wait_ge(used, last)
                for q in range(2):
                    dve.wait_ge(ff_silu, turn * 2 + (q + 1))
                    vv.tensor_tensor(sil[:, q], sil[:, q], ps[2 + q][:], ALU.mult).then_inc(ff_a, 1)
                for q in range(2):
                    dve.wait_ge(ff_hi, turn * 2 + (q + 1))
                    vv.tensor_tensor(alo[:, q], sil[:, q], ahi[:, q].bitcast(F32), ALU.subtract).then_inc(ff_lo, 1)

            def odd_modulation(unit):
                dve.wait_ge(cols_made, unit + (ADA // 2 + 1))
                bias = vec[:, bass.ds(unit * 4 + VEC["o_ada_b"].start, 4)]
                vv.tensor_tensor(omod[:, bass.ds(unit * 4, 4), :], ps[6][:, 0:8].rearrange("p (t c) -> p t c", c=2),
                                 bias.unsqueeze(2).to_broadcast([P, 4, 2]), ALU.add).then_inc(oa_read, 1)

            until(J_FFN + 6)
            activate(0, J_FFN + 4)
            until(J_FFN + 7)
            with dve.Fori(0, FF_PAIRS - 1) as r:
                for x in range(2, 4):
                    split(J_BODY + x, r, 6, width_of(J_BODY + x))
                odd_modulation(r)
                add_down(r, r * 6 + (J_BODY + 3))
                for x in range(4, 7):
                    split(J_BODY + x, r, 6, width_of(J_BODY + x))
                activate(r + 1, r * 6 + (J_BODY + 5))
                split(J_BODY + 7, r, 6, width_of(J_BODY + 7))
            odd_modulation(FF_PAIRS - 1)
            done[0] = J_TAIL + 2
            until(J_TAIL + 3)
            add_down(FF_PAIRS - 1, J_TAIL + 1)
            until(J_OWIN)
            odd_modulation(FF_PAIRS)
            dve.wait_ge(oa_read, FF_PAIRS + 1)
            gains(omod, 0, "o_norm1", 2)
            gains(omod, 1, "o_norm2", 2)
            for d in range(KT):
                dve.wait_ge(ff_added, 4 + 8 * FF_PAIRS) if d == 0 else None
                for s in range(2):
                    m = vv.scalar_tensor_tensor(out=res[:, d, s * L:(s + 1) * L], in0=facc[:, d, s * L:(s + 1) * L],
                                                scalar=emod[:, 40 + d, s:s + 1], in1=res[:, d, s * L:(s + 1) * L],
                                                op0=ALU.mult, op1=ALU.add)
                m.then_inc(res_done, 1)
            until(J_OWIN + 1)
            norm_dve(2, res, sq, rstd, T, omod, 0)

            def qk_norm(y):
                dve.wait_ge(q_root, y + 1)
                own.step(vv.reciprocal(rr[:], rr[:]))
                dve.wait_ge(q_raw, 1 + 2 * y)
                vv.scalar_tensor_tensor(out=qn[:, y], in0=qraw[:, y], scalar=col("q_norm" if y else "k_norm"),
                                        in1=rr[:], op0=ALU.mult, op1=ALU.mult).then_inc(q_n, 1)

            def qk_turn(y):
                dve.wait_ge(q_rot, y + 1)
                n = T if y else L
                dve.wait_ge(zeroed, 2)
                for dst, src, i in ((qsq, qn[:, y, 0:n], 0), (qraw, ps[6 + y % 2][:, 0:n], 1)):
                    d = dst[:, y, 0:n]
                    if y:
                        m = vv.tensor_tensor(half(d), half(src), rope[:, i:i + 1, :].to_broadcast([P, 2, L]), ALU.mult)
                    else:
                        m = vv.tensor_tensor(d, src, rope[:, i, :], ALU.mult)
                own.step(m)
                if y:
                    vv.tensor_tensor(qt[:, 2 * y - 2:2 * y, :], half(qsq[:, y]), half(qraw[:, y]),
                                     ALU.add).then_inc(q_done, 1)
                else:
                    for g in range(2):
                        rows = slice(64 * g, 64 * g + 64)
                        vv.tensor_tensor(kpad[rows, g, 0:L], qsq[rows, 0, 0:L], qraw[rows, 0, 0:L], ALU.add)
                        m = vv.tensor_copy(kpad[rows, g, L:T], qn[rows, 0, L:T])
                    m.then_inc(q_done, 1)

            def pad_v():
                dve.wait_ge(v_ps, 1)
                dve.wait_ge(zeroed, 2)
                v = ps[5][:].rearrange("p (s c) -> p s c", s=4)
                vv.tensor_copy(vpad[:, :, 0, 0:64], v[:, :, 0:64])
                vv.tensor_copy(vpad[:, :, 1, 64:128], v[:, :, 64:128]).then_inc(v_done, 1)

            for n in range(2 * OWIN):
                until(min(J_OWIN + n // 2 + 3, J_MOE))
                i, kind = (n - 6) // 3, (n - 6) % 3
                if n >= 6 and kind:
                    dve.wait_ge(*((used, J_OWIN + n // 2 + 1) if n % 2 else (q_ps, n // 2 + 1)))
                if n >= 6 and kind == 1:
                    dve.wait_ge(s_gc, i + 1)
                    vv.tensor_tensor(gm[:], gcs[:], ps[n % 4][:, 0:L], ALU.mult).then_inc(s_hx, 1)
                    dve.wait_ge(s_hx, i + 1)
                    own.step(vv.tensor_scalar(gcv[:], gm[:], col("sc", 4 + i), None, ALU.mult))
                    own.step(vv.scalar_tensor_tensor(out=gcv[:, 1:L], in0=gm[:, 0:L - 1], scalar=col("sc", i),
                                                     in1=gcv[:, 1:L], op0=ALU.mult, op1=ALU.add))
                    own.step(vv.scalar_tensor_tensor(out=gcv[:, 0:L - 1], in0=gm[:, 1:L], scalar=col("sc", 8 + i),
                                                     in1=gcv[:, 0:L - 1], op0=ALU.mult, op1=ALU.add))
                if n >= 6 and kind == 2:
                    vv.tensor_tensor(ysc[:, i], ps[n % 4][:, 0:L], gcv[:], ALU.mult).then_inc(s_y, 1)
                    dve.wait_ge(s_y, i + 1)
                if n == 4:
                    pad_v()
                    qk_norm(0)
                if n == 7:
                    qk_turn(0)
                    qk_norm(1)
                if n == 9:
                    qk_norm(2)
                if n == 10:
                    qk_turn(1)
                if n == 12:
                    qk_turn(2)
            dve.wait_ge(m_hi, 9)
            vv.tensor_tensor(hlo[:, 4:8, 0:L], ysc[:], hhi[:, 4:8, 0:L].bitcast(F32), ALU.subtract).then_inc(m_ready, 1)

            dve.wait_ge(c_mask, 16)
            for b in range(2):
                for x in range(8):
                    g = 8 * b + x
                    dve.wait_ge(a_ctx, g + 1)
                    vv.scalar_tensor_tensor(out=sc[:, x, 0:L], in0=ps[x % 4][:, 0:L], scalar=0.125, in1=mask[:, b],
                                            op0=ALU.mult, op1=ALU.add).then_inc(a_loc, 1)
                dve.wait_ge(a_ctx, 8 * b + 8)
                dve.wait_ge(a_loc, 8 * b + 8)
                own.step(vv.tensor_reduce(smax[:], sc[:], AX.X, ALU.max))
                own.step(vv.tensor_tensor(smax[:], smax[:], col("sink", 0, 8), ALU.max))
                vv.tensor_tensor(esink[:], col("sink", 0, 8), smax[:], ALU.subtract)
                vv.tensor_scalar(nmax[:], smax[:], -1.0, None, ALU.mult).then_inc(a_max, 1)
                dve.wait_ge(a_exp, 8 * b + 8)
                own.step(vv.tensor_tensor(sden[:], ssm[:], esink[:], ALU.add))
                own.step(vv.reciprocal(sden[:], sden[:]))
                for x in range(8):
                    vv.tensor_scalar(sc[:, x], sc[:, x], sden[:, x:x + 1], None, ALU.mult).then_inc(a_p, 1)
                dve.wait_ge(m_hi, 10 + b)
                vv.tensor_tensor(hlo[:, 0:4, b * P:(b + 1) * P], ps[6 + b][:].rearrange("p (k c) -> p k c", k=4),
                                 hhi[:, 0:4, b * P:(b + 1) * P].bitcast(F32), ALU.subtract).then_inc(m_ready, 1)

            for n in range(KT):
                residual(n, J_OWOUT + n // 2, 8, omod, L, min(J_OWOUT + n // 2 + 3, J_MOE))
            norm_dve(3, res, sq, rstd, L, omod, 24, full=ht)

            def by_expert(x):
                return x.unsqueeze(2).to_broadcast([P, 2, NEXP, NEXP])

            def by_token(x):
                return x.unsqueeze(2).to_broadcast([P, 2, NEXP])

            dve.wait_ge(c_moe, 64)
            vv.memset(ps[4][:], 0.0).then_inc(e_a, 1)
            vv.memset(ps[5][:], 0.0).then_inc(e_lo, 1)
            dve.wait_ge(r_lg, 1)
            own.step(vv.tensor_tensor(lg[:], ps[6][:, 0:16].rearrange("p (t e) -> p t e", t=2),
                                      col("router_b", 0, 8).unsqueeze(1).to_broadcast([P, 2, NEXP]), ALU.add))
            own.step(vv.tensor_reduce(top[:], lg[:], AX.X, ALU.max))
            vv.tensor_tensor(ex[:], lg[:], by_token(top[:]), ALU.subtract).then_inc(r_sub, 1)
            mine = lg[:].unsqueeze(3).to_broadcast([P, 2, NEXP, NEXP])
            vv.tensor_tensor(gt[:], by_expert(lg[:]), mine, ALU.is_gt)
            own.step(vv.tensor_tensor(eq[:], by_expert(lg[:]), mine, ALU.is_equal))
            own.step(vv.tensor_tensor(eq[:], eq[:], low[:].unsqueeze(1).to_broadcast([P, 2, NEXP, NEXP]), ALU.mult))
            own.step(vv.tensor_tensor(gt[:], gt[:], eq[:], ALU.add))
            own.step(vv.tensor_reduce(rank[:], gt[:], AX.X, ALU.add))
            vv.tensor_scalar(sel[:], rank[:], 2.0, None, ALU.is_lt).then_inc(r_sel, 1)
            dve.wait_ge(r_sel, 1)
            dve.wait_ge(r_exp, 1)
            own.step(vv.tensor_tensor(ex[:], ex[:], sel[:], ALU.mult))
            own.step(vv.tensor_reduce(den[:], ex[:], AX.X, ALU.add))
            own.step(vv.reciprocal(den[:], den[:]))
            own.step(vv.tensor_tensor(ctab[:, :, 0:NEXP], ex[:], by_token(den[:]), ALU.mult))
            dve.wait_ge(r_pos, 1)
            slot = ptab[:, :, 0:NEXP]
            own.step(vv.scalar_tensor_tensor(out=slot, in0=ps[7][:, 0:16].rearrange("p (t e) -> p t e", t=2),
                                             scalar=1.0, in1=sel[:], op0=ALU.add, op1=ALU.mult))
            own.step(vv.tensor_scalar(slot, slot, 1.0, None, ALU.subtract))
            own.step(vv.tensor_scalar(ov[:], ps[7][:, 16:24], float(P), None, ALU.is_gt))
            ovb = ov[:].unsqueeze(1).to_broadcast([P, NEXP, NEXP])
            own.step(vv.tensor_tensor(gt[:, 0], low[:], ovb, ALU.mult))
            own.step(vv.tensor_reduce(ovr[:], gt[:, 0], AX.X, ALU.add))
            for i in range(OVER):
                own.step(vv.scalar_tensor_tensor(out=osel[:], in0=ovr[:], scalar=float(i), in1=ov[:],
                                                 op0=ALU.is_equal, op1=ALU.mult))
                both = osel[:].unsqueeze(1).to_broadcast([P, 2, NEXP])
                own.step(vv.scalar_tensor_tensor(out=obc[:], in0=slot, scalar=float(1 - P), in1=both,
                                                 op0=ALU.add, op1=ALU.mult))
                own.step(vv.tensor_reduce(ptab[:, :, NEXP + i], obc[:], AX.X, ALU.add))
                own.step(vv.tensor_scalar(ptab[:, :, NEXP + i:NEXP + i + 1], ptab[:, :, NEXP + i:NEXP + i + 1],
                                          1.0, None, ALU.subtract))
                own.step(vv.tensor_tensor(obc[:], ctab[:, :, 0:NEXP], both, ALU.mult))
                own.step(vv.tensor_reduce(ctab[:, :, NEXP + i], obc[:], AX.X, ALU.add))
                own.step(vv.tensor_tensor(obc[:, 0], osel[:], enum[:], ALU.mult))
                own.step(vv.tensor_reduce(info[:, 1 + i:2 + i], obc[:, 0], AX.X, ALU.add))
            own.step(vv.memset(ptab[:, :, NTAB - 1:NTAB], -1.0))
            own.step(vv.memset(ctab[:, :, NTAB - 1:NTAB], 0.0))
            own.step(vv.tensor_reduce(info[:, 0:1], ov[:], AX.X, ALU.add))
            vv.tensor_copy(infoi[:], info[:]).then_inc(r_tab, 1)

            def one_hot(turn):
                vv.tensor_copy(cw[:].unsqueeze(2), ctab[:, :, bass.ds(turn, 1)])
                for t in range(2):
                    m = vv.tensor_scalar(hot[:, t], iota[:], ptab[:, t, bass.ds(turn, 1)], None, ALU.is_equal)
                m.then_inc(hot_made, 1)

            dve.wait_ge(c_iota, 16)
            one_hot(0)
            for i in range(4):
                at = slice((i % 2) * 512, (i % 2) * 512 + 512)
                dve.wait_ge(t_hi, i + 1)
                vv.tensor_tensor(hklo[:, i // 2, at], ps[i][:], hkhi[:, i // 2, at].bitcast(F32),
                                 ALU.subtract).then_inc(t_lo, 1)

            def gathered_lo(h, count):
                dve.wait_ge(g_hi, count)
                k = slice(4 * h, 4 * h + 4)
                vv.tensor_tensor(glo[:, k, :], ps[7][:].rearrange("p (k c) -> p k c", k=4), ghi[:, k, :].bitcast(F32),
                                 ALU.subtract).then_inc(misc_free, 1)

            gathered_lo(0, 1)
            gathered_lo(1, 2)
            dve.wait_ge(zeroed, 4)

            def result_lo_part(count):
                for n in range(2):
                    dve.wait_ge(e_yhi, count - 1 + n)
                    m = vv.scalar_tensor_tensor(out=ylo[:, n * CHUNK:(n + 1) * CHUNK], in0=ps[4 + n][:], scalar=wslot[:],
                                                in1=yhi[:, n * CHUNK:(n + 1) * CHUNK].bitcast(F32),
                                                op0=ALU.mult, op1=ALU.subtract)
                m.then_inc(e_y, 1)

            def add_scattered(q, count):
                dve.wait_ge(misc, count)
                vv.tensor_tensor(macc[:, 2 * q:2 * q + 2, :], macc[:, 2 * q:2 * q + 2, :], half(ps[7][:]),
                                 ALU.add).then_inc(misc_free, 1)

            def round_of(r):
                def chunk_lo(c):
                    dve.wait_ge(e_hi, NCH * r + c + 1)
                    vv.tensor_tensor(atlo[:], ps[6][:].rearrange("p (k c) -> p k c", k=4), athi[:].bitcast(F32),
                                     ALU.subtract).then_inc(e_lo, 1)

                for x in range(ROUND_BLOCKS):
                    if x == 3:
                        result_lo_part(2 * r + 2)
                    for c in range(NCH):
                        if x == gate_block(c) + 6:
                            dve.wait_ge(used, r * ROUND_BLOCKS + (J_MOE + gate_block(c) + 4))
                            dve.wait_ge(e_silu, NCH * r + c + 1)
                            vv.tensor_tensor(am[:], sg[:], ps[2 + c % 2][:], ALU.mult).then_inc(e_a, 1)
                        if c < NCH - 1 and x == down_block(c):
                            chunk_lo(c)
                    if x in (6, 12, 18, 24):
                        q = x // 6 - 1
                        add_scattered(q, 7 * r + (3 + q))
                    if x == 31:
                        dve.wait_ge(misc, 7 * r + 7)
                        one_hot(r + 1)
                    if x == 40:
                        gathered_lo(0, 2 * r + 3)
                    split(J_MOE + x, r, ROUND_BLOCKS)
                chunk_lo(NCH - 1)
                gathered_lo(1, 2 * r + 4)

            with dve.Fori(0, NEXP) as r:
                round_of(r)
            crowded = dve.value_load(infoi[0:1, 0:1], min_val=0, max_val=OVER)
            with dve.Fori(NEXP, NEXP + OVER) as r:
                with dve.If(r < crowded + NEXP):
                    round_of(r)
            result_lo_part(crowded * 2 + (2 * NEXP + 2))
            for q in range(4):
                add_scattered(q, crowded * 7 + (7 * NEXP + 3 + q))
            for k in range(KT):
                dve.wait_ge(misc_free, crowded * 7 + (7 * NEXP + 3 + k // 2))
                vv.scalar_tensor_tensor(out=res[:, k, 0:L], in0=macc[:, k], scalar=omod[:, 40 + k, 0:1],
                                        in1=res[:, k, 0:L], op0=ALU.mult, op1=ALU.add).then_inc(y_done, 1)

        @block.gpsimd
        def _(pool):
            gp = nc.gpsimd

            def split(j, turn=0, per=0, n=BLK):
                slot, uses = block_at(j, turn, per)
                if slot != POOL_SLOT:
                    return
                pool.wait_ge(hi_made, turn * per + (j + 1) if per else j + 1)
                gp.tensor_tensor(wlo[:, j % SPLIT, 0:n], raw[:, slot, 0:n], whi[:, j % SPLIT, 0:n].bitcast(F32),
                                 ALU.subtract).then_inc(raw_free[slot], 1)

            done = [0]

            def until(j_end):
                while done[0] < j_end:
                    j = done[0]
                    split(j, n=width_of(j))
                    done[0] += 1

            def sums(n, sqb, s, width):
                for d in range(1, KT):
                    pool.wait_ge(n_sq, 8 * n + d + 1)
                    if d > 1:
                        pool.wait_ge(n_sum, 7 * n + d - 1)
                    first = sqb[:, 0, 0:width] if d == 1 else s[:, 0:width]
                    gp.tensor_tensor(s[:, 0:width], first, sqb[:, d % 2, 0:width], ALU.add).then_inc(n_sum, 1)

            gp.memset(ones[:], 1.0).then_inc(setup, 1)
            gp.memset(eps[:], EPS).then_inc(setup, 1)
            until(6)
            sums(0, sq0, ssum0, T)
            pool.wait_ge(n_ready, KT)
            pool.wait_ge(f_kcopy, 10)
            pool.dma_start(tabs[:], a["c_four"]).then_inc(c_four, 16)
            pool.dma_start(bdft[:], a["c_bdft"]).then_inc(c_four, 16)
            until(J_WOUT)
            pool.wait_ge(m_ps, 2)
            pool.dma_start(tabs[:], a["c_inv"]).then_inc(c_g, 16)
            for i in range(HT):
                pool.wait_ge(x_prod, i + 1)
                gp.tensor_tensor(tmp[:, 0], tmp[:, 0], tmp[:, 1], ALU.subtract)
                gp.tensor_tensor(tmp[:, 2], tmp[:, 2], tmp[:, 3], ALU.add).then_inc(x_spec, 1)
            until(J_WOUT + 3)
            pool.wait_ge(m_ready, 8)
            pool.dma_start(res[:], a["xt"].rearrange("(k p) t -> p k t", p=P)).then_inc(c_res, 16)
            until(J_FFN)
            sums(1, sq, ssum, T)
            pool.wait_ge(m_ready, 8)
            for i in range(4):
                gp.memset(facc[:, 2 * i:2 * i + 2], 0.0).then_inc(ff_added, 1)
            until(J_FFN + 7)
            with pool.Fori(0, FF_PAIRS - 1) as r:
                for x in range(2, 8):
                    split(J_BODY + x, r, 6, width_of(J_BODY + x))
            done[0] = J_TAIL + 2
            until(J_OWIN + 1)
            sums(2, sq, ssum, T)
            pool.wait_ge(res_done, 16)
            gp.memset(kpad[:], 0.0).then_inc(zeroed, 1)
            gp.memset(vpad[:], 0.0).then_inc(zeroed, 1)
            for src, dst in ((a["c_rope"], rope[:]), (a["c_sq"][2], rot[:]), (a["c_sq"][3], bd64[:])):
                pool.dma_start(dst, src).then_inc(c_odd, 16)
            pool.dma_start(mask[:], a["c_mask"]).then_inc(c_mask, 16)
            until(J_MOE)
            sums(3, sq, ssum, L)
            pool.wait_ge(m_ready, 11)
            for src, dst in ((a["c_rw"], rw[:]), (a["c_low"], low[:]), (a["c_enum"], enum[:])):
                pool.dma_start(dst, src).then_inc(c_moe, 16)
            pool.dma_start(tri[:], a["c_tri"]).then_inc(c_moe, 16)
            pool.dma_start(iota[:], a["c_iota"]).then_inc(c_iota, 16)
            gp.memset(hott[:].bitcast(F32), 0.0).then_inc(zeroed, 1)
            gp.memset(wslot[:], 0.0)
            pool.wait_ge(n_ready, 32)
            gp.memset(macc[:], 0.0).then_inc(zeroed, 1)

            def round_of(r):
                for x in range(ROUND_BLOCKS):
                    split(J_MOE + x, r, ROUND_BLOCKS)

            with pool.Fori(0, NEXP) as r:
                round_of(r)
            pool.wait_ge(r_tab, 1)
            crowded = pool.value_load(infoi[0:1, 0:1], min_val=0, max_val=OVER)
            with pool.Fori(NEXP, NEXP + OVER) as r:
                with pool.If(r < crowded + NEXP):
                    round_of(r)


def tables():
    f = np.float64
    t = np.arange(L)
    k = np.arange(L)
    ang = 2 * np.pi * np.outer(t, k) / (2 * L)
    cos, sin = np.cos(ang), -np.sin(ang)
    nyquist = np.cos(np.pi * t)
    sin_n = sin.copy()
    sin_n[:, 0] = nyquist
    cos_n = cos[:, 0:P].copy()
    cos_n[:, 0] = nyquist
    rows = lambda x: np.ascontiguousarray(
        x.reshape(-1, P, x.shape[-1]).transpose(1, 0, 2)).astype(np.float32)
    weight = np.where(k == 0, 1.0, 2.0)[:, None] / (2 * L)
    inv_im = 2 * sin.T / (2 * L)
    inv_im[0] = nyquist / (2 * L)
    ch = np.arange(64)
    blocks = lambda x: np.kron(np.eye(2), x)
    ang64 = 2 * np.pi * np.outer(ch, ch) / 64
    bdft = np.concatenate([blocks(np.cos(ang64)), blocks(np.sin(ang64))], 1) / 8
    angl = 2 * np.pi * np.outer(t, t) / L
    four = np.concatenate([np.cos(angl), -np.sin(angl)], 1) / 16
    f32 = np.float32
    pos = np.linspace(0.0, 1.0, L, dtype=f32)
    bands = 16
    a = f32(2.0 * np.pi / L) * np.arange(L, dtype=f32)[:, None] * np.linspace(1e-4, bands - 1, bands, dtype=f32)[None]
    z = np.concatenate([pos[:, None], np.cos(a), -np.sin(a)], 1)
    deltas = np.abs(np.linspace(np.log(1e-2) / 1.5, np.log(1e-2) / 0.3, HY, dtype=f32))
    decay = np.exp(-pos[:, None] * deltas[None])
    p = np.arange(P) % 64
    place = np.where((p < 32)[:, None], (t // 64)[None], (t % 64)[None]).astype(f32)
    freq = (10000.0 ** (-(p % 16).astype(f32) / 16)).astype(f32)
    turn = place * freq[:, None]
    rope = np.stack([np.cos(turn), np.sin(turn)], 1)
    rot = np.zeros((P, P))
    for i in range(P):
        if i % 32 < 16:
            rot[i + 16, i] = -1.0
        else:
            rot[i - 16, i] = 1.0
    q = np.arange(P)
    mask = np.stack([np.where(np.abs(t[None] - (b * P + q)[:, None]) <= 128, 0.0, -1e30) for b in range(2)], 1)
    tri = np.stack([(q[:, None] < q[None]).astype(f), np.ones((P, P))], 1)
    e = np.arange(NEXP)
    low = np.broadcast_to((e[None, :] < e[:, None]).astype(f), (P, NEXP, NEXP))
    return {
        "c_sq": np.stack([np.eye(P), np.full((P, P), 1.0 / D), rot, blocks(np.full((64, 64), 1.0 / 64))]),
        "c_z": z.T, "c_decay": rows(decay), "c_dft": rows(np.concatenate([cos, sin_n], 1)),
        "c_dft2": rows(np.concatenate([sin[:, 0:P], cos_n], 1)),
        "c_four": rows(four), "c_bdft": bdft,
        "c_inv": rows(np.concatenate([cos.T * weight, inv_im])).reshape(P, 2, 512),
        "c_rope": rope, "c_mask": mask, "c_low": low, "c_enum": np.broadcast_to(e, (P, NEXP)),
        "c_tri": tri, "c_iota": np.broadcast_to(q, (P, P)),
    }


def column_tiles(w):
    n = w.shape[1] // 256
    return w.reshape(KT, P, n, 256).transpose(2, 1, 0, 3).reshape(n, P, BLK)


def by_tiles(w, order, axis):
    tiles = np.split(w, w.shape[axis] // P, axis)
    return np.concatenate([tiles[i] for i in order], axis)


def vectors(x):
    v = np.zeros((P, NVEC), np.float32)

    def put(name, a):
        v[:a.shape[0], VEC[name]] = a

    def cols(a):
        return a.reshape(-1, P).T

    for n in ("e_ada_b", "o_ada_b", "e_norm1", "e_norm2", "o_norm1", "o_norm2"):
        put(n, cols(x[n]))
    put("short", cols(x["e_hy_short"]))
    put("skip", cols(x["e_hy_skip"]))
    put("b1", x["e_hy_b1"].T)
    put("freq", x["e_hy_freq"].T)
    put("b2", x["e_hy_b2"].T)
    put("q_norm", np.concatenate([x["o_q_norm"].T] * 2))
    put("k_norm", np.concatenate([x["o_k_norm"].T] * 2))
    put("sc", cols(x["o_sc_conv"]))
    put("sink", np.broadcast_to(x["o_sink"][:, HEADS], (P, NEXP)))
    put("router_b", np.broadcast_to(x["o_router_b"], (P, NEXP)))
    put("cond", np.stack([cols(x["c"]), cols(x["c_ctx"])], 2).reshape(P, 16))
    return v


def layout(x):
    a = {k: np.ascontiguousarray(v, dtype=np.float32) for k, v in tables().items()}
    a["c_vec"] = vectors(x)
    a["xt"] = np.concatenate([x["x"][0].T, x["ctx"][0].T], 1)
    a["c_w12"] = np.zeros((64, P), np.float32)
    a["c_w12"][0:33, 0:64] = x["e_hy_w1"][0]
    a["c_w12"][:, 64:] = x["e_hy_w2"][0]
    a["c_w3"] = x["e_hy_w3"][0]
    a["w_ada"] = x["e_ada_w"][0].reshape(2, 4, P, ADA // 2, CHUNK).transpose(3, 0, 2, 1, 4).reshape(ADA, P, BLK)
    a["w_in"] = column_tiles(by_tiles(x["e_w_in"][0], WIN_TILES, 1))
    a["w_out"] = column_tiles(x["e_w_out"][0])
    parts = {"gate": column_tiles(x["e_ffn_wg"][0]), "up": column_tiles(x["e_ffn_wu"][0]),
             "down": x["e_ffn_wd"][0].reshape(FF_PAIRS, 2, P, D).transpose(0, 2, 1, 3).reshape(FF_PAIRS, P, BLK)}
    mod = x["o_ada_w"][0].reshape(KT, P, ADA // 2, CHUNK).transpose(2, 1, 0, 3)
    for kind, k in MOD_TILES.items():
        parts[kind] = np.zeros((ADA // 2, P, BLK), np.float32)
        parts[kind][:, :, 0:len(k) * CHUNK] = mod[:, :, k.start:k.stop].reshape(ADA // 2, P, -1)
    a["w_ffn"] = np.stack([parts[kind][FFN_KINDS[:j].count(kind)] for j, kind in enumerate(FFN_KINDS)])
    w = x["o_w_in"][0]
    heads = np.split(w[:, 0:512], 8, 1)
    w = np.concatenate([heads[h] for h in HEADS] + [w[:, 512:]], 1)
    a["w_oin"] = column_tiles(by_tiles(w, OWIN_TILES, 1))
    w = x["o_w_out"][0]
    heads = np.split(w[0:512], 8, 0)
    a["w_oout"] = column_tiles(np.concatenate([heads[h] for h in HEADS] + [w[512:]], 0))
    gate, up = (x[n][0].reshape(NEXP, 2, 4, P, NCH, CHUNK).transpose(4, 0, 1, 3, 2, 5)
                for n in ("o_moe_wg", "o_moe_wu"))
    down = x["o_moe_wd"][0].reshape(NEXP, NCH, 2, 2, P, D).transpose(1, 0, 2, 4, 3, 5)
    moe = np.empty((NEXP, ROUND_BLOCKS, P, BLK), np.float32)
    for c in range(NCH):
        g = gate_block(c)
        moe[:, g:g + 2] = gate[c].reshape(NEXP, 2, P, BLK)
        moe[:, g + 2:g + 4] = up[c].reshape(NEXP, 2, P, BLK)
        d = down_block(c)
        moe[:, d:d + 2] = down[c].reshape(NEXP, 2, P, BLK)
    a["w_moe"] = moe.reshape(NEXP * ROUND_BLOCKS, P, BLK)
    a["c_rw"] = x["o_router_w"][0].reshape(KT, P, NEXP).transpose(1, 0, 2)
    return a


def kernel(**inputs):
    import concourse.bacc as bacc
    from concourse.bass_utils import run_bass_kernel_spmd

    arrays = {n: np.ascontiguousarray(v) for n, v in layout({n: np.asarray(v) for n, v in inputs.items()}).items()}
    nc = bacc.Bacc("TRN2", target_bir_lowering=False, num_devices=1)
    a = {n: nc.dram_tensor(n, v.shape, F32, kind="ExternalInput").ap() for n, v in arrays.items()}
    out = nc.dram_tensor("out", (D, L), F32, kind="ExternalOutput").ap()
    build(nc, a, out)
    r = run_bass_kernel_spmd(nc, [arrays], core_ids=[0])
    return np.ascontiguousarray(r.results[0]["out"].T)[None]
```

```python
from contextlib import ExitStack

import numpy as np
import concourse.bass as bass
from concourse import mybir

F32 = mybir.dt.float32
F32R = mybir.dt.float32r
I32 = mybir.dt.int32
ACT = mybir.ActivationFunctionType
ALU = mybir.AluOpType
AX = mybir.AxisListType

P = 128
D = 1024
KT = D // P
L = 256
T = 2 * L
EPS = 1e-6
HY = 768
HT = HY // P
HALF = HY // 2
FF_PAIRS = 2816 // 256
NEXP = 8
CHUNK = 512
NCH = 3584 // CHUNK
ROUND_BLOCKS = 6 * NCH
OVER = 3
NTAB = NEXP + OVER + 1

RAW = 6
SPLIT = 3
BLK = 2048
POOL_SLOT = 5

ADA, WIN, WOUT = 24, 10, 4
EARLY = 4
LATE = EARLY + WIN // 2
OWIN, OWOUT = 9, 4
FFN_BODY = ["gate", "mod0", "down", "mod1", "up", "mod2"]
FFN_KINDS = ["gate", "up", "mod0", "mod1", "mod2"] + (FF_PAIRS - 1) * FFN_BODY + ["down", "mod0", "mod1", "mod2"]
MOD_TILES = {"mod0": range(0, 3), "mod1": range(3, 6), "mod2": range(6, 8)}
J_LATE = 2 * LATE + WIN
J_FFN = ADA + WIN + WOUT
J_BODY = J_FFN + 5
J_TAIL = J_BODY + 6 * (FF_PAIRS - 1)
J_OWIN = J_FFN + len(FFN_KINDS)
J_OWOUT = J_OWIN + OWIN
J_MOE = J_OWOUT + OWOUT

WIN_TILES = [18, 19] + [s + 2 * i + a for i in range(3) for s in (6, 12, 0) for a in range(2)]
OWIN_TILES = [4, 5, 0, 1, 2, 3] + [6 + s + i for i in range(4) for s in (4, 8, 0)]

VEC = {}


def _columns():
    at = 0
    for name, n in (("e_ada_b", 48), ("o_ada_b", 48), ("e_norm1", 8), ("e_norm2", 8), ("o_norm1", 8),
                    ("o_norm2", 8), ("short", 54), ("skip", 6), ("b1", 1), ("freq", 1), ("b2", 1),
                    ("q_norm", 1), ("k_norm", 1), ("sc", 12), ("sink", 8), ("router_b", 8), ("cond", 16)):
        VEC[name] = slice(at, at + n)
        at += n
    return at


NVEC = _columns()


HEADS = [h for i in range(4) for h in (i, i + 4)]

ROUND = 1.5 * 2 ** 23
TURN = (6.28125, float(2 * np.pi - 6.28125))


def gate_block(c):
    return 6 * c - 2 if c else 0


def down_block(c):
    return 6 * c + 8 if c < NCH - 1 else ROUND_BLOCKS - 2


class Steps:

    def __init__(self, engine, sem):
        self.engine, self.sem, self.n = engine, sem, 0

    def step(self, instruction):
        instruction.then_inc(self.sem, 1)
        self.n += 1
        self.engine.wait_ge(self.sem, self.n)


def win_at(b):
    return 2 * EARLY + 2 * b


def ada_at(i):
    if i < 2 * EARLY:
        return i
    if i < 2 * LATE:
        return win_at(i - 2 * EARLY) + 1
    return J_LATE + (0, 1, 2, 3, 7, 9)[i - 2 * LATE]


def wout_at(b):
    return J_LATE + (4, 5, 6, 8)[b]


def width_of(j):
    kind = FFN_KINDS[j - J_FFN] if J_FFN <= j < J_OWIN else ""
    return len(MOD_TILES[kind]) * CHUNK if kind in MOD_TILES else BLK


def block_at(j, turn=0, per=0):
    uses = j // RAW + 1
    return j % RAW, (uses + turn * (per // RAW) if per else uses)


def build(nc, a, out):
    ctx = ExitStack()
    with ctx:
        def sb(name, shape, dt=F32, where=ctx):
            return where.enter_context(nc.sbuf_tensor(name, shape, dt))

        def sem(name):
            return ctx.enter_context(nc.semaphore(name))

        raw = sb("raw", [P, RAW, BLK])
        whi = sb("whi", [P, SPLIT, BLK], F32R)
        wlo = sb("wlo", [P, SPLIT, BLK], F32R)
        hhi = sb("hhi", [P, KT, T], F32R)
        hlo = sb("hlo", [P, KT, T], F32R)
        vec = sb("vec", [P, NVEC])
        ident = sb("ident", [P, P])
        mean = sb("mean", [P, P])
        emod = sb("emod", [P, 48, 2])
        omod = sb("omod", [P, 48, 2])
        gain = sb("gain", [P, 4, KT, 2])
        scond = sb("scond", [P, KT, 2])
        sc4 = sb("sc4", [P, KT, 4], F32R)
        rows = sb("rows", [4, 2, CHUNK])
        pick = sb("pick", [4, 2])
        eps = sb("eps", [P, 1])
        idle = sb("idle", [P, 1])
        ones = sb("ones", [P, 1])
        il1 = sb("il1", [P, HT])

        even = ExitStack()
        kf = sb("kf", [P, 5, HY], where=even)
        bdft = sb("bdft", [P, 256], where=even)
        dft = sb("dft", [P, 2, 512], where=even)
        start = ExitStack()
        xin = sb("xin", [P, KT, T], where=start)
        dft2 = sb("dft2", [P, 2, 256], where=start)
        decay = sb("decay", [P, 2, HY], where=start)
        hf = sb("hf", [P, 2, HALF], where=start)
        hb = sb("hb", [P, 2, HALF], where=start)
        hs = sb("hs", [P, 2, HALF], where=start)
        hd = sb("hd", [P, 2, HALF], where=start)
        w3 = sb("w3", [64, 2 * HY], where=start)
        w12 = sb("w12", [64, 128], where=start)
        zt = sb("zt", [33, L], where=start)
        sred = sb("sred", [64, L], where=start)
        sq0 = sb("sq0", [P, 2, T], where=start)
        ssum0 = sb("ssum0", [P, T], where=start)
        rstd0 = sb("rstd0", [P, T], where=start)
        sarg = ssum0[0:64, 0:L]
        start.close()
        x0c = sb("x0c", [P, HT, T], where=even)
        u = sb("u", [P, HT, T], where=even)
        fwhi = sb("fwhi", [P, 2, 512], F32R, where=even)
        fwlo = sb("fwlo", [P, 2, 512], F32R, where=even)
        invhi = sb("invhi", [P, 2, 512], F32R, where=even)
        invlo = sb("invlo", [P, 2, 512], F32R, where=even)
        fnt = sb("fnt", [P, 2, T], where=even)
        tmp = sb("tmp", [P, 4, T], where=even)
        even.close()

        res = sb("res", [P, KT, T])
        norm = ExitStack()
        sq = sb("sq", [P, 2, T], where=norm)
        ssum = sb("ssum", [P, T], where=norm)
        rstd = sb("rstd", [P, T], where=norm)
        ffn = ExitStack()
        facc = sb("facc", [P, KT, T], where=ffn)
        ahi = sb("ahi", [P, 2, T], F32R, where=ffn)
        alo = sb("alo", [P, 2, T], F32R, where=ffn)
        sil = sb("sil", [P, 2, T], where=ffn)
        ffn.close()
        odd = ExitStack()
        qt = sb("qt", [P, 4, L], where=odd)
        kpad = sb("kpad", [P, 2, T], where=odd)
        vpad = sb("vpad", [P, 4, 2, P], where=odd)
        ysc = sb("ysc", [P, 4, L], where=odd)
        mask = sb("mask", [P, 2, L], where=odd)
        smax = sb("smax", [P, 8], where=odd)
        nmax = sb("nmax", [P, 8], where=odd)
        ssm = sb("ssm", [P, 8], where=odd)
        esink = sb("esink", [P, 8], where=odd)
        sden = sb("sden", [P, 8], where=odd)
        mix = ExitStack()
        qraw = sb("qraw", [P, 3, T], where=mix)
        qsq = sb("qsq", [P, 3, T], where=mix)
        qn = sb("qn", [P, 3, T], where=mix)
        rr = sb("rr", [P, T], where=mix)
        ra = sb("ra", [P, L], where=mix)
        rb = sb("rb", [P, L], where=mix)
        vt = sb("vt", [P, T], where=mix)
        gcs = sb("gcs", [P, L], where=mix)
        gm = sb("gm", [P, L], where=mix)
        gcv = sb("gcv", [P, L], where=mix)
        rope = sb("rope", [P, 2, L], where=mix)
        rot = sb("rot", [P, P], where=mix)
        bd64 = sb("bd64", [P, P], where=mix)
        mix.close()
        sc = sb("sc", [P, 8, T], where=odd)
        pt = sb("pt", [P, 2, 4, P], where=odd)
        odd.close()
        norm.close()
        macc = sb("macc", [P, KT, L])
        route = ExitStack()
        ht = sb("ht", [P, KT, L], where=route)
        route.close()
        yhi = sb("yhi", [P, D], F32R)
        ylo = sb("ylo", [P, D], F32R)
        hkhi = sb("hkhi", [P, 2, D], F32R)
        hklo = sb("hklo", [P, 2, D], F32R)
        rw = sb("rw", [P, KT, NEXP])
        lg = sb("lg", [P, 2, NEXP])
        gt = sb("gt", [P, 2, NEXP, NEXP])
        eq = sb("eq", [P, 2, NEXP, NEXP])
        low = sb("low", [P, NEXP, NEXP])
        rank = sb("rank", [P, 2, NEXP])
        sel = sb("sel", [P, 2, NEXP])
        top = sb("top", [P, 2])
        ex = sb("ex", [P, 2, NEXP])
        den = sb("den", [P, 2])
        ov = sb("ov", [P, NEXP])
        ovr = sb("ovr", [P, NEXP])
        osel = sb("osel", [P, NEXP])
        obc = sb("obc", [P, 2, NEXP])
        enum = sb("enum", [P, NEXP])
        info = sb("info", [P, 4])
        infoi = sb("infoi", [P, 4], I32)
        tri = sb("tri", [P, 2, P])
        iota = sb("iota", [P, P])
        ptab = sb("ptab", [P, 2, NTAB])
        ctab = sb("ctab", [P, 2, NTAB])
        cw = sb("cw", [P, 2])
        hot = sb("hot", [P, 2, P], F32R)
        hott = sb("hott", [P, L], F32R)
        wslot = sb("wslot", [P, 1])
        ghi = sb("ghi", [P, KT, P], F32R)
        glo = sb("glo", [P, KT, P], F32R)
        sg = sb("sg", [P, CHUNK])
        am = sb("am", [P, CHUNK])
        athi = sb("athi", [P, 4, P], F32R)
        atlo = sb("atlo", [P, 4, P], F32R)
        ps = [ctx.enter_context(nc.psum_tensor(f"ps{i}", [P, 512], F32)) for i in range(8)]

        raw_loaded = [sem(f"raw_loaded{i}") for i in range(RAW)]
        raw_free = [sem(f"raw_free{i}") for i in range(RAW)]
        hi_made = sem("hi_made")
        used = sem("used")
        c_vec = sem("c_vec")
        c_net = sem("c_net")
        c_even = sem("c_even")
        c_x = sem("c_x")
        c_filt = sem("c_filt")
        c_four = sem("c_four")
        c_g = sem("c_g")
        c_res = sem("c_res")
        c_odd = sem("c_odd")
        c_mask = sem("c_mask")
        c_moe = sem("c_moe")
        c_iota = sem("c_iota")
        setup = sem("setup")
        zeroed = sem("zeroed")
        pick_made = sem("pick_made")
        silu_c = sem("silu_c")
        f_ps = sem("f_ps")
        f_arg = sem("f_arg")
        f_sin = sem("f_sin")
        f_taps = sem("f_taps")
        f_abs = sem("f_abs")
        f_k = sem("f_k")
        f_kcopy = sem("f_kcopy")
        f_l1 = sem("f_l1")
        n_sq = sem("n_sq")
        n_sum = sem("n_sum")
        n_mean = sem("n_mean")
        n_root = sem("n_root")
        n_h = sem("n_h")
        n_hi = sem("n_hi")
        n_ready = sem("n_ready")
        w_ps = sem("w_ps")
        w_mid = sem("w_mid")
        w_free = sem("w_free")
        u_made = sem("u_made")
        ut_ps = sem("ut_ps")
        ut_hi = sem("ut_hi")
        ut_lo = sem("ut_lo")
        tab_hi = sem("tab_hi")
        tab_lo = sem("tab_lo")
        fn_ab = sem("fn_ab")
        fn_abc = sem("fn_abc")
        m_ps = sem("m_ps")
        m_z = sem("m_z")
        m_hi = sem("m_hi")
        m_ready = sem("m_ready")
        x_ps = sem("x_ps")
        x_prod = sem("x_prod")
        x_im = sem("x_im")
        x_re_sum = sem("x_re_sum")
        x_im_sum = sem("x_im_sum")
        x_re_hi = sem("x_re_hi")
        x_im_hi = sem("x_im_hi")
        x_re_lo = sem("x_re_lo")
        x_im_lo = sem("x_im_lo")
        skips = sem("skips")
        o_ps = sem("o_ps")
        res_done = sem("res_done")
        act_s = sem("act_s")
        rows_made = sem("rows_made")
        cols_made = sem("cols_made")
        emod_made = sem("emod_made")
        oa_read = sem("oa_read")
        ff_in = sem("ff_in")
        ff_silu = sem("ff_silu")
        ff_a = sem("ff_a")
        ff_hi = sem("ff_hi")
        ff_lo = sem("ff_lo")
        ff_d = sem("ff_d")
        ff_added = sem("ff_added")
        q_ps = sem("q_ps")
        q_sq = sem("q_sq")
        q_raw = sem("q_raw")
        q_ms = sem("q_ms")
        q_root = sem("q_root")
        q_n = sem("q_n")
        q_rot = sem("q_rot")
        q_done = sem("q_done")
        v_copy = sem("v_copy")
        v_ps = sem("v_ps")
        v_done = sem("v_done")
        s_gc = sem("s_gc")
        s_hx = sem("s_hx")
        s_y = sem("s_y")
        a_s = sem("a_s")
        a_ctx = sem("a_ctx")
        a_loc = sem("a_loc")
        a_max = sem("a_max")
        a_sink = sem("a_sink")
        a_exp = sem("a_exp")
        a_p = sem("a_p")
        a_t = sem("a_t")
        a_tc = sem("a_tc")
        a_o = sem("a_o")
        r_lg = sem("r_lg")
        r_sub = sem("r_sub")
        r_exp = sem("r_exp")
        r_sel = sem("r_sel")
        r_pos = sem("r_pos")
        r_tab = sem("r_tab")
        t_ps = sem("t_ps")
        t_hi = sem("t_hi")
        t_lo = sem("t_lo")
        misc = sem("misc")
        misc_free = sem("misc_free")
        hot_made = sem("hot_made")
        g_hi = sem("g_hi")
        e_silu = sem("e_silu")
        e_a = sem("e_a")
        e_t = sem("e_t")
        e_hi = sem("e_hi")
        e_lo = sem("e_lo")
        e_yhi = sem("e_yhi")
        e_y = sem("e_y")
        y_done = sem("y_done")
        stored = sem("stored")
        dve_s = sem("dve_s")

        block = ctx.enter_context(nc.Block())

        def oin_free(n):
            if n < 6:
                return (v_copy, 1) if n == 1 else (q_raw, max(n, 1))
            return (s_gc, s_hx, s_y)[(n - 6) % 3], (n - 6) // 3 + 1

        def col(name, i=0, n=1):
            at = VEC[name].start + i
            return vec[:, at:at + n]

        def half(ap):
            return ap.rearrange("p (s t) -> p s t", s=2)

        @block.sync
        def _(sp):
            def load(slot, uses, src, n=BLK):
                if not (isinstance(uses, int) and uses == 1):
                    sp.wait_ge(raw_free[slot], uses - 1)
                sp.dma_start(raw[:, slot, 0:n], src).then_inc(raw_loaded[slot], 16)

            def at(src, i):
                return src[bass.ds(i, 1)].rearrange("a p n -> p (a n)")

            for j in range(2 * EARLY):
                load(*block_at(j), a["w_ada"][j])
            for b in range(WIN):
                load(*block_at(win_at(b)), a["w_in"][b])
                load(*block_at(win_at(b) + 1), a["w_ada"][2 * EARLY + b])
            blocks = [(ada_at(i), a["w_ada"][i]) for i in range(2 * LATE, ADA)]
            blocks += [(wout_at(b), a["w_out"][b]) for b in range(WOUT)]
            for j, src in sorted(blocks, key=lambda block: block[0]):
                load(*block_at(j), src)

            def load_ffn(j, src, turn=0, per=0):
                n = width_of(j)
                load(*block_at(j, turn, per), src[:, 0:n], n)

            for j in range(J_FFN, J_BODY):
                load_ffn(j, a["w_ffn"][j - J_FFN])
            with sp.Fori(0, FF_PAIRS - 1) as r:
                for x in range(6):
                    load_ffn(J_BODY + x, at(a["w_ffn"], r * 6 + (J_BODY - J_FFN + x)), r, 6)
            for j in range(J_TAIL, J_OWIN):
                load_ffn(j, a["w_ffn"][j - J_FFN])
            for j in range(OWIN):
                load(*block_at(J_OWIN + j), a["w_oin"][j])
            for j in range(OWOUT):
                load(*block_at(J_OWOUT + j), a["w_oout"][j])

            def round_of(r, expert):
                for i in range(ROUND_BLOCKS):
                    load(*block_at(J_MOE + i, r, ROUND_BLOCKS), at(a["w_moe"], expert * ROUND_BLOCKS + i))

            with sp.Fori(0, NEXP) as r:
                round_of(r, r)
            sp.wait_ge(r_tab, 1)
            crowded = sp.value_load(infoi[0:1, 0:1], min_val=0, max_val=OVER)
            with sp.Fori(NEXP, NEXP + OVER) as r:
                with sp.If(r < crowded + NEXP):
                    round_of(r, sp.value_load(infoi[0:1, bass.ds(r - (NEXP - 1), 1)], min_val=0, max_val=NEXP - 1))
            load(*block_at(J_MOE, crowded + NEXP, ROUND_BLOCKS), a["w_moe"][0])
            result = out.rearrange("(k p) t -> p k t", p=P)
            for n in range(2):
                k = slice(n * KT // 2, (n + 1) * KT // 2)
                sp.wait_ge(y_done, (n + 1) * KT // 2)
                sp.dma_start(result[:, k], res[:, k, 0:L]).then_inc(stored, 16)
            sp.wait_ge(stored, 32)

        @block.tensor
        def _(pe):
            mm = nc.tensor.matmul

            def wait_block(j, turn=0, per=0):
                slot, uses = block_at(j, turn, per)
                pe.wait_ge(raw_free[slot], uses)

            def three(dst, w, x, start, stop):
                mm(dst, w[0], x[0], start=start, stop=False)
                mm(dst, w[0], x[1], start=False, stop=False)
                return mm(dst, w[1], x[0], start=False, stop=stop)

            def hidden(k, n):
                return hhi[:, k, 0:n], hlo[:, k, 0:n]

            def weights(j, at):
                return whi[:, j % SPLIT, at:at + P], wlo[:, j % SPLIT, at:at + P]

            def modulation(j, tiles, bank, turn=0, per=0):
                wait_block(j, turn, per)
                for i, k in enumerate(tiles):
                    at = slice(i * CHUNK, (i + 1) * CHUNK)
                    mm(ps[bank][0:4, :], sc4[:, k, :], whi[:, j % SPLIT, at], start=(k == 0), stop=False)
                    m = mm(ps[bank][0:4, :], sc4[:, k, :], wlo[:, j % SPLIT, at], start=False, stop=(k == KT - 1))
                m.then_inc(used, 1)

            def even_modulation(i):
                c, h = i // 2, i % 2
                if c and h == 0:
                    pe.wait_ge(rows_made, c)
                modulation(ada_at(i), range(4 * h, 4 * h + 4), 6)

            def to_columns(bank, at, buf, made):
                pe.wait_ge(rows_made, made)
                for q in range(4):
                    m = mm(ps[bank][:, at + 2 * q:at + 2 * q + 2], rows[:, buf, q * P:(q + 1) * P], pick[:],
                           start=True, stop=True)
                m.then_inc(cols_made, 1)

            def even_columns(c):
                if c == 0:
                    pe.wait_ge(pick_made, 1)
                to_columns(7, 8 * c, c % 2, c + 1)

            def filter_taps(h):
                pe.wait_ge(f_sin, 2)
                if h:
                    pe.wait_ge(f_taps, 1)
                for t in range(2):
                    for side in range(2):
                        m = mm(ps[2 * side + t][:, 0:HALF], sred[:, t * P:(t + 1) * P],
                               w3[:, side * HY + h * HALF:side * HY + (h + 1) * HALF], start=True, stop=True)
                m.then_inc(f_ps, 1)

            def filter_spectrum(h, also=None):
                pe.wait_ge(f_taps, h + 1)
                tiles = ((dft, 0, hs), (dft2, P, hs), (dft, P, hs), (dft2, 0, hd), (dft, 3 * P, hd))
                for m_, (table, at, src) in enumerate(tiles):
                    n = 5 * h + m_
                    if n >= 2:
                        pe.wait_ge(f_kcopy, n - 1)
                    for k in range(2):
                        m = mm(ps[4 + n % 2][:, 0:HALF], table[:, k, at:at + P], src[:, k, :],
                               start=(k == 0), stop=(k == 1))
                    m.then_inc(f_k, 1)
                    if also and m_ == 1:
                        also()
                pe.wait_ge(f_abs, h + 1)
                pe.wait_ge(emod_made, 1)
                for c in range(3):
                    for i, src in enumerate((hf, hf, hb, hb)):
                        at = 4 * ADA + 3 * h + c
                        m = mm(ps[7][:, at:at + 1], src[:, i % 2, c * P:(c + 1) * P], ones[:],
                               start=(i == 0), stop=(i == 3))
                m.then_inc(f_l1, 1)

            pe.wait_ge(c_net, 16 * 2)
            mm(ps[0][0:64, 0:L], w12[0:33, 0:64], zt[:], start=True, stop=True).then_inc(f_ps, 1)
            pe.wait_ge(silu_c, 1)
            for i in (0, 1):
                even_modulation(i)
            pe.wait_ge(f_sin, 1)
            mm(ps[1][0:64, 0:L], w12[0:64, 64:128], sred[:], start=True, stop=True).then_inc(f_ps, 1)
            for i in (2, 3):
                even_modulation(i)
            even_columns(0)
            pe.wait_ge(c_filt, 16 * 4)
            filter_taps(0)
            for i in (4, 5):
                even_modulation(i)
            even_columns(1)
            for i in (6, 7):
                even_modulation(i)
            even_columns(2)
            even_columns(3)

            def norm_mean(n, s, width):
                pe.wait_ge(n_sum, 7 * n + 7)
                mm(ps[5 if n == 1 else 6][:, 0:width], mean[:], s[:, 0:width], start=True, stop=True).then_inc(n_mean, 1)


            def between():
                filter_taps(1)
                norm_mean(0, ssum0, T)

            filter_spectrum(0, also=between)
            filter_spectrum(1)

            def transpose_u(c):
                if c == 0:
                    pe.wait_ge(u_made, HT)
                if c >= 2:
                    pe.wait_ge(ut_lo, c - 1)
                for s in range(4):
                    m = nc.tensor.transpose(ps[4 + c % 2][:, s * P:(s + 1) * P], u[:, c, s * P:(s + 1) * P], ident[:])
                m.then_inc(ut_ps, 1)

            for n in range(2 * WIN):
                j, q = n // 2, n % 2
                if q == 0:
                    wait_block(win_at(j))
                if n >= 4:
                    pe.wait_ge(w_free, n - 3)
                for k in range(KT):
                    if n == 0:
                        pe.wait_ge(n_ready, k + 1)
                    m = three(ps[n % 4][:], weights(win_at(j), k * 256 + q * P), hidden(k, T), k == 0, k == KT - 1)
                m.then_inc(used if q else w_ps, 1)
                if q:
                    even_modulation(2 * EARLY + j)
                    if j >= 2 and j % 2 == 0:
                        even_columns(EARLY + j // 2 - 1)

            def forward(i):
                pe.wait_ge(ut_lo, i + 1)
                if i == 0:
                    pe.wait_ge(tab_lo, 1)
                if i >= 2:
                    pe.wait_ge(x_prod, i - 1)
                hi, lo = (x[:, i].rearrange("p (s k c) -> p s k c", s=2, k=2) for x in (hhi, hlo))
                for part in range(4):
                    at = slice(part * P, (part + 1) * P)
                    for k in range(2):
                        m = three(half(ps[2 * (i % 2) + part // 2][:, (part % 2) * 256:(part % 2) * 256 + 256]),
                                  (fwhi[:, k, at], fwlo[:, k, at]), (hi[:, :, k, :], lo[:, :, k, :]),
                                  k == 0, k == 1)
                m.then_inc(x_ps, 1)

            inverse = [x[:].rearrange("p a (b n) -> p (a b) n", b=2) for x in (invhi, invlo)]

            def backward(i):
                if i == 0:
                    pe.wait_ge(tab_lo, 2)
                    pe.wait_ge(ut_lo, HT)
                else:
                    pe.wait_ge(m_z, i - 1) if i >= 2 else None
                pe.wait_ge(x_im_lo, i + 1)
                pe.wait_ge(x_re_lo, i + 1)
                for s in range(2):
                    for n, part in enumerate((2, 3, 0, 1)):
                        spec = [x[:, HT + part // 2].rearrange("p (m s c) -> p m s c", m=2, s=2)[:, part % 2, s, :]
                                for x in (hhi, hlo)]
                        m = three(ps[4 + i % 2][:, s * L:(s + 1) * L], spec, [x[:, part, :] for x in inverse],
                                  n == 0, n == 3)
                m.then_inc(m_ps, 1)

            def fourier_channels(q):
                if q == 0:
                    pe.wait_ge(c_four, 32)
                pe.wait_ge(x_prod, HT - 1 + q)
                for s in range(4):
                    m = mm(ps[2 * q + s // 2][:, (s % 2) * 256:(s % 2) * 256 + 256], fnt[:, q, s * P:(s + 1) * P],
                           bdft[:], start=True, stop=True)
                m.then_inc(fn_ab, 1)

            def fourier_tokens(q):
                pe.wait_ge(m_z, HT - 1 + q)
                pe.wait_ge(fn_abc, q + 1)
                ab = tmp[:, 2 * q:2 * q + 2, :].rearrange("p a (b n) -> p (a b) n", b=2)
                for s in range(2):
                    for i in range(4):
                        k, part = i // 2, i % 2
                        m = mm(ps[4 + q][:, s * L:(s + 1) * L], ab[:, 2 * s + k, part * P:(part + 1) * P],
                               dft[:, k, part * L:(part + 1) * L], start=(i == 0), stop=(i == 3))
                m.then_inc(m_ps, 1)

            transpose_u(0)
            transpose_u(1)
            forward(0)
            transpose_u(2)
            transpose_u(3)
            forward(1)
            transpose_u(4)
            transpose_u(5)
            for i in range(HT):
                if 1 <= i < HT - 1:
                    forward(i + 1)
                if i == HT - 1:
                    fourier_channels(0)
                    fourier_channels(1)
                backward(i)
                if i < 4:
                    even_modulation(2 * LATE + i)
                if i in (0, 2, 4):
                    if i == 0:
                        pe.wait_ge(emod_made, 2)
                    even_columns(LATE - 1 + i // 2)
            fourier_tokens(0)
            fourier_tokens(1)

            def four_tiles(blocks, order, widths, ready, done):
                for j in blocks:
                    wait_block(j)
                for i, k in enumerate(order):
                    pe.wait_ge(ready[0], ready[1][i])
                    for n in range(4):
                        m = three(ps[n][:, 0:widths[n]], weights(blocks[n // 2], k * 256 + n % 2 * P),
                                  hidden(k, widths[n]), i == 0, i == KT - 1)
                        if i == KT - 1:
                            m.then_inc(used if n % 2 else done, 1)

            def project_out(blocks, order, width, base, ready, between=None):
                four_tiles(blocks[0:2], order, 4 * (width,), (m_ready, ready), o_ps)
                for n in range(4, KT):
                    j, q = blocks[n // 2], n % 2
                    if q == 0:
                        if between and n == KT - 2:
                            between()
                        wait_block(j)
                    pe.wait_ge(res_done, base + n - 3)
                    for i, k in enumerate(order):
                        m = three(ps[n % 4][:, 0:width], weights(j, k * 256 + q * P), hidden(k, width),
                                  i == 0, i == KT - 1)
                    m.then_inc(used if q else o_ps, 1)

            project_out([wout_at(b) for b in range(WOUT)], range(KT), T, 0, range(1, 9),
                        between=lambda: even_modulation(ADA - 2))
            even_modulation(ADA - 1)
            norm_mean(1, ssum, T)
            pe.wait_ge(emod_made, 3)
            even_columns(ADA // 2 - 1)

            def ffn_in(j, bank, free, turn, pair, per):
                wait_block(j, turn, per)
                pe.wait_ge(free, 2 * pair)
                for q in range(2):
                    for k in range(KT):
                        m = three(ps[bank + q][:], weights(j, k * 256 + q * P), hidden(k, T), k == 0, k == KT - 1)
                m.then_inc(used, 1)

            def ffn_down(j, turn, pair, per):
                wait_block(j, turn, per)
                pe.wait_ge(ff_lo, 2 * pair + 2)
                for d in range(KT):
                    if d == 2:
                        pe.wait_ge(oa_read, pair + 1)
                    pe.wait_ge(ff_added, 8 * pair + (d + 2 if d >= 3 else 4))
                    three(ps[4 + d % 3][:], weights(j, d * P), (ahi[:, 0], alo[:, 0]), True, False)
                    m = three(ps[4 + d % 3][:], weights(j, D + d * P), (ahi[:, 1], alo[:, 1]), False, True)
                    m.then_inc(used if d == KT - 1 else ff_d, 1)

            def odd_columns(pair):
                pe.wait_ge(ff_added, 8 * pair + 4)
                to_columns(6, 0, 0, pair + (ADA // 2 + 1))

            def odd_modulation(j, kind, turn=0, per=0):
                modulation(j, MOD_TILES[kind], 7, turn, per)

            four_tiles((J_FFN, J_FFN + 1), range(KT), 4 * (T,), (n_ready, range(9, 17)), ff_in)
            pe.wait_ge(emod_made, 4)
            odd_modulation(J_FFN + 2, "mod0")
            odd_modulation(J_FFN + 3, "mod1")
            odd_modulation(J_FFN + 4, "mod2")
            with pe.Fori(0, FF_PAIRS - 1) as r:
                ffn_in(J_BODY, 0, ff_silu, r, r + 1, 6)
                odd_columns(r)
                odd_modulation(J_BODY + 1, "mod0", r, 6)
                ffn_down(J_BODY + 2, r, r, 6)
                odd_modulation(J_BODY + 3, "mod1", r, 6)
                ffn_in(J_BODY + 4, 2, ff_a, r, r + 1, 6)
                odd_modulation(J_BODY + 5, "mod2", r, 6)
            odd_columns(FF_PAIRS - 1)
            ffn_down(J_TAIL, 0, FF_PAIRS - 1, 0)
            odd_modulation(J_TAIL + 1, "mod0")
            odd_modulation(J_TAIL + 2, "mod1")
            odd_modulation(J_TAIL + 3, "mod2")
            pe.wait_ge(ff_added, 8 * FF_PAIRS + 4)
            norm_mean(2, ssum, T)
            to_columns(5, 0, 0, FF_PAIRS + (ADA // 2 + 1))

            def qk_square(y):
                pe.wait_ge(q_sq, 1 if y == 0 else 1 + 2 * y)
                if y == 0:
                    pe.wait_ge(c_odd, 48)
                if y == 1:
                    pe.wait_ge(v_done, 1)
                if y == 2:
                    pe.wait_ge(q_root, 1)
                mm(ps[4 + y % 2][:], bd64[:], qsq[:, y], start=True, stop=True).then_inc(q_ms, 1)

            def qk_rotate(y):
                pe.wait_ge(q_n, y + 1)
                if y == 2:
                    pe.wait_ge(q_done, 1)
                mm(ps[6 + y % 2][:], rot[:], qn[:, y], start=True, stop=True).then_inc(q_rot, 1)

            def transpose_v():
                pe.wait_ge(v_copy, 1)
                for s in range(4):
                    m = nc.tensor.transpose(ps[5][:, s * P:(s + 1) * P], vt[:, s * P:(s + 1) * P], ident[:])
                m.then_inc(v_ps, 1)

            four_tiles((J_OWIN, J_OWIN + 1), range(KT), (T, T, L, L), (n_ready, range(17, 25)), q_ps)
            for n in range(4, 2 * OWIN):
                j, q = n // 2, n % 2
                if q == 0:
                    wait_block(J_OWIN + j)
                pe.wait_ge(*oin_free(n - 4))
                for k in range(KT):
                    m = three(ps[n % 4][:, 0:L], weights(J_OWIN + j, k * 256 + q * P), hidden(k, L),
                              k == 0, k == KT - 1)
                m.then_inc(used if q else q_ps, 1)
                if n == 4:
                    qk_square(0)
                    transpose_v()
                if n == 6:
                    qk_rotate(0)
                    qk_square(1)
                if n == 8:
                    qk_square(2)
                if n == 9:
                    qk_rotate(1)
                if n == 11:
                    qk_rotate(2)

            pe.wait_ge(q_done, 3)
            pe.wait_ge(s_y, 4)
            def scores(g):
                for i in range(4):
                    head = HEADS[4 * (g % 2) + i]
                    if g:
                        pe.wait_ge(a_ctx, 4 * g + i - 3)
                        pe.wait_ge(a_loc, 4 * g + i - 3)
                    else:
                        pe.wait_ge(*oin_free(14 + (i + 2) % 4))
                    mm(ps[i][:], qt[:, head % 4, g // 2 * P:(g // 2 + 1) * P], kpad[:, head // 4, :],
                       start=True, stop=True).then_inc(a_s, 1)

            def values(g):
                for i in range(5):
                    n, x = 4 * g + i, 4 * (g % 2) + i
                    if i < 4:
                        pe.wait_ge(a_p, n + 1)
                        if n >= 2:
                            pe.wait_ge(a_tc, n - 1)
                        for s in range(4):
                            m = nc.tensor.transpose(ps[4 + i % 2][:, s * P:(s + 1) * P],
                                                    sc[:, x, s * P:(s + 1) * P], ident[:])
                        m.then_inc(a_t, 1)
                    if i >= 1:
                        y = x - 1
                        pe.wait_ge(a_tc, n)
                        for s in range(4):
                            m = mm(ps[6 + g // 2][:, (y // 2) * P:(y // 2 + 1) * P], vpad[:, s, y % 2, :],
                                   pt[:, y % 2, s, :], start=(s == 0 and y % 2 == 0), stop=(s == 3 and y % 2 == 1))
                        m.then_inc(a_o, 1)

            scores(0)
            scores(1)
            pe.wait_ge(v_done, 1)
            for g in range(4):
                values(g)
                if g < 2:
                    scores(g + 2)

            pe.wait_ge(a_ctx, 16)
            pe.wait_ge(a_loc, 16)
            project_out([J_OWOUT + b for b in range(OWOUT)], (4, 5, 6, 7, 0, 1, 2, 3), L, 16, (9, 9, 9, 9, 11, 11, 11, 11))
            pe.wait_ge(res_done, 16 + KT)
            norm_mean(3, ssum, L)

            pe.wait_ge(c_moe, 64)
            for k in range(KT):
                pe.wait_ge(n_h, 24 + k + 1)
                for t in range(2):
                    m = mm(ps[6 + t][:, 0:NEXP], ht[:, k, t * P:(t + 1) * P], rw[:, k, :],
                           start=(k == 0), stop=(k == KT - 1))
                if k == KT - 1:
                    m.then_inc(r_lg, 1)
                for t in range(2):
                    m = nc.tensor.transpose(ps[2 * t + k // 4][:, k % 4 * P:(k % 4 + 1) * P],
                                            ht[:, k, t * P:(t + 1) * P], ident[:])
                    if k % 4 == 3:
                        m.then_inc(t_ps, 1)
            pe.wait_ge(r_sel, 1)
            mm(ps[7][:, 0:8], tri[:, 0], sel[:, 0], start=True, stop=True)
            mm(ps[7][:, 8:16], tri[:, 1], sel[:, 0], start=True, stop=False)
            mm(ps[7][:, 8:16], tri[:, 0], sel[:, 1], start=False, stop=True)
            mm(ps[7][:, 16:24], tri[:, 1], sel[:, 0], start=True, stop=False)
            mm(ps[7][:, 16:24], tri[:, 1], sel[:, 1], start=False, stop=True).then_inc(r_pos, 1)

            def gather(h, made, bank=7):
                pe.wait_ge(hot_made, made)
                for kk in range(4):
                    k = 4 * h + kk
                    for i in range(4):
                        src = hklo if i % 2 else hkhi
                        m = mm(ps[bank][:, kk * P:(kk + 1) * P], src[:, i // 2, k * P:(k + 1) * P], hot[:, i // 2],
                               start=(i == 0), stop=(i == 3))
                m.then_inc(misc, 1)

            def scatter(q, bank=7):
                for kk in range(2):
                    k = 2 * q + kk
                    mm(ps[bank][:, kk * L:(kk + 1) * L], yhi[:, k * P:(k + 1) * P], hott[:], start=True, stop=False)
                    m = mm(ps[bank][:, kk * L:(kk + 1) * L], ylo[:, k * P:(k + 1) * P], hott[:], start=False,
                           stop=True)
                m.then_inc(misc, 1)

            pe.wait_ge(t_lo, 4)
            gather(0, 1)
            gather(1, 1, bank=0)

            def round_of(r):
                def block_wait(i):
                    wait_block(J_MOE + i, r, ROUND_BLOCKS)
                    return J_MOE + i

                def rhs(j, at):
                    return whi[:, j % SPLIT, at:at + CHUNK], wlo[:, j % SPLIT, at:at + CHUNK]

                def chunk_in(c, first, bank):
                    for h in range(2):
                        j = block_wait(first + h)
                        for kk in range(4):
                            k = 4 * h + kk
                            w = rhs(j, kk * CHUNK)
                            mm(ps[bank][:], ghi[:, k], w[0], start=(k == 0), stop=False)
                            mm(ps[bank][:], ghi[:, k], w[1], start=False, stop=False)
                            m = mm(ps[bank][:], glo[:, k], w[0], start=False, stop=(k == KT - 1))
                        m.then_inc(used, 1)

                def gate(c):
                    if c == 0:
                        pe.wait_ge(misc_free, 7 * r + 2)
                    pe.wait_ge(e_a, NCH * r + (max(c - 1, 0) + 1))
                    chunk_in(c, gate_block(c), c % 2)

                def up(c):
                    chunk_in(c, gate_block(c) + 2, 2 + c % 2)

                def turn(c):
                    pe.wait_ge(e_a, NCH * r + (c + 2))
                    pe.wait_ge(e_lo, NCH * r + (c + 1))
                    for i in range(4):
                        m = nc.tensor.transpose(ps[6][:, i * P:(i + 1) * P], am[:, i * P:(i + 1) * P], ident[:])
                    m.then_inc(e_t, 1)

                def down(c):
                    pe.wait_ge(e_lo, NCH * r + (c + 2))
                    if c == 0:
                        pe.wait_ge(e_y, r + 1)
                    for h in range(2):
                        j = block_wait(down_block(c) + h)
                        for i in range(4):
                            f, n = 2 * h + i // 2, i % 2
                            w = rhs(j, (i // 2) * D + n * CHUNK)
                            mm(ps[4 + n][:], athi[:, f], w[0], start=(c == 0 and f == 0), stop=False)
                            mm(ps[4 + n][:], athi[:, f], w[1], start=False, stop=False)
                            m = mm(ps[4 + n][:], atlo[:, f], w[0], start=False, stop=(c == NCH - 1 and f == 3))
                        m.then_inc(used, 1)

                def spare(i):
                    pe.wait_ge(misc_free, 2 + 7 * r + i)

                for c in range(NCH):
                    gate(c)
                    if c:
                        turn(c - 1)
                    up(c)
                    if c == NCH - 1:
                        spare(5)
                        gather(0, r + 2)
                    if c:
                        down(c - 1)
                    if c == 0:
                        pe.wait_ge(e_y, r + 1)
                    if c < 4:
                        spare(c)
                        scatter(c)
                    if c == 4:
                        spare(4)
                        for t in range(2):
                            nc.tensor.transpose(ps[7][:, t * P:(t + 1) * P], hot[:, t].bitcast(F32), ident[:])
                        for t in range(2):
                            m = mm(ps[7][:, 256:257], hot[:, t].bitcast(F32), cw[:, t:t + 1],
                                   start=(t == 0), stop=(t == 1))
                        m.then_inc(misc, 1)
                turn(NCH - 1)
                spare(6)
                gather(1, r + 2)
                down(NCH - 1)

            with pe.Fori(0, NEXP) as r:
                round_of(r)
            crowded = pe.value_load(infoi[0:1, 0:1], min_val=0, max_val=OVER)
            with pe.Fori(NEXP, NEXP + OVER) as r:
                with pe.If(r < crowded + NEXP):
                    round_of(r)
            pe.wait_ge(e_y, crowded + (NEXP + 1))
            for q in range(4):
                scatter(q, bank=q)

        @block.scalar
        def _(act):
            def copy(dst, src, scale=1.0):
                return nc.scalar.activation(dst, src, ACT.Copy, scale=scale)

            def split(j, turn=0, per=0, n=BLK):
                slot, uses = block_at(j, turn, per)
                act.wait_ge(raw_loaded[slot], uses * 16)
                if per or j >= SPLIT:
                    act.wait_ge(used, turn * per + (j - SPLIT + 1) if per else j - SPLIT + 1)
                copy(whi[:, j % SPLIT, 0:n], raw[:, slot, 0:n]).then_inc(hi_made, 1)

            done = [0]

            def until(j_end):
                while done[0] < j_end:
                    j = done[0]
                    split(j, n=width_of(j))
                    done[0] += 1

            act.dma_start(vec[:], a["c_vec"]).then_inc(c_vec, 16)
            for src, dst in ((a["c_z"], zt[:]), (a["c_w12"], w12[:])):
                act.dma_start(dst, src).then_inc(c_net, 16)
            for src, dst in ((a["c_sq"][0], ident[:]), (a["c_sq"][1], mean[:])):
                act.dma_start(dst, src).then_inc(c_even, 16)
            for src, dst in ((a["c_w3"], w3[:]), (a["c_decay"], decay[:])):
                act.dma_start(dst, src).then_inc(c_filt, 16)
            act.dma_start(xin[:], a["xt"].rearrange("(k p) t -> p k t", p=P)).then_inc(c_x, 16)
            for src, dst in ((a["c_dft"], dft[:]), (a["c_dft2"], dft2[:])):
                act.dma_start(dst, src).then_inc(c_filt, 16)
            act.wait_ge(c_vec, 16)
            nc.scalar.activation(scond[:], col("cond", 0, 16).rearrange("p (k c) -> p k c", c=2),
                                 ACT.Silu).then_inc(act_s, 1)
            act.wait_ge(act_s, 1)
            copy(sc4[:, :, 0:2], scond[:]).then_inc(act_s, 1)

            def copy_rows(bank, buf, block, cols):
                act.wait_ge(used, block)
                if cols is not None:
                    act.wait_ge(cols_made, cols)
                copy(rows[:, buf], ps[bank][0:4, :]).then_inc(rows_made, 1)

            def even_rows(c):
                copy_rows(6, c % 2, ada_at(2 * c + 1) + 1, c - 1 if c >= 2 else None)

            def filter_sine(i):
                act.wait_ge(f_arg, i + 1)
                nc.scalar.activation(sred[:], sarg, ACT.Sin).then_inc(f_sin, 1)

            def filter_abs(h):
                act.wait_ge(f_taps, h + 1)
                nc.scalar.activation(hf[:], hf[:], ACT.Abs)
                nc.scalar.activation(hb[:], hb[:], ACT.Abs).then_inc(f_abs, 1)

            def filter_copy(n):
                act.wait_ge(f_k, n + 1)
                h, m = n // 5, n % 5
                copy(kf[:, m, h * HALF:(h + 1) * HALF], ps[4 + n % 2][:, 0:HALF]).then_inc(f_kcopy, 1)

            def norm_squares(n, src, ready, sqb, width, tiles=range(KT)):
                for d in tiles:
                    act.wait_ge(*ready(d))
                    if d >= 2:
                        act.wait_ge(n_sum, 7 * n + max(1, d - 2))
                    nc.scalar.activation(sqb[:, d % 2, 0:width], src[:, d, 0:width], ACT.Square).then_inc(n_sq, 1)

            def norm_root(n, rs, width):
                act.wait_ge(n_mean, n + 1)
                nc.scalar.activation(rs[:, 0:width], ps[5 if n == 1 else 6][:, 0:width], ACT.Sqrt,
                                     bias=eps[:]).then_inc(n_root, 1)

            def norm_scale(n, sqb, width, h_free, mod, shift, full=None, also=None):
                act.wait_ge(used, h_free) if h_free else None
                for d in range(KT):
                    act.wait_ge(n_h, 8 * n + d + 1)
                    if full is None:
                        for s in range(width // L):
                            at = slice(s * L, (s + 1) * L)
                            m = nc.scalar.activation(hhi[:, d, at], sqb[:, d % 2, at], ACT.Identity,
                                                     bias=mod[:, shift + d, s:s + 1])
                    else:
                        m = copy(hhi[:, d, 0:width], full[:, d, :])
                    m.then_inc(n_hi, 1)
                    if also:
                        also(d)

            until(1)
            filter_sine(0)
            until(3)
            even_rows(0)
            until(4)
            filter_sine(1)
            until(5)
            even_rows(1)
            until(7)
            even_rows(2)
            until(8)
            filter_abs(0)
            norm_squares(0, xin, lambda d: (c_x, 16), sq0, T, range(0, 3))
            even_rows(3)
            norm_squares(0, xin, lambda d: (c_x, 16), sq0, T, range(3, KT))
            act.wait_ge(setup, 2)

            def behind_norm(d):
                if d == 0:
                    filter_copy(4)
                if d == 2:
                    filter_abs(1)
                if d >= 4:
                    filter_copy(d + 1)

            filter_copy(0)
            norm_root(0, rstd0, T)
            for n in range(1, 4):
                filter_copy(n)
            norm_scale(0, sq0, T, 0, emod, 0, also=behind_norm)
            until(10)
            filter_copy(9)

            for n, tile in enumerate(WIN_TILES):
                until(win_at(n // 2) + 3)
                act.wait_ge(*((used, win_at(n // 2) + 1) if n % 2 else (w_ps, n // 2 + 1)))
                if n == 6:
                    act.wait_ge(c_g, 16)
                    copy(invhi[:], dft[:]).then_inc(tab_hi, 1)
                if n < 2:
                    copy(fnt[:, n], ps[n % 4][:]).then_inc(w_free, 1)
                    if n == 0:
                        copy(fwhi[:], dft[:]).then_inc(tab_hi, 1)
                    if n:
                        until(win_at(0) + 4)
                    continue
                i, kind, q = (n - 2) // 6, (n - 2) % 6 // 2, n % 2
                dst = (tmp[:, q], tmp[:, 2 + q], x0c[:, 2 * i + q])[kind]
                if kind < 2 and i:
                    act.wait_ge(u_made, 2 * i)
                nc.scalar.activation(dst, ps[n % 4][:], ACT.Identity, scale=col("short", 18 + tile)).then_inc(w_mid, 1)
                if n % 2:
                    until(win_at(n // 2) + 4)
                    if n // 2 % 2:
                        even_rows(EARLY + n // 4)

            for c in range(HT):
                act.wait_ge(ut_ps, c + 1)
                copy(hhi[:, c], ps[4 + c % 2][:]).then_inc(ut_hi, 1)
                nc.scalar.activation(u[:, c], u[:, c], ACT.Identity, scale=col("skip", c)).then_inc(skips, 1)

            def result_hi_part(i):
                act.wait_ge(m_z, i + 1)
                copy(hhi[:, i], x0c[:, i]).then_inc(m_hi, 1)

            for i in range(HT):
                if i:
                    act.wait_ge(m_ps, i)
                act.wait_ge(x_im_sum, i + 1)
                copy(hhi[:, HT + 1], tmp[:, 2]).then_inc(x_im_hi, 1)
                act.wait_ge(x_re_sum, i + 1)
                copy(hhi[:, HT], tmp[:, 0]).then_inc(x_re_hi, 1)
                if i:
                    result_hi_part(i - 1)
                if i in (2, 4):
                    even_rows(LATE - 1 + i // 2)
                if i < 5:
                    until(J_LATE + 3 + i)
            act.wait_ge(x_re_lo, HT)
            act.wait_ge(x_im_lo, HT)
            for q in range(2):
                act.wait_ge(fn_ab, q + 1)
                copy(tmp[:, 2 * q], ps[2 * q][:])
                copy(tmp[:, 2 * q + 1], ps[2 * q + 1][:]).then_inc(fn_abc, 1)
            result_hi_part(HT - 1)
            for q in range(2):
                act.wait_ge(m_ps, HT + q + 1)
                copy(hhi[:, HT + q], ps[4 + q][:]).then_inc(m_hi, 1)

            for j in range(WOUT):
                act.wait_ge(used, wout_at(j) + 1)
                until(J_LATE + (8, 9, 10, 12)[j])
                if j:
                    norm_squares(1, res, lambda d: (res_done, d + 1), sq, T, range(2 * j if j > 1 else 0, 2 * j + 2))
            norm_root(1, rstd, T)
            even_rows(ADA // 2 - 1)
            norm_scale(1, sq, T, J_FFN, emod, 24)

            def silu(turn):
                for q in range(2):
                    act.wait_ge(ff_lo, turn)
                    nc.scalar.activation(sil[:, q], ps[q][:], ACT.Silu).then_inc(ff_silu, 1)

            def split_a(turn):
                for q in range(2):
                    act.wait_ge(ff_a, turn + q + 1)
                    copy(ahi[:, q], sil[:, q]).then_inc(ff_hi, 1)

            def odd_rows(pair, block):
                copy_rows(7, 0, block, pair + ADA // 2)

            until(J_FFN + 3)
            act.wait_ge(used, J_FFN + 1)
            silu(0)
            until(J_FFN + 4)
            split_a(0)
            until(J_FFN + 7)
            with act.Fori(0, FF_PAIRS - 1) as r:
                odd_rows(r, r * 6 + J_BODY)
                for x in range(2, 4):
                    split(J_BODY + x, r, 6, width_of(J_BODY + x))
                act.wait_ge(used, r * 6 + (J_BODY + 1))
                silu(r * 2 + 2)
                for x in range(4, 8):
                    split(J_BODY + x, r, 6, width_of(J_BODY + x))
                split_a(r * 2 + 2)
            odd_rows(FF_PAIRS - 1, J_TAIL)
            done[0] = J_TAIL + 2
            until(J_TAIL + 3)
            norm_squares(2, res, lambda d: (res_done, 8 + d + 1), sq, T)
            until(J_OWIN)
            norm_root(2, rstd, T)
            odd_rows(FF_PAIRS, J_OWIN)
            until(J_OWIN + 2)
            norm_scale(2, sq, T, J_TAIL + 1, omod, 0)

            def qk_root(y):
                act.wait_ge(q_ms, y + 1)
                act.wait_ge(q_n, y) if y else None
                nc.scalar.activation(rr[:], ps[4 + y % 2][:], ACT.Sqrt, bias=eps[:]).then_inc(q_root, 1)

            for n in range(2 * OWIN):
                until(min(J_OWIN + n // 2 + 3, J_MOE))
                if n < 6 or (n - 6) % 3 == 0:
                    act.wait_ge(*((used, J_OWIN + n // 2 + 1) if n % 2 else (q_ps, n // 2 + 1)))
                src = ps[n % 4]
                if n == 0:
                    nc.scalar.activation(qsq[:, 0], src[:], ACT.Square).then_inc(q_sq, 1)
                    copy(qraw[:, 0], src[:]).then_inc(q_raw, 1)
                elif n == 1:
                    copy(vt[:], src[:]).then_inc(v_copy, 1)
                elif n < 6:
                    y, at = n // 2, (n % 2) * L
                    nc.scalar.activation(qsq[:, y, at:at + L], src[:, 0:L], ACT.Square).then_inc(q_sq, 1)
                    copy(qraw[:, y, at:at + L], src[:, 0:L]).then_inc(q_raw, 1)
                elif (n - 6) % 3 == 0:
                    if n > 6:
                        act.wait_ge(s_hx, (n - 6) // 3)
                    copy(gcs[:], src[:, 0:L]).then_inc(s_gc, 1)
                if n == 4:
                    qk_root(0)
                if n == 7:
                    qk_root(1)
                if n == 9:
                    qk_root(2)
            act.wait_ge(used, J_OWOUT)
            act.wait_ge(s_y, 4)
            copy(hhi[:, 4:8, 0:L], ysc[:]).then_inc(m_hi, 1)

            def context_scores(g):
                for i in range(4):
                    x = 4 * (g % 2) + i
                    act.wait_ge(a_s, 4 * g + i + 1)
                    if g >= 2:
                        act.wait_ge(a_t, 4 * g + i - 7)
                    copy(sc[:, x, L:T], ps[i][:, L:T], 0.125).then_inc(a_ctx, 1)

            def exponentials(g):
                act.wait_ge(a_max, g + 1)
                at = slice(4 * (g % 2), 4 * (g % 2) + 4)
                nc.scalar.activation(esink[:, at], esink[:, at], ACT.Exp).then_inc(a_sink, 1)
                for x in range(4 * (g % 2), 4 * (g % 2) + 4):
                    nc.scalar.activation(sc[:, x], sc[:, x], ACT.Exp, bias=nmax[:, x:x + 1],
                                         accum_out=ssm[:, x:x + 1]).then_inc(a_exp, 1)

            def copy_transposed(g):
                for i in range(4):
                    n = 4 * g + i
                    act.wait_ge(a_t, n + 1)
                    if n >= 2:
                        act.wait_ge(a_o, n - 1)
                    copy(pt[:, i % 2], ps[4 + i % 2][:].rearrange("p (s c) -> p s c", s=4)).then_inc(a_tc, 1)

            def attended(b):
                act.wait_ge(a_o, 8 * b + 8)
                copy(hhi[:, 0:4, b * P:(b + 1) * P],
                     ps[6 + b][:].rearrange("p (k c) -> p k c", k=4)).then_inc(m_hi, 1)

            context_scores(0)
            context_scores(1)
            exponentials(0)
            exponentials(1)
            copy_transposed(0)
            context_scores(2)
            copy_transposed(1)
            exponentials(2)
            context_scores(3)
            attended(0)
            copy_transposed(2)
            exponentials(3)
            copy_transposed(3)
            attended(1)
            for j in range(OWOUT):
                act.wait_ge(used, J_OWOUT + j + 1)
                until(min(J_OWOUT + j + 4, J_MOE))
                if j:
                    norm_squares(3, res, lambda d: (res_done, 16 + d + 1), sq, L,
                                 range(2 * j if j > 1 else 0, 2 * j + 2))
            norm_root(3, rstd, L)
            norm_scale(3, sq, L, J_MOE, omod, 24, full=ht)

            act.wait_ge(r_sub, 1)
            nc.scalar.activation(ex[:], ex[:], ACT.Exp).then_inc(r_exp, 1)
            for n, i in enumerate((0, 2, 1, 3)):
                act.wait_ge(t_ps, n + 1)
                copy(hkhi[:, i // 2, (i % 2) * 512:(i % 2) * 512 + 512], ps[i][:]).then_inc(t_hi, 1)

            def split_gathered(h, count, bank=7):
                act.wait_ge(misc, count)
                copy(ghi[:, 4 * h:4 * h + 4, :], ps[bank][:].rearrange("p (k c) -> p k c", k=4)).then_inc(g_hi, 1)

            split_gathered(0, 1)
            split_gathered(1, 2, bank=0)

            def result_hi():
                for n in range(2):
                    nc.scalar.activation(yhi[:, n * CHUNK:(n + 1) * CHUNK], ps[4 + n][:], ACT.Identity,
                                         scale=wslot[:]).then_inc(e_yhi, 1)

            act.wait_ge(zeroed, 4)
            act.wait_ge(e_a, 1)
            act.wait_ge(e_lo, 1)

            def round_of(r):
                def chunk_hi(c):
                    act.wait_ge(e_t, NCH * r + c + 1)
                    copy(athi[:], ps[6][:].rearrange("p (k c) -> p k c", k=4)).then_inc(e_hi, 1)

                nc.scalar.activation(idle[:], eps[:], ACT.Silu)
                for x in range(1, ROUND_BLOCKS):
                    if x == 3:
                        act.wait_ge(used, r * ROUND_BLOCKS + J_MOE)
                        act.wait_ge(misc_free, 7 * r + 2)
                        result_hi()
                    for c in range(NCH):
                        if x == gate_block(c) + 4:
                            act.wait_ge(used, r * ROUND_BLOCKS + (J_MOE + gate_block(c) + 2))
                            act.wait_ge(e_a, NCH * r + (c + 1))
                            nc.scalar.activation(sg[:], ps[c % 2][:], ACT.Silu).then_inc(e_silu, 1)
                        if c < NCH - 1 and x == down_block(c):
                            chunk_hi(c)
                    if x == 30:
                        act.wait_ge(misc, 7 * r + 7)
                        copy(hott[:], ps[7][:, 0:L])
                        copy(wslot[:], ps[7][:, L:L + 1]).then_inc(misc_free, 1)
                    if x == 40:
                        split_gathered(0, 7 * r + 8)
                    split(J_MOE + x, r, ROUND_BLOCKS)
                chunk_hi(NCH - 1)
                split(J_MOE + ROUND_BLOCKS, r, ROUND_BLOCKS)
                split_gathered(1, 7 * r + 9)

            split(J_MOE)
            with act.Fori(0, NEXP) as r:
                round_of(r)
            crowded = act.value_load(infoi[0:1, 0:1], min_val=0, max_val=OVER)
            with act.Fori(NEXP, NEXP + OVER) as r:
                with act.If(r < crowded + NEXP):
                    round_of(r)
            act.wait_ge(used, crowded * ROUND_BLOCKS + (NEXP * ROUND_BLOCKS + J_MOE))
            result_hi()

        @block.vector
        def _(dve):
            vv = nc.vector
            own = Steps(dve, dve_s)

            def split(j, turn=0, per=0, n=BLK):
                slot, uses = block_at(j, turn, per)
                if slot == POOL_SLOT:
                    return
                dve.wait_ge(hi_made, turn * per + (j + 1) if per else j + 1)
                vv.tensor_tensor(wlo[:, j % SPLIT, 0:n], raw[:, slot, 0:n], whi[:, j % SPLIT, 0:n].bitcast(F32),
                                 ALU.subtract).then_inc(raw_free[slot], 1)

            done = [0]

            def until(j_end):
                while done[0] < j_end:
                    j = done[0]
                    split(j, n=width_of(j))
                    done[0] += 1

            def filter_argument(i):
                dve.wait_ge(f_ps, i + 1)
                if i:
                    dve.wait_ge(f_sin, 1)
                own.step(vv.tensor_scalar(sarg, ps[i][0:64, 0:L], col("b1" if i == 0 else "b2")[0:64],
                                          col("freq")[0:64], ALU.add, ALU.mult))
                own.step(vv.tensor_scalar(rstd0[0:64, 0:L], sarg, float(1 / (2 * np.pi)), ROUND, ALU.mult, ALU.add))
                own.step(vv.tensor_scalar(rstd0[0:64, 0:L], rstd0[0:64, 0:L], ROUND, None, ALU.subtract))
                for part in TURN:
                    own.step(vv.scalar_tensor_tensor(out=sarg, in0=rstd0[0:64, 0:L], scalar=-part, in1=sarg,
                                                     op0=ALU.mult, op1=ALU.add))
                vv.tensor_scalar(sarg, sarg, 3.1415925, -3.1415925, ALU.min, ALU.max).then_inc(f_arg, 1)

            def filter_taps(h):
                dve.wait_ge(f_ps, 3 + h)
                if h:
                    dve.wait_ge(f_l1, 1)
                for t in range(2):
                    vv.tensor_tensor(hf[:, t], ps[t][:, 0:HALF], decay[:, t, h * HALF:(h + 1) * HALF], ALU.mult)
                    m = vv.tensor_tensor(hb[:, t], ps[2 + t][:, 0:HALF], decay[:, t, h * HALF:(h + 1) * HALF], ALU.mult)
                own.step(m)
                own.step(vv.memset(hb[0:1, 0, :], 0.0))
                vv.tensor_tensor(hs[:], hf[:], hb[:], ALU.add)
                vv.tensor_tensor(hd[:], hf[:], hb[:], ALU.subtract).then_inc(f_taps, 1)

            dve.wait_ge(c_vec, 16)
            dve.wait_ge(act_s, 2)
            vv.tensor_tensor(sc4[:, :, 2:4], scond[:], sc4[:, :, 0:2].bitcast(F32), ALU.subtract).then_inc(silu_c, 1)
            filter_argument(0)
            until(3)
            dve.wait_ge(c_even, 32)
            vv.tensor_tensor(pick[:], ident[0:4, 0:2], ident[0:4, 2:4], ALU.add).then_inc(pick_made, 1)
            filter_argument(1)
            until(5)
            dve.wait_ge(c_filt, 16 * 4)
            filter_taps(0)
            until(8)

            def gains(mod, i, norm, g):
                own.step(vv.scalar_tensor_tensor(out=gain[:, g + i], in0=mod[:, 8 + 24 * i:16 + 24 * i, :], scalar=1.0,
                                                 in1=col(norm, 0, 8).unsqueeze(2).to_broadcast([P, 8, 2]),
                                                 op0=ALU.add, op1=ALU.mult))

            def even_mod(t0, t1):
                own.step(vv.tensor_tensor(emod[:, t0:t1], ps[7][:, 2 * t0:2 * t1].rearrange("p (t c) -> p t c", c=2),
                                          col("e_ada_b", t0, t1 - t0).unsqueeze(2).to_broadcast([P, t1 - t0, 2]),
                                          ALU.add))

            def norm_reciprocal(n, rs, width):
                dve.wait_ge(n_root, n + 1)
                own.step(vv.reciprocal(rs[:, 0:width], rs[:, 0:width]))

            def norm_dve(n, src, sqb, rs, width, mod, shift, full=None, also=None):
                halves = [slice(s * L, (s + 1) * L) for s in range(width // L)]

                def lo(d):
                    dve.wait_ge(n_hi, 8 * n + d + 1)
                    if full is not None:
                        m = vv.tensor_tensor(hlo[:, d, 0:width], full[:, d, :], hhi[:, d, 0:width].bitcast(F32),
                                             ALU.subtract)
                    else:
                        for s, at in enumerate(halves):
                            m = vv.scalar_tensor_tensor(out=hlo[:, d, at], in0=sqb[:, d % 2, at],
                                                        scalar=mod[:, shift + d, s:s + 1],
                                                        in1=hhi[:, d, at].bitcast(F32), op0=ALU.add, op1=ALU.subtract)
                    m.then_inc(n_ready, 1)

                for d in range(KT):
                    h = sqb[:, d % 2, 0:width] if full is None else full[:, d, :]
                    if d >= 2:
                        dve.wait_ge(n_ready, 8 * n + d - 1)
                    for s, at in enumerate(halves):
                        m = vv.scalar_tensor_tensor(out=h[:, at], in0=src[:, d, at], scalar=gain[:, n, d, s:s + 1],
                                                    in1=rs[:, at], op0=ALU.mult, op1=ALU.mult)
                    if full is not None:
                        own.step(m)
                        m = vv.tensor_scalar(h, h, mod[:, shift + d, 0:1], None, ALU.add)
                    m.then_inc(n_h, 1)
                    if d:
                        lo(d - 1)
                    if also:
                        also(d)
                lo(KT - 1)

            dve.wait_ge(cols_made, EARLY)
            even_mod(0, 4 * EARLY)
            vv.engine_nop().then_inc(emod_made, 1)
            gains(emod, 0, "e_norm1", 0)
            norm_reciprocal(0, rstd0, T)
            norm_dve(0, xin, sq0, rstd0, T, emod, 0, also=lambda d: filter_taps(1) if d == 1 else None)

            for n, tile in enumerate(WIN_TILES):
                until(win_at(n // 2) + 3)
                if n in (0, 6):
                    dve.wait_ge(tab_hi, 1 if n == 0 else 2)
                    hi, lo = (fwhi, fwlo) if n == 0 else (invhi, invlo)
                    vv.tensor_tensor(lo[:], dft[:], hi[:].bitcast(F32), ALU.subtract).then_inc(tab_lo, 1)
                if n < 2:
                    if n:
                        until(win_at(0) + 4)
                    continue
                i, kind, q = (n - 2) // 6, (n - 2) % 6 // 2, n % 2
                dst = half((tmp[:, q], tmp[:, 2 + q], x0c[:, 2 * i + q])[kind])
                src = half(ps[n % 4][:])
                dve.wait_ge(w_mid, n - 1)
                own.step(vv.scalar_tensor_tensor(out=dst[:, :, 1:L], in0=src[:, :, 0:L - 1], scalar=col("short", tile),
                                                 in1=dst[:, :, 1:L], op0=ALU.mult, op1=ALU.add))
                vv.scalar_tensor_tensor(out=dst[:, :, 0:L - 1], in0=src[:, :, 1:L], scalar=col("short", 36 + tile),
                                        in1=dst[:, :, 0:L - 1], op0=ALU.mult, op1=ALU.add).then_inc(w_free, 1)
                if kind == 1:
                    dve.wait_ge(w_free, n + 1)
                    vv.tensor_tensor(u[:, 2 * i + q], tmp[:, q], tmp[:, 2 + q], ALU.mult).then_inc(u_made, 1)
                if n % 2:
                    until(win_at(n // 2) + 4)
            dve.wait_ge(cols_made, LATE - 1)
            dve.wait_ge(f_l1, 2)
            vv.reciprocal(il1[:], ps[7][:, 4 * ADA:4 * ADA + HT]).then_inc(emod_made, 1)

            def transposed_lo(c):
                dve.wait_ge(ut_hi, c + 1)
                vv.tensor_tensor(hlo[:, c], ps[4 + c % 2][:], hhi[:, c].bitcast(F32), ALU.subtract).then_inc(ut_lo, 1)

            def products(i):
                dve.wait_ge(x_ps, i + 1)
                if i:
                    dve.wait_ge(x_im_lo, i)
                    dve.wait_ge(x_re_lo, i)
                at = slice(i * P, (i + 1) * P)
                re, im = ps[2 * (i % 2)], ps[2 * (i % 2) + 1]
                for n, x, k, done in ((2, re, kf[:, 3:5, at], None), (3, im, kf[:, 1:3, at], x_im),
                                      (0, re, kf[:, 0:3:2, at], None), (1, im, kf[:, 3:5, at], x_prod)):
                    m = vv.tensor_tensor(tmp[:, n].rearrange("p (m s c) -> p m s c", m=2, s=2),
                                         x[:].rearrange("p (m s c) -> p m s c", m=2, s=2),
                                         k.unsqueeze(2).to_broadcast([P, 2, 2, P]), ALU.mult)
                    if done is not None:
                        m.then_inc(done, 1)
                dve.wait_ge(x_prod, i + 1)
                vv.tensor_tensor(tmp[:, 0], tmp[:, 0], tmp[:, 1], ALU.subtract).then_inc(x_re_sum, 1)

            def real_lo(i):
                dve.wait_ge(x_re_hi, i + 1)
                vv.tensor_tensor(hlo[:, HT], tmp[:, 0], hhi[:, HT].bitcast(F32), ALU.subtract).then_inc(x_re_lo, 1)

            def result(i):
                dve.wait_ge(m_ps, i + 1)
                dve.wait_ge(skips, i + 1)
                own.step(vv.scalar_tensor_tensor(out=u[:, i], in0=ps[4 + i % 2][:], scalar=il1[:, i:i + 1],
                                                 in1=u[:, i], op0=ALU.mult, op1=ALU.add))
                vv.tensor_tensor(x0c[:, i], u[:, i], x0c[:, i], ALU.mult).then_inc(m_z, 1)

            def result_lo(i):
                dve.wait_ge(m_hi, i + 1)
                vv.tensor_tensor(hlo[:, i], x0c[:, i], hhi[:, i].bitcast(F32), ALU.subtract).then_inc(m_ready, 1)

            for c in range(3):
                transposed_lo(c)
            products(0)
            for c in range(3, HT):
                transposed_lo(c)
            for i in range(HT):
                if i:
                    products(i)
                    result(i - 1)
                real_lo(i)
                if i:
                    result_lo(i - 1)
                if i < 5:
                    until(J_LATE + 2 + i)
            result(HT - 1)
            result_lo(HT - 1)
            dve.wait_ge(cols_made, ADA // 2 - 1)
            even_mod(4 * EARLY, 2 * ADA - 4)
            vv.engine_nop().then_inc(emod_made, 1)
            gains(emod, 1, "e_norm2", 0)
            for q in range(2):
                dve.wait_ge(m_hi, HT + q + 1)
                vv.tensor_tensor(hlo[:, HT + q], ps[4 + q][:], hhi[:, HT + q].bitcast(F32),
                                 ALU.subtract).then_inc(m_ready, 1)

            def residual(n, j, base, mod, width, lookahead):
                until(lookahead)
                dve.wait_ge(*((used, j + 1) if n % 2 else (o_ps, base // 2 + n // 2 + 1)))
                for s in range(width // L):
                    m = vv.scalar_tensor_tensor(out=res[:, n, s * L:(s + 1) * L], in0=ps[n % 4][:, s * L:(s + 1) * L],
                                                scalar=mod[:, 16 + n, s:s + 1], in1=res[:, n, s * L:(s + 1) * L],
                                                op0=ALU.mult, op1=ALU.add)
                m.then_inc(res_done, 1)

            dve.wait_ge(c_res, 16)
            for n in range(KT):
                residual(n, wout_at(n // 2), 0, emod, T, J_LATE + (8, 8, 8, 9, 9, 9, 10, 11)[n])
            until(J_FFN + 2)
            norm_reciprocal(1, rstd, T)
            norm_dve(1, res, sq, rstd, T, emod, 24)
            dve.wait_ge(cols_made, ADA // 2)
            even_mod(2 * ADA - 4, 2 * ADA)
            vv.engine_nop().then_inc(emod_made, 1)

            def add_down(turn, last, also=None):
                for d in range(KT):
                    if d < KT - 1:
                        dve.wait_ge(ff_d, turn * 7 + d + 1)
                    else:
                        dve.wait_ge(used, last)
                    dve.wait_ge(ff_added, turn * 8 + (d + 1))
                    vv.tensor_tensor(facc[:, d], facc[:, d], ps[4 + d % 3][:], ALU.add).then_inc(ff_added, 1)
                    if also:
                        also(d)

            def activate(turn, last):
                dve.wait_ge(used, last)
                for q in range(2):
                    dve.wait_ge(ff_silu, turn * 2 + (q + 1))
                    vv.tensor_tensor(sil[:, q], sil[:, q], ps[2 + q][:], ALU.mult).then_inc(ff_a, 1)
                for q in range(2):
                    dve.wait_ge(ff_hi, turn * 2 + (q + 1))
                    vv.tensor_tensor(alo[:, q], sil[:, q], ahi[:, q].bitcast(F32), ALU.subtract).then_inc(ff_lo, 1)

            def odd_modulation(unit, bank=6):
                dve.wait_ge(cols_made, unit + (ADA // 2 + 1))
                bias = vec[:, bass.ds(unit * 4 + VEC["o_ada_b"].start, 4)]
                vv.tensor_tensor(omod[:, bass.ds(unit * 4, 4), :], ps[bank][:, 0:8].rearrange("p (t c) -> p t c", c=2),
                                 bias.unsqueeze(2).to_broadcast([P, 4, 2]), ALU.add).then_inc(oa_read, 1)

            until(J_FFN + 4)
            activate(0, J_FFN + 2)
            until(J_FFN + 7)
            with dve.Fori(0, FF_PAIRS - 1) as r:
                for x in range(2, 4):
                    split(J_BODY + x, r, 6, width_of(J_BODY + x))
                odd_modulation(r)
                add_down(r, r * 6 + (J_BODY + 3))
                for x in range(4, 7):
                    split(J_BODY + x, r, 6, width_of(J_BODY + x))
                activate(r + 1, r * 6 + (J_BODY + 5))
                split(J_BODY + 7, r, 6, width_of(J_BODY + 7))
            odd_modulation(FF_PAIRS - 1)
            done[0] = J_TAIL + 2
            until(J_TAIL + 3)
            def residual_down(d):
                dve.wait_ge(ff_added, 8 * (FF_PAIRS - 1) + 4 + d + 1)
                for s in range(2):
                    m = vv.scalar_tensor_tensor(out=res[:, d, s * L:(s + 1) * L], in0=facc[:, d, s * L:(s + 1) * L],
                                                scalar=emod[:, 40 + d, s:s + 1], in1=res[:, d, s * L:(s + 1) * L],
                                                op0=ALU.mult, op1=ALU.add)
                m.then_inc(res_done, 1)

            add_down(FF_PAIRS - 1, J_TAIL + 1, also=residual_down)
            until(J_OWIN)
            norm_reciprocal(2, rstd, T)
            odd_modulation(FF_PAIRS, 5)
            dve.wait_ge(oa_read, FF_PAIRS + 1)
            gains(omod, 0, "o_norm1", 2)
            gains(omod, 1, "o_norm2", 2)
            until(J_OWIN + 2)
            norm_dve(2, res, sq, rstd, T, omod, 0)

            def qk_norm(y):
                dve.wait_ge(q_root, y + 1)
                own.step(vv.reciprocal(rr[:], rr[:]))
                dve.wait_ge(q_raw, 1 + 2 * y)
                vv.scalar_tensor_tensor(out=qn[:, y], in0=qraw[:, y], scalar=col("q_norm" if y else "k_norm"),
                                        in1=rr[:], op0=ALU.mult, op1=ALU.mult).then_inc(q_n, 1)

            def qk_turn(y):
                dve.wait_ge(q_rot, y + 1)
                n = T if y else L
                dve.wait_ge(zeroed, 2)
                for dst, src, i in ((qsq, qn[:, y, 0:n], 0), (qraw, ps[6 + y % 2][:, 0:n], 1)):
                    d = dst[:, y, 0:n]
                    if y:
                        m = vv.tensor_tensor(half(d), half(src), rope[:, i:i + 1, :].to_broadcast([P, 2, L]), ALU.mult)
                    else:
                        m = vv.tensor_tensor(d, src, rope[:, i, :], ALU.mult)
                own.step(m)
                if y:
                    vv.tensor_tensor(qt[:, 2 * y - 2:2 * y, :], half(qsq[:, y]), half(qraw[:, y]),
                                     ALU.add).then_inc(q_done, 1)
                else:
                    for g in range(2):
                        rows = slice(64 * g, 64 * g + 64)
                        vv.tensor_tensor(kpad[rows, g, 0:L], qsq[rows, 0, 0:L], qraw[rows, 0, 0:L], ALU.add)
                        m = vv.tensor_copy(kpad[rows, g, L:T], qn[rows, 0, L:T])
                    m.then_inc(q_done, 1)

            def pad_v():
                dve.wait_ge(v_ps, 1)
                dve.wait_ge(zeroed, 2)
                v = ps[5][:].rearrange("p (s c) -> p s c", s=4)
                vv.tensor_copy(vpad[:, :, 0, 0:64], v[:, :, 0:64])
                vv.tensor_copy(vpad[:, :, 1, 64:128], v[:, :, 64:128]).then_inc(v_done, 1)

            for n in range(2 * OWIN):
                until(min(J_OWIN + n // 2 + 3, J_MOE))
                i, kind = (n - 6) // 3, (n - 6) % 3
                if n >= 6 and kind:
                    dve.wait_ge(*((used, J_OWIN + n // 2 + 1) if n % 2 else (q_ps, n // 2 + 1)))
                if n >= 6 and kind == 1:
                    dve.wait_ge(s_gc, i + 1)
                    vv.tensor_tensor(gm[:], gcs[:], ps[n % 4][:, 0:L], ALU.mult).then_inc(s_hx, 1)
                    dve.wait_ge(s_hx, i + 1)
                    own.step(vv.tensor_scalar(gcv[:], gm[:], col("sc", 4 + i), None, ALU.mult))
                    own.step(vv.scalar_tensor_tensor(out=gcv[:, 1:L], in0=gm[:, 0:L - 1], scalar=col("sc", i),
                                                     in1=gcv[:, 1:L], op0=ALU.mult, op1=ALU.add))
                    own.step(vv.scalar_tensor_tensor(out=gcv[:, 0:L - 1], in0=gm[:, 1:L], scalar=col("sc", 8 + i),
                                                     in1=gcv[:, 0:L - 1], op0=ALU.mult, op1=ALU.add))
                if n >= 6 and kind == 2:
                    vv.tensor_tensor(ysc[:, i], ps[n % 4][:, 0:L], gcv[:], ALU.mult).then_inc(s_y, 1)
                    dve.wait_ge(s_y, i + 1)
                if n == 4:
                    pad_v()
                    qk_norm(0)
                if n == 7:
                    qk_turn(0)
                    qk_norm(1)
                if n == 9:
                    qk_norm(2)
                if n == 10:
                    qk_turn(1)
                if n == 12:
                    qk_turn(2)
            dve.wait_ge(m_hi, 9)
            vv.tensor_tensor(hlo[:, 4:8, 0:L], ysc[:], hhi[:, 4:8, 0:L].bitcast(F32), ALU.subtract).then_inc(m_ready, 1)

            dve.wait_ge(c_mask, 16)
            def maxima(g):
                at = slice(4 * (g % 2), 4 * (g % 2) + 4)
                for i in range(4):
                    dve.wait_ge(a_ctx, 4 * g + i + 1)
                    vv.scalar_tensor_tensor(out=sc[:, 4 * (g % 2) + i, 0:L], in0=ps[i][:, 0:L], scalar=0.125,
                                            in1=mask[:, g // 2], op0=ALU.mult, op1=ALU.add).then_inc(a_loc, 1)
                dve.wait_ge(a_loc, 4 * g + 4)
                own.step(vv.tensor_reduce(smax[:, at], sc[:, at], AX.X, ALU.max))
                own.step(vv.tensor_tensor(smax[:, at], smax[:, at], col("sink", 4 * (g % 2), 4), ALU.max))
                vv.tensor_tensor(esink[:, at], col("sink", 4 * (g % 2), 4), smax[:, at], ALU.subtract)
                vv.tensor_scalar(nmax[:, at], smax[:, at], -1.0, None, ALU.mult).then_inc(a_max, 1)

            def probabilities(g):
                at = slice(4 * (g % 2), 4 * (g % 2) + 4)
                dve.wait_ge(a_exp, 4 * g + 4)
                own.step(vv.tensor_tensor(sden[:, at], ssm[:, at], esink[:, at], ALU.add))
                own.step(vv.reciprocal(sden[:, at], sden[:, at]))
                for x in range(4 * (g % 2), 4 * (g % 2) + 4):
                    vv.tensor_scalar(sc[:, x], sc[:, x], sden[:, x:x + 1], None, ALU.mult).then_inc(a_p, 1)

            def attended_lo(b):
                dve.wait_ge(m_hi, 10 + b)
                vv.tensor_tensor(hlo[:, 0:4, b * P:(b + 1) * P], ps[6 + b][:].rearrange("p (k c) -> p k c", k=4),
                                 hhi[:, 0:4, b * P:(b + 1) * P].bitcast(F32), ALU.subtract).then_inc(m_ready, 1)

            maxima(0)
            maxima(1)
            probabilities(0)
            probabilities(1)
            maxima(2)
            probabilities(2)
            maxima(3)
            attended_lo(0)
            probabilities(3)
            attended_lo(1)

            for n in range(KT):
                residual(n, J_OWOUT + n // 2, 8, omod, L, min(J_OWOUT + n // 2 + 3, J_MOE))
            vv.memset(ps[4][:], 0.0).then_inc(e_a, 1)
            vv.memset(ps[5][:], 0.0).then_inc(e_lo, 1)
            norm_reciprocal(3, rstd, L)
            norm_dve(3, res, sq, rstd, L, omod, 24, full=ht)

            def by_expert(x):
                return x.unsqueeze(2).to_broadcast([P, 2, NEXP, NEXP])

            def by_token(x):
                return x.unsqueeze(2).to_broadcast([P, 2, NEXP])

            dve.wait_ge(c_moe, 64)
            dve.wait_ge(r_lg, 1)
            for t in range(2):
                m = vv.tensor_tensor(lg[:, t], ps[6 + t][:, 0:NEXP], col("router_b", 0, 8), ALU.add)
            own.step(m)
            own.step(vv.tensor_reduce(top[:], lg[:], AX.X, ALU.max))
            vv.tensor_tensor(ex[:], lg[:], by_token(top[:]), ALU.subtract).then_inc(r_sub, 1)
            mine = lg[:].unsqueeze(3).to_broadcast([P, 2, NEXP, NEXP])
            vv.tensor_tensor(gt[:], by_expert(lg[:]), mine, ALU.is_gt)
            own.step(vv.tensor_tensor(eq[:], by_expert(lg[:]), mine, ALU.is_equal))
            own.step(vv.tensor_tensor(eq[:], eq[:], low[:].unsqueeze(1).to_broadcast([P, 2, NEXP, NEXP]), ALU.mult))
            own.step(vv.tensor_tensor(gt[:], gt[:], eq[:], ALU.add))
            own.step(vv.tensor_reduce(rank[:], gt[:], AX.X, ALU.add))
            vv.tensor_scalar(sel[:], rank[:], 2.0, None, ALU.is_lt).then_inc(r_sel, 1)
            dve.wait_ge(r_sel, 1)
            dve.wait_ge(r_exp, 1)
            own.step(vv.tensor_tensor(ex[:], ex[:], sel[:], ALU.mult))
            own.step(vv.tensor_reduce(den[:], ex[:], AX.X, ALU.add))
            own.step(vv.reciprocal(den[:], den[:]))
            own.step(vv.tensor_tensor(ctab[:, :, 0:NEXP], ex[:], by_token(den[:]), ALU.mult))
            dve.wait_ge(r_pos, 1)
            slot = ptab[:, :, 0:NEXP]
            own.step(vv.scalar_tensor_tensor(out=slot, in0=ps[7][:, 0:16].rearrange("p (t e) -> p t e", t=2),
                                             scalar=1.0, in1=sel[:], op0=ALU.add, op1=ALU.mult))
            own.step(vv.tensor_scalar(slot, slot, 1.0, None, ALU.subtract))
            own.step(vv.tensor_scalar(ov[:], ps[7][:, 16:24], float(P), None, ALU.is_gt))

            def one_hot(turn):
                vv.tensor_copy(cw[:].unsqueeze(2), ctab[:, :, bass.ds(turn, 1)])
                for t in range(2):
                    m = vv.tensor_scalar(hot[:, t], iota[:], ptab[:, t, bass.ds(turn, 1)], None, ALU.is_equal)
                m.then_inc(hot_made, 1)

            dve.wait_ge(c_iota, 16)
            one_hot(0)
            for n, i in enumerate((0, 2, 1, 3)):
                at = slice((i % 2) * 512, (i % 2) * 512 + 512)
                dve.wait_ge(t_hi, n + 1)
                vv.tensor_tensor(hklo[:, i // 2, at], ps[i][:], hkhi[:, i // 2, at].bitcast(F32),
                                 ALU.subtract).then_inc(t_lo, 1)

            ovb = ov[:].unsqueeze(1).to_broadcast([P, NEXP, NEXP])
            own.step(vv.tensor_tensor(gt[:, 0], low[:], ovb, ALU.mult))
            own.step(vv.tensor_reduce(ovr[:], gt[:, 0], AX.X, ALU.add))
            for i in range(OVER):
                own.step(vv.scalar_tensor_tensor(out=osel[:], in0=ovr[:], scalar=float(i), in1=ov[:],
                                                 op0=ALU.is_equal, op1=ALU.mult))
                both = osel[:].unsqueeze(1).to_broadcast([P, 2, NEXP])
                own.step(vv.scalar_tensor_tensor(out=obc[:], in0=slot, scalar=float(1 - P), in1=both,
                                                 op0=ALU.add, op1=ALU.mult))
                own.step(vv.tensor_reduce(ptab[:, :, NEXP + i], obc[:], AX.X, ALU.add))
                own.step(vv.tensor_scalar(ptab[:, :, NEXP + i:NEXP + i + 1], ptab[:, :, NEXP + i:NEXP + i + 1],
                                          1.0, None, ALU.subtract))
                own.step(vv.tensor_tensor(obc[:], ctab[:, :, 0:NEXP], both, ALU.mult))
                own.step(vv.tensor_reduce(ctab[:, :, NEXP + i], obc[:], AX.X, ALU.add))
                own.step(vv.tensor_tensor(obc[:, 0], osel[:], enum[:], ALU.mult))
                own.step(vv.tensor_reduce(info[:, 1 + i:2 + i], obc[:, 0], AX.X, ALU.add))
            own.step(vv.memset(ptab[:, :, NTAB - 1:NTAB], -1.0))
            own.step(vv.memset(ctab[:, :, NTAB - 1:NTAB], 0.0))
            own.step(vv.tensor_reduce(info[:, 0:1], ov[:], AX.X, ALU.add))
            vv.tensor_copy(infoi[:], info[:]).then_inc(r_tab, 1)

            def gathered_lo(h, count, bank=7):
                dve.wait_ge(g_hi, count)
                k = slice(4 * h, 4 * h + 4)
                vv.tensor_tensor(glo[:, k, :], ps[bank][:].rearrange("p (k c) -> p k c", k=4), ghi[:, k, :].bitcast(F32),
                                 ALU.subtract).then_inc(misc_free, 1)

            gathered_lo(0, 1)
            gathered_lo(1, 2, bank=0)
            dve.wait_ge(zeroed, 4)

            def result_lo_part(count):
                for n in range(2):
                    dve.wait_ge(e_yhi, count - 1 + n)
                    m = vv.scalar_tensor_tensor(out=ylo[:, n * CHUNK:(n + 1) * CHUNK], in0=ps[4 + n][:], scalar=wslot[:],
                                                in1=yhi[:, n * CHUNK:(n + 1) * CHUNK].bitcast(F32),
                                                op0=ALU.mult, op1=ALU.subtract)
                m.then_inc(e_y, 1)

            def add_scattered(q, count, bank=7):
                dve.wait_ge(misc, count)
                vv.tensor_tensor(macc[:, 2 * q:2 * q + 2, :], macc[:, 2 * q:2 * q + 2, :], half(ps[bank][:]),
                                 ALU.add).then_inc(misc_free, 1)

            def round_of(r):
                def chunk_lo(c):
                    dve.wait_ge(e_hi, NCH * r + c + 1)
                    vv.tensor_tensor(atlo[:], ps[6][:].rearrange("p (k c) -> p k c", k=4), athi[:].bitcast(F32),
                                     ALU.subtract).then_inc(e_lo, 1)

                for x in range(1, ROUND_BLOCKS):
                    if x == 3:
                        result_lo_part(2 * r + 2)
                    for c in range(NCH):
                        if x == gate_block(c) + 6:
                            dve.wait_ge(used, r * ROUND_BLOCKS + (J_MOE + gate_block(c) + 4))
                            dve.wait_ge(e_silu, NCH * r + c + 1)
                            vv.tensor_tensor(am[:], sg[:], ps[2 + c % 2][:], ALU.mult).then_inc(e_a, 1)
                        if c < NCH - 1 and x == down_block(c):
                            chunk_lo(c)
                    if x in (6, 12, 18, 24):
                        q = x // 6 - 1
                        add_scattered(q, 7 * r + (3 + q))
                    if x == 31:
                        dve.wait_ge(misc, 7 * r + 7)
                        one_hot(r + 1)
                    if x == 40:
                        gathered_lo(0, 2 * r + 3)
                    split(J_MOE + x, r, ROUND_BLOCKS)
                chunk_lo(NCH - 1)
                split(J_MOE + ROUND_BLOCKS, r, ROUND_BLOCKS)
                gathered_lo(1, 2 * r + 4)

            split(J_MOE)
            with dve.Fori(0, NEXP) as r:
                round_of(r)
            crowded = dve.value_load(infoi[0:1, 0:1], min_val=0, max_val=OVER)
            with dve.Fori(NEXP, NEXP + OVER) as r:
                with dve.If(r < crowded + NEXP):
                    round_of(r)
            result_lo_part(crowded * 2 + (2 * NEXP + 2))
            for q in range(4):
                add_scattered(q, crowded * 7 + (7 * NEXP + 3 + q), bank=q)
                dve.wait_ge(misc_free, crowded * 7 + (7 * NEXP + 3 + q))
                for k in (2 * q, 2 * q + 1):
                    vv.scalar_tensor_tensor(out=res[:, k, 0:L], in0=macc[:, k], scalar=omod[:, 40 + k, 0:1],
                                            in1=res[:, k, 0:L], op0=ALU.mult, op1=ALU.add).then_inc(y_done, 1)

        @block.gpsimd
        def _(pool):
            gp = nc.gpsimd

            def split(j, turn=0, per=0, n=BLK):
                slot, uses = block_at(j, turn, per)
                if slot != POOL_SLOT:
                    return
                pool.wait_ge(hi_made, turn * per + (j + 1) if per else j + 1)
                gp.tensor_tensor(wlo[:, j % SPLIT, 0:n], raw[:, slot, 0:n], whi[:, j % SPLIT, 0:n].bitcast(F32),
                                 ALU.subtract).then_inc(raw_free[slot], 1)

            done = [0]

            def until(j_end):
                while done[0] < j_end:
                    j = done[0]
                    split(j, n=width_of(j))
                    done[0] += 1

            def sums(n, sqb, s, width):
                for d in range(1, KT):
                    pool.wait_ge(n_sq, 8 * n + d + 1)
                    if d > 1:
                        pool.wait_ge(n_sum, 7 * n + d - 1)
                    first = sqb[:, 0, 0:width] if d == 1 else s[:, 0:width]
                    gp.tensor_tensor(s[:, 0:width], first, sqb[:, d % 2, 0:width], ALU.add).then_inc(n_sum, 1)

            gp.memset(ones[:], 1.0).then_inc(setup, 1)
            gp.memset(eps[:], EPS).then_inc(setup, 1)
            until(6)
            sums(0, sq0, ssum0, T)
            pool.wait_ge(n_ready, KT)
            pool.wait_ge(f_kcopy, 10)
            pool.dma_start(bdft[:], a["c_bdft"]).then_inc(c_four, 16)
            pool.wait_ge(tab_lo, 1)
            pool.dma_start(dft[:], a["c_inv"]).then_inc(c_g, 16)
            until(win_at(3))
            pool.wait_ge(tab_lo, 2)
            pool.dma_start(dft[:], a["c_four"]).then_inc(c_four, 16)
            until(J_LATE + 2)
            for i in range(HT):
                pool.wait_ge(x_im, i + 1)
                gp.tensor_tensor(tmp[:, 2], tmp[:, 2], tmp[:, 3], ALU.add).then_inc(x_im_sum, 1)
                pool.wait_ge(x_im_hi, i + 1)
                gp.tensor_tensor(hlo[:, HT + 1], tmp[:, 2], hhi[:, HT + 1].bitcast(F32),
                                 ALU.subtract).then_inc(x_im_lo, 1)
            pool.wait_ge(x_prod, HT)
            pool.wait_ge(fn_ab, 2)
            pool.dma_start(res[:], a["xt"].rearrange("(k p) t -> p k t", p=P)).then_inc(c_res, 16)
            until(J_FFN + 2)
            pool.wait_ge(m_ready, 8)
            sums(1, sq, ssum, T)
            pool.wait_ge(m_ready, 8)
            for i in range(4):
                gp.memset(facc[:, 2 * i:2 * i + 2], 0.0).then_inc(ff_added, 1)
            until(J_FFN + 7)
            with pool.Fori(0, FF_PAIRS - 1) as r:
                for x in range(2, 8):
                    split(J_BODY + x, r, 6, width_of(J_BODY + x))
            done[0] = J_TAIL + 2
            until(J_OWIN)
            sums(2, sq, ssum, T)
            until(J_OWIN + 2)
            pool.wait_ge(res_done, 16)
            gp.memset(kpad[:], 0.0).then_inc(zeroed, 1)
            gp.memset(vpad[:], 0.0).then_inc(zeroed, 1)
            for src, dst in ((a["c_rope"], rope[:]), (a["c_sq"][2], rot[:]), (a["c_sq"][3], bd64[:])):
                pool.dma_start(dst, src).then_inc(c_odd, 16)
            pool.dma_start(mask[:], a["c_mask"]).then_inc(c_mask, 16)
            until(J_MOE)
            sums(3, sq, ssum, L)
            pool.wait_ge(m_ready, 11)
            for src, dst in ((a["c_rw"], rw[:]), (a["c_low"], low[:]), (a["c_enum"], enum[:])):
                pool.dma_start(dst, src).then_inc(c_moe, 16)
            pool.dma_start(tri[:], a["c_tri"]).then_inc(c_moe, 16)
            pool.dma_start(iota[:], a["c_iota"]).then_inc(c_iota, 16)
            gp.memset(hott[:].bitcast(F32), 0.0).then_inc(zeroed, 1)
            gp.memset(wslot[:], 0.0)
            pool.wait_ge(n_ready, 32)
            gp.memset(macc[:], 0.0).then_inc(zeroed, 1)

            def round_of(r):
                for x in range(ROUND_BLOCKS):
                    split(J_MOE + x, r, ROUND_BLOCKS)

            with pool.Fori(0, NEXP) as r:
                round_of(r)
            pool.wait_ge(r_tab, 1)
            crowded = pool.value_load(infoi[0:1, 0:1], min_val=0, max_val=OVER)
            with pool.Fori(NEXP, NEXP + OVER) as r:
                with pool.If(r < crowded + NEXP):
                    round_of(r)


def tables():
    f = np.float64
    t = np.arange(L)
    k = np.arange(L)
    ang = 2 * np.pi * np.outer(t, k) / (2 * L)
    cos, sin = np.cos(ang), -np.sin(ang)
    nyquist = np.cos(np.pi * t)
    sin_n = sin.copy()
    sin_n[:, 0] = nyquist
    cos_n = cos[:, 0:P].copy()
    cos_n[:, 0] = nyquist
    rows = lambda x: np.ascontiguousarray(
        x.reshape(-1, P, x.shape[-1]).transpose(1, 0, 2)).astype(np.float32)
    weight = np.where(k == 0, 1.0, 2.0)[:, None] / (2 * L)
    inv_im = 2 * sin.T / (2 * L)
    inv_im[0] = nyquist / (2 * L)
    ch = np.arange(64)
    blocks = lambda x: np.kron(np.eye(2), x)
    ang64 = 2 * np.pi * np.outer(ch, ch) / 64
    bdft = np.concatenate([blocks(np.cos(ang64)), blocks(np.sin(ang64))], 1) / 8
    angl = 2 * np.pi * np.outer(t, t) / L
    four = np.concatenate([np.cos(angl), -np.sin(angl)], 1) / 16
    f32 = np.float32
    pos = np.linspace(0.0, 1.0, L, dtype=f32)
    bands = 16
    a = f32(2.0 * np.pi / L) * np.arange(L, dtype=f32)[:, None] * np.linspace(1e-4, bands - 1, bands, dtype=f32)[None]
    z = np.concatenate([pos[:, None], np.cos(a), -np.sin(a)], 1)
    deltas = np.abs(np.linspace(np.log(1e-2) / 1.5, np.log(1e-2) / 0.3, HY, dtype=f32))
    decay = np.exp(-pos[:, None] * deltas[None])
    p = np.arange(P) % 64
    place = np.where((p < 32)[:, None], (t // 64)[None], (t % 64)[None]).astype(f32)
    freq = (10000.0 ** (-(p % 16).astype(f32) / 16)).astype(f32)
    turn = place * freq[:, None]
    rope = np.stack([np.cos(turn), np.sin(turn)], 1)
    rot = np.zeros((P, P))
    for i in range(P):
        if i % 32 < 16:
            rot[i + 16, i] = -1.0
        else:
            rot[i - 16, i] = 1.0
    q = np.arange(P)
    mask = np.stack([np.where(np.abs(t[None] - (b * P + q)[:, None]) <= 128, 0.0, -1e30) for b in range(2)], 1)
    tri = np.stack([(q[:, None] < q[None]).astype(f), np.ones((P, P))], 1)
    e = np.arange(NEXP)
    low = np.broadcast_to((e[None, :] < e[:, None]).astype(f), (P, NEXP, NEXP))
    return {
        "c_sq": np.stack([np.eye(P), np.full((P, P), 1.0 / D), rot, blocks(np.full((64, 64), 1.0 / 64))]),
        "c_z": z.T, "c_decay": rows(decay), "c_dft": rows(np.concatenate([cos, sin_n], 1)),
        "c_dft2": rows(np.concatenate([sin[:, 0:P], cos_n], 1)),
        "c_four": rows(four), "c_bdft": bdft,
        "c_inv": rows(np.concatenate([cos.T * weight, inv_im])).reshape(P, 2, 512),
        "c_rope": rope, "c_mask": mask, "c_low": low, "c_enum": np.broadcast_to(e, (P, NEXP)),
        "c_tri": tri, "c_iota": np.broadcast_to(q, (P, P)),
    }


def column_tiles(w):
    n = w.shape[1] // 256
    return w.reshape(KT, P, n, 256).transpose(2, 1, 0, 3).reshape(n, P, BLK)


def by_tiles(w, order, axis):
    tiles = np.split(w, w.shape[axis] // P, axis)
    return np.concatenate([tiles[i] for i in order], axis)


def vectors(x):
    v = np.zeros((P, NVEC), np.float32)

    def put(name, a):
        v[:a.shape[0], VEC[name]] = a

    def cols(a):
        return a.reshape(-1, P).T

    for n in ("e_ada_b", "o_ada_b", "e_norm1", "e_norm2", "o_norm1", "o_norm2"):
        put(n, cols(x[n]))
    put("short", cols(x["e_hy_short"]))
    put("skip", cols(x["e_hy_skip"]))
    put("b1", x["e_hy_b1"].T)
    put("freq", x["e_hy_freq"].T)
    put("b2", x["e_hy_b2"].T)
    put("q_norm", np.concatenate([x["o_q_norm"].T] * 2))
    put("k_norm", np.concatenate([x["o_k_norm"].T] * 2))
    put("sc", cols(x["o_sc_conv"]))
    put("sink", np.broadcast_to(x["o_sink"][:, HEADS], (P, NEXP)))
    put("router_b", np.broadcast_to(x["o_router_b"], (P, NEXP)))
    put("cond", np.stack([cols(x["c"]), cols(x["c_ctx"])], 2).reshape(P, 16))
    return v


def layout(x):
    a = {k: np.ascontiguousarray(v, dtype=np.float32) for k, v in tables().items()}
    a["c_vec"] = vectors(x)
    a["xt"] = np.concatenate([x["x"][0].T, x["ctx"][0].T], 1)
    a["c_w12"] = np.zeros((64, P), np.float32)
    a["c_w12"][0:33, 0:64] = x["e_hy_w1"][0]
    a["c_w12"][:, 64:] = x["e_hy_w2"][0]
    a["c_w3"] = x["e_hy_w3"][0]
    a["w_ada"] = x["e_ada_w"][0].reshape(2, 4, P, ADA // 2, CHUNK).transpose(3, 0, 2, 1, 4).reshape(ADA, P, BLK)
    a["w_in"] = column_tiles(by_tiles(x["e_w_in"][0], WIN_TILES, 1))
    a["w_out"] = column_tiles(x["e_w_out"][0])
    parts = {"gate": column_tiles(x["e_ffn_wg"][0]), "up": column_tiles(x["e_ffn_wu"][0]),
             "down": x["e_ffn_wd"][0].reshape(FF_PAIRS, 2, P, D).transpose(0, 2, 1, 3).reshape(FF_PAIRS, P, BLK)}
    mod = x["o_ada_w"][0].reshape(KT, P, ADA // 2, CHUNK).transpose(2, 1, 0, 3)
    for kind, k in MOD_TILES.items():
        parts[kind] = np.zeros((ADA // 2, P, BLK), np.float32)
        parts[kind][:, :, 0:len(k) * CHUNK] = mod[:, :, k.start:k.stop].reshape(ADA // 2, P, -1)
    a["w_ffn"] = np.stack([parts[kind][FFN_KINDS[:j].count(kind)] for j, kind in enumerate(FFN_KINDS)])
    w = x["o_w_in"][0]
    heads = np.split(w[:, 0:512], 8, 1)
    w = np.concatenate([heads[h] for h in HEADS] + [w[:, 512:]], 1)
    a["w_oin"] = column_tiles(by_tiles(w, OWIN_TILES, 1))
    w = x["o_w_out"][0]
    heads = np.split(w[0:512], 8, 0)
    a["w_oout"] = column_tiles(np.concatenate([heads[h] for h in HEADS] + [w[512:]], 0))
    gate, up = (x[n][0].reshape(NEXP, 2, 4, P, NCH, CHUNK).transpose(4, 0, 1, 3, 2, 5)
                for n in ("o_moe_wg", "o_moe_wu"))
    down = x["o_moe_wd"][0].reshape(NEXP, NCH, 2, 2, P, D).transpose(1, 0, 2, 4, 3, 5)
    moe = np.empty((NEXP, ROUND_BLOCKS, P, BLK), np.float32)
    for c in range(NCH):
        g = gate_block(c)
        moe[:, g:g + 2] = gate[c].reshape(NEXP, 2, P, BLK)
        moe[:, g + 2:g + 4] = up[c].reshape(NEXP, 2, P, BLK)
        d = down_block(c)
        moe[:, d:d + 2] = down[c].reshape(NEXP, 2, P, BLK)
    a["w_moe"] = moe.reshape(NEXP * ROUND_BLOCKS, P, BLK)
    a["c_rw"] = x["o_router_w"][0].reshape(KT, P, NEXP).transpose(1, 0, 2)
    return a


def kernel(**inputs):
    import concourse.bacc as bacc
    from concourse.bass_utils import run_bass_kernel_spmd

    arrays = {n: np.ascontiguousarray(v) for n, v in layout({n: np.asarray(v) for n, v in inputs.items()}).items()}
    nc = bacc.Bacc("TRN2", target_bir_lowering=False, num_devices=1)
    a = {n: nc.dram_tensor(n, v.shape, F32, kind="ExternalInput").ap() for n, v in arrays.items()}
    out = nc.dram_tensor("out", (D, L), F32, kind="ExternalOutput").ap()
    build(nc, a, out)
    r = run_bass_kernel_spmd(nc, [arrays], core_ids=[0])
    return np.ascontiguousarray(r.results[0]["out"].T)[None]
```
